# Optimizing a Trainium2 kernel written in Bass

```python
import jax, jax.numpy as jnp
from jax import lax
import numpy as np
import math

D_MODEL = 1024
BATCH = 1
SEQ = 256
DEPTH = 2

N_MIXERS = 2
HEAD_DIM = 64
FOX_HEADS = D_MODEL // HEAD_DIM
DIL_HEADS = D_MODEL // HEAD_DIM
DIL_CONFIGS = ((128, 1), (512, 4), (2048, 16))
N_DIL_GROUPS = len(DIL_CONFIGS)
ROPE_THETA = 500000.0
ROPE_DIM = HEAD_DIM // 4
D_FF = 2816
Q_BLOCK = 128
EPS = 1e-6
MACARON_WEIGHT = 0.5
N_SUBLAYERS = 3
N_FOX_LAYERS = (DEPTH + 1) // 2
N_DIL_LAYERS = DEPTH // 2
FOX_IN = 3 * FOX_HEADS * HEAD_DIM + FOX_HEADS
DIL_IN = N_DIL_GROUPS * 3 * DIL_HEADS * HEAD_DIM


def rms_norm(x, g):
    xf = x.astype(jnp.float32)
    y = xf * lax.rsqrt(jnp.mean(xf * xf, axis=-1, keepdims=True) + EPS)
    return (y * g.astype(jnp.float32)).astype(x.dtype)

def modulate(h, shift, scale):
    return h * (1.0 + scale[:, None, :]) + shift[:, None, :]

def swiglu(h, w_gate, w_up, w_down):
    return (jax.nn.silu(h @ w_gate) * (h @ w_up)) @ w_down

def rope_tables(positions):
    half = ROPE_DIM // 2
    inv_freq = ROPE_THETA ** (-(jnp.arange(half, dtype=jnp.float32) * 2.0 / ROPE_DIM))
    ang = positions.astype(jnp.float32)[..., None] * inv_freq
    return jnp.cos(ang)[:, :, None, :], jnp.sin(ang)[:, :, None, :]

def apply_rope(x, cos, sin):
    half = ROPE_DIM // 2
    xr = x[..., :ROPE_DIM].astype(jnp.float32)
    x1, x2 = xr[..., :half], xr[..., half:]
    rot = jnp.concatenate([x1 * cos - x2 * sin, x2 * cos + x1 * sin], axis=-1).astype(x.dtype)
    return jnp.concatenate([rot, x[..., ROPE_DIM:]], axis=-1)

def fox_attention(h, w_in, b_f, q_gain, k_gain, w_out):
    B, S, _ = h.shape
    H, hd = FOX_HEADS, HEAD_DIM
    proj = h @ w_in
    qkv = proj[..., : 3 * H * hd].reshape(B, S, 3, H, hd)
    f_logit = proj[..., 3 * H * hd:].astype(jnp.float32) + b_f.astype(jnp.float32)
    q = rms_norm(qkv[:, :, 0], q_gain).transpose(0, 2, 1, 3)
    k = rms_norm(qkv[:, :, 1], k_gain).transpose(0, 2, 1, 3)
    v = qkv[:, :, 2].transpose(0, 2, 1, 3)
    cum = jnp.cumsum(jax.nn.log_sigmoid(f_logit), axis=1).transpose(0, 2, 1)
    scale = hd ** -0.5
    outs = []
    for blk in range(S // Q_BLOCK):
        q0 = blk * Q_BLOCK
        kv_len = q0 + Q_BLOCK
        logits = jnp.einsum("bhqd,bhkd->bhqk", q[:, :, q0:kv_len], k[:, :, :kv_len]).astype(jnp.float32) * scale
        logits = logits + cum[:, :, q0:kv_len, None] - cum[:, :, None, :kv_len]
        q_idx = q0 + jnp.arange(Q_BLOCK)
        k_idx = jnp.arange(kv_len)
        mask = k_idx[None, :] <= q_idx[:, None]
        logits = jnp.where(mask[None, None], logits, -jnp.inf)
        p = jax.nn.softmax(logits, axis=-1).astype(v.dtype)
        outs.append(jnp.einsum("bhqk,bhkd->bhqd", p, v[:, :, :kv_len]))
    o = jnp.concatenate(outs, axis=2).transpose(0, 2, 1, 3).reshape(B, S, H * hd)
    return o @ w_out

def dilated_group(q, k, v, window, dilation):
    B, S, H, hd = q.shape
    n_keys = window // dilation + 1
    offsets = dilation * jnp.arange(n_keys)
    scale = hd ** -0.5

    def block_fn(q0):
        qb = lax.dynamic_slice_in_dim(q, q0, Q_BLOCK, axis=1)
        t = q0 + jnp.arange(Q_BLOCK)
        idx = t[:, None] - offsets[None, :]
        valid = idx >= 0
        idx_c = jnp.maximum(idx, 0)
        kb = jnp.take(k, idx_c, axis=1)
        vb = jnp.take(v, idx_c, axis=1)
        logits = jnp.einsum("bqhd,bqkhd->bhqk", qb, kb).astype(jnp.float32) * scale
        logits = jnp.where(valid[None, None], logits, -jnp.inf)
        lse = jax.nn.logsumexp(logits, axis=-1)
        p = jnp.exp(logits - lse[..., None]).astype(v.dtype)
        ob = jnp.einsum("bhqk,bqkhd->bqhd", p, vb)
        return ob, lse

    starts = jnp.arange(S // Q_BLOCK) * Q_BLOCK
    o, lse = lax.map(block_fn, starts)
    o = o.transpose(1, 0, 2, 3, 4).reshape(B, S, H, hd)
    lse = lse.transpose(1, 0, 3, 2).reshape(B, S, H)
    return o, lse

def dilated_attention(h, cos, sin, w_in, q_gain, k_gain, w_out):
    B, S, _ = h.shape
    H, hd = DIL_HEADS, HEAD_DIM
    proj = (h @ w_in).reshape(B, S, N_DIL_GROUPS, 3, H, hd)
    outs, lses = [], []
    for g, (window, dilation) in enumerate(DIL_CONFIGS):
        q = apply_rope(rms_norm(proj[:, :, g, 0], q_gain[g]), cos, sin)
        k = apply_rope(rms_norm(proj[:, :, g, 1], k_gain[g]), cos, sin)
        o, lse = dilated_group(q, k, proj[:, :, g, 2], window, dilation)
        outs.append(o)
        lses.append(lse)
    alpha = jax.nn.softmax(jnp.stack(lses, axis=0), axis=0)
    o = jnp.sum(alpha[..., None] * jnp.stack(outs, axis=0).astype(jnp.float32), axis=0).astype(h.dtype)
    return o.reshape(B, S, H * hd) @ w_out

def first_inputs(seed: int = 0) -> dict:
    key = jax.random.key(seed)
    ks = jax.random.split(key, 20)
    D = D_MODEL
    nrm = jax.random.normal
    x = nrm(ks[0], (BATCH, SEQ, D), jnp.float32)
    c = nrm(ks[1], (BATCH, D), jnp.float32)
    offs = jax.random.randint(ks[2], (BATCH, 1), 0, 4096, dtype=jnp.int32)
    positions = (offs + jnp.arange(SEQ, dtype=jnp.int32)[None, :]).astype(jnp.int32)
    mod_w = nrm(ks[3], (DEPTH, D, N_SUBLAYERS * 3 * D), jnp.float32) * (0.5 * D ** -0.5)
    mod_b = nrm(ks[4], (DEPTH, N_SUBLAYERS * 3 * D), jnp.float32) * 0.01
    norm_g = 1.0 + 0.02 * nrm(ks[5], (DEPTH, N_SUBLAYERS, D), jnp.float32)
    ffn_w_gate = nrm(ks[6], (DEPTH, 2, D, D_FF), jnp.float32) * D ** -0.5
    ffn_w_up = nrm(ks[7], (DEPTH, 2, D, D_FF), jnp.float32) * D ** -0.5
    ffn_w_down = nrm(ks[8], (DEPTH, 2, D_FF, D), jnp.float32) * D_FF ** -0.5
    fox_w_in = nrm(ks[9], (N_FOX_LAYERS, D, FOX_IN), jnp.float32) * D ** -0.5
    fox_b_f = jax.random.uniform(ks[10], (N_FOX_LAYERS, FOX_HEADS), jnp.float32, 1.0, 6.0)
    fox_q_g = 1.0 + 0.02 * nrm(ks[11], (N_FOX_LAYERS, HEAD_DIM), jnp.float32)
    fox_k_g = 1.0 + 0.02 * nrm(ks[12], (N_FOX_LAYERS, HEAD_DIM), jnp.float32)
    fox_w_out = nrm(ks[13], (N_FOX_LAYERS, FOX_HEADS * HEAD_DIM, D), jnp.float32) * (FOX_HEADS * HEAD_DIM) ** -0.5
    dil_w_in = nrm(ks[14], (N_DIL_LAYERS, D, DIL_IN), jnp.float32) * D ** -0.5
    dil_q_g = 1.0 + 0.02 * nrm(ks[15], (N_DIL_LAYERS, N_DIL_GROUPS, HEAD_DIM), jnp.float32)
    dil_k_g = 1.0 + 0.02 * nrm(ks[16], (N_DIL_LAYERS, N_DIL_GROUPS, HEAD_DIM), jnp.float32)
    dil_w_out = nrm(ks[17], (N_DIL_LAYERS, DIL_HEADS * HEAD_DIM, D), jnp.float32) * (DIL_HEADS * HEAD_DIM) ** -0.5
    return {"x": x, "c": c, "positions": positions, "mod_w": mod_w, "mod_b": mod_b,
            "norm_g": norm_g, "ffn_w_gate": ffn_w_gate, "ffn_w_up": ffn_w_up,
            "ffn_w_down": ffn_w_down, "fox_w_in": fox_w_in, "fox_b_f": fox_b_f,
            "fox_q_g": fox_q_g, "fox_k_g": fox_k_g, "fox_w_out": fox_w_out,
            "dil_w_in": dil_w_in, "dil_q_g": dil_q_g, "dil_k_g": dil_k_g, "dil_w_out": dil_w_out}

def first_block(x, c, positions, mod_w, mod_b, norm_g, ffn_w_gate, ffn_w_up, ffn_w_down,
              fox_w_in, fox_b_f, fox_q_g, fox_k_g, fox_w_out,
              dil_w_in, dil_q_g, dil_k_g, dil_w_out):
    B = x.shape[0]
    D = x.shape[-1]
    cos, sin = rope_tables(positions)
    c_act = jax.nn.silu(c)
    for i in range(DEPTH):
        mod = (c_act @ mod_w[i] + mod_b[i]).reshape(B, N_SUBLAYERS, 3, D)
        shift, scale, gate = mod[:, :, 0], mod[:, :, 1], mod[:, :, 2]
        h = modulate(rms_norm(x, norm_g[i, 0]), shift[:, 0], scale[:, 0])
        x = x + MACARON_WEIGHT * gate[:, 0, None, :] * swiglu(h, ffn_w_gate[i, 0], ffn_w_up[i, 0], ffn_w_down[i, 0])
        h = modulate(rms_norm(x, norm_g[i, 1]), shift[:, 1], scale[:, 1])
        j = i // N_MIXERS
        if i % N_MIXERS == 0:
            y = fox_attention(h, fox_w_in[j], fox_b_f[j], fox_q_g[j], fox_k_g[j], fox_w_out[j])
        else:
            y = dilated_attention(h, cos, sin, dil_w_in[j], dil_q_g[j], dil_k_g[j], dil_w_out[j])
        x = x + gate[:, 1, None, :] * y
        h = modulate(rms_norm(x, norm_g[i, 2]), shift[:, 2], scale[:, 2])
        x = x + MACARON_WEIGHT * gate[:, 2, None, :] * swiglu(h, ffn_w_gate[i, 1], ffn_w_up[i, 1], ffn_w_down[i, 1])
    return x


GRID_W = 64
NA_HEADS = 8
NA_HEAD_DIM = 64
NA_WIN_ROWS = 8
NA_WIN_COLS = 16
NA_W = NA_HEADS * NA_HEAD_DIM
RET_HEADS = 4
RET_QK_DIM = 128
RET_V_DIM = 256
RET_CHUNK = 128
RET_QK_W = RET_HEADS * RET_QK_DIM
RET_V_W = RET_HEADS * RET_V_DIM
ROPE_BASE = 10000.0
IN_SIZES = (NA_W, NA_W, NA_W, RET_QK_W, RET_QK_W, RET_V_W, RET_V_W, D_MODEL, D_MODEL)
IN_SPLITS = tuple(int(s) for s in np.cumsum(IN_SIZES)[:-1])
D_IN = int(sum(IN_SIZES))
CONV_W = 3
PLE_DIM = 256
LN_EPS = 1e-5
GN_EPS = 1e-6
DEEPNORM_ALPHA = (2.0 * DEPTH) ** 0.25
DEEPNORM_BETA = (8.0 * DEPTH) ** -0.25


def layer_norm(x, g, b):
    xf = x.astype(jnp.float32)
    mu = jnp.mean(xf, axis=-1, keepdims=True)
    var = jnp.mean(jnp.square(xf - mu), axis=-1, keepdims=True)
    y = (xf - mu) * lax.rsqrt(var + LN_EPS) * g.astype(jnp.float32) + b.astype(jnp.float32)
    return y.astype(x.dtype)

def rotary(x, pos):
    half = x.shape[-1] // 2
    inv = ROPE_BASE ** (-jnp.arange(half, dtype=jnp.float32) / half)
    ang = pos[:, None] * inv[None, :]
    cos, sin = jnp.cos(ang), jnp.sin(ang)
    x1, x2 = x[..., :half].astype(jnp.float32), x[..., half:].astype(jnp.float32)
    return jnp.concatenate([x1 * cos - x2 * sin, x2 * cos + x1 * sin], axis=-1).astype(x.dtype)

def neighbourhood_attention(q, k, v, rpb):
    B, T, H, dh = q.shape
    rows = T // GRID_W
    wr = min(NA_WIN_ROWS, rows)
    scale = dh ** -0.5
    q_g = q.reshape(B, rows, GRID_W, H, dh).transpose(1, 0, 3, 2, 4)
    k_g = k.reshape(B, rows, GRID_W, H, dh).transpose(0, 3, 1, 2, 4)
    v_g = v.reshape(B, rows, GRID_W, H, dh).transpose(0, 3, 1, 2, 4)
    cols = np.arange(GRID_W)
    col_start = np.clip(cols - NA_WIN_COLS // 2, 0, GRID_W - NA_WIN_COLS)
    col_idx = col_start[:, None] + np.arange(NA_WIN_COLS)[None, :]
    col_off = col_idx - cols[:, None] + (NA_WIN_COLS - 1)

    def row_step(args):
        r, q_row = args
        rs = jnp.clip(r - wr // 2, 0, rows - wr)
        k_rows = lax.dynamic_slice_in_dim(k_g, rs, wr, axis=2)
        v_rows = lax.dynamic_slice_in_dim(v_g, rs, wr, axis=2)
        k_win = jnp.take(k_rows, col_idx, axis=3)
        v_win = jnp.take(v_rows, col_idx, axis=3)
        s = jnp.einsum('bhcd,bhrckd->bhcrk', q_row, k_win).astype(jnp.float32) * scale
        row_off = rs + jnp.arange(wr) - r + (NA_WIN_ROWS - 1)
        bias = jnp.take(rpb[:, row_off], col_off, axis=2)
        s = s + bias.transpose(0, 2, 1, 3)[None].astype(jnp.float32)
        pr = jax.nn.softmax(s.reshape(B, H, GRID_W, wr * NA_WIN_COLS), axis=-1)
        pr = pr.reshape(B, H, GRID_W, wr, NA_WIN_COLS).astype(v.dtype)
        return jnp.einsum('bhcrk,bhrckd->bhcd', pr, v_win)

    out = lax.map(row_step, (jnp.arange(rows), q_g))
    return out.transpose(1, 0, 3, 2, 4).reshape(B, T, H * dh)

def retention_dir(q, k, v, gamma, include_diag):
    B, H, T, dk = q.shape
    dv = v.shape[-1]
    C = RET_CHUNK
    n = T // C
    qc = q.reshape(B, H, n, C, dk)
    kc = k.reshape(B, H, n, C, dk)
    vc = v.reshape(B, H, n, C, dv)
    log_g = jnp.log(gamma)
    i = np.arange(C)
    diff = i[:, None] - i[None, :]
    mask = (diff >= 0) if include_diag else (diff > 0)
    dpos = np.maximum(diff, 0).astype(np.float32)
    decay_in = jnp.where(mask[None], jnp.exp(log_g[:, None, None] * dpos[None]), 0.0)
    s = jnp.einsum('bhnid,bhnjd->bhnij', qc, kc) * decay_in[None, :, None]
    inner = jnp.einsum('bhnij,bhnje->bhnie', s, vc)
    zeta = jnp.exp(log_g[:, None] * (C - 1 - i).astype(np.float32))
    xi = jnp.exp(log_g[:, None] * (i + 1).astype(np.float32))
    chunk_decay = jnp.exp(log_g * C)
    kv = jnp.einsum('bhnjd,bhnje->nbhde', kc * zeta[None, :, None, :, None], vc)

    def body(S, kv_c):
        return S * chunk_decay[None, :, None, None] + kv_c, S

    S0 = jnp.zeros((B, H, dk, dv), kv.dtype)
    _, S_prev = lax.scan(body, S0, kv)
    cross = jnp.einsum('bhnid,nbhde->bhnie', qc, S_prev) * xi[None, :, None, :, None]
    return (inner + cross).reshape(B, H, T, dv)

def bidirectional_retention(q, k, v, g, decay_f, decay_b):
    B, T, H, dk = q.shape
    pos = jnp.arange(T, dtype=jnp.float32)
    qh = rotary(q.transpose(0, 2, 1, 3), pos)
    kh = rotary(k.transpose(0, 2, 1, 3), pos) * (dk ** -0.5)
    vh = v.reshape(B, T, H, RET_V_DIM).transpose(0, 2, 1, 3)
    gam_f = jax.nn.sigmoid(decay_f.astype(jnp.float32))
    gam_b = jax.nn.sigmoid(decay_b.astype(jnp.float32))
    fwd = retention_dir(qh, kh, vh, gam_f, True)
    bwd = jnp.flip(retention_dir(jnp.flip(qh, 2), jnp.flip(kh, 2), jnp.flip(vh, 2), gam_b, False), 2)
    o = (fwd + bwd).astype(jnp.float32)
    mu = jnp.mean(o, axis=-1, keepdims=True)
    var = jnp.mean(jnp.square(o - mu), axis=-1, keepdims=True)
    o = ((o - mu) * lax.rsqrt(var + GN_EPS)).astype(v.dtype)
    o = o.transpose(0, 2, 1, 3).reshape(B, T, H * RET_V_DIM)
    return jax.nn.silu(g) * o

def conv_glu_ffn(x, w_up, conv_w, conv_b, w_down):
    h = x @ w_up
    hp = jnp.pad(h, ((0, 0), (1, 1), (0, 0)))
    h = hp[:, :-2] * conv_w[0] + hp[:, 1:-1] * conv_w[1] + hp[:, 2:] * conv_w[2] + conv_b
    a, b = jnp.split(h, 2, axis=-1)
    return (jax.nn.gelu(a) * b) @ w_down

def second_inputs(seed: int = 0) -> dict:
    key = jax.random.key(seed)
    ks = jax.random.split(key, 20)
    f32 = jnp.float32
    nrm = lambda k, shape: jax.random.normal(k, shape, f32)
    beta = DEEPNORM_BETA
    col_scale = np.ones((D_IN,), np.float32)
    col_scale[2 * NA_W:3 * NA_W] = beta
    v0 = 3 * NA_W + 2 * RET_QK_W
    col_scale[v0:v0 + RET_V_W] = beta
    gam = 1.0 - 2.0 ** (-5.0 - np.arange(RET_HEADS))
    base_logit = jnp.asarray(np.log(gam / (1.0 - gam)), f32)
    return {
        "x": nrm(ks[0], (BATCH, SEQ, D_MODEL)),
        "p": nrm(ks[1], (DEPTH, BATCH, SEQ, PLE_DIM)),
        "w_in": nrm(ks[2], (DEPTH, D_MODEL, D_IN)) * (D_MODEL ** -0.5) * jnp.asarray(col_scale),
        "na_rpb": 0.02 * nrm(ks[3], (DEPTH, NA_HEADS, 2 * NA_WIN_ROWS - 1, 2 * NA_WIN_COLS - 1)),
        "ret_decay_f": base_logit + 0.01 * nrm(ks[4], (DEPTH, RET_HEADS)),
        "ret_decay_b": base_logit + 0.01 * nrm(ks[5], (DEPTH, RET_HEADS)),
        "w_branch_a": nrm(ks[6], (DEPTH, NA_W, D_MODEL)) * (NA_W ** -0.5) * beta,
        "w_branch_b": nrm(ks[7], (DEPTH, RET_V_W, D_MODEL)) * (RET_V_W ** -0.5) * beta,
        "w_out": nrm(ks[8], (DEPTH, D_MODEL, D_MODEL)) * (D_MODEL ** -0.5) * beta,
        "ln1_g": 1.0 + 0.02 * nrm(ks[9], (DEPTH, D_MODEL)),
        "ln1_b": 0.02 * nrm(ks[10], (DEPTH, D_MODEL)),
        "w_up": nrm(ks[11], (DEPTH, D_MODEL, 2 * D_FF)) * (D_MODEL ** -0.5) * beta,
        "conv_w": nrm(ks[12], (DEPTH, CONV_W, 2 * D_FF)) * (CONV_W ** -0.5),
        "conv_b": 0.02 * nrm(ks[13], (DEPTH, 2 * D_FF)),
        "w_down": nrm(ks[14], (DEPTH, D_FF, D_MODEL)) * (D_FF ** -0.5) * beta,
        "w_ple_gate": nrm(ks[15], (DEPTH, D_MODEL, D_MODEL)) * (D_MODEL ** -0.5),
        "w_ple_proj": nrm(ks[16], (DEPTH, PLE_DIM, D_MODEL)) * (PLE_DIM ** -0.5) * beta,
        "ln2_g": 1.0 + 0.02 * nrm(ks[17], (DEPTH, D_MODEL)),
        "ln2_b": 0.02 * nrm(ks[18], (DEPTH, D_MODEL)),
    }

def second_block(x, p, w_in, na_rpb, ret_decay_f, ret_decay_b, w_branch_a, w_branch_b, w_out,
              ln1_g, ln1_b, w_up, conv_w, conv_b, w_down, w_ple_gate, w_ple_proj, ln2_g, ln2_b):
    B, T, _ = x.shape
    for i in range(DEPTH):
        proj = x @ w_in[i]
        q_na, k_na, v_na, q_r, k_r, v_r, g_r, gate_a, gate_b = jnp.split(proj, IN_SPLITS, axis=-1)
        ya = neighbourhood_attention(q_na.reshape(B, T, NA_HEADS, NA_HEAD_DIM),
                                     k_na.reshape(B, T, NA_HEADS, NA_HEAD_DIM),
                                     v_na.reshape(B, T, NA_HEADS, NA_HEAD_DIM), na_rpb[i])
        yb = bidirectional_retention(q_r.reshape(B, T, RET_HEADS, RET_QK_DIM),
                                     k_r.reshape(B, T, RET_HEADS, RET_QK_DIM),
                                     v_r, g_r, ret_decay_f[i], ret_decay_b[i])
        merged = jax.nn.sigmoid(gate_a) * (ya @ w_branch_a[i]) + jax.nn.sigmoid(gate_b) * (yb @ w_branch_b[i])
        y = merged @ w_out[i]
        x = layer_norm(DEEPNORM_ALPHA * x + y, ln1_g[i], ln1_b[i])
        ffn = conv_glu_ffn(x, w_up[i], conv_w[i], conv_b[i], w_down[i])
        ple = jax.nn.sigmoid(x @ w_ple_gate[i]) * (p[i] @ w_ple_proj[i])
        x = layer_norm(DEEPNORM_ALPHA * x + ffn + ple, ln2_g[i], ln2_b[i])
    return x


def setup_inputs(seed=0):
    out = dict(first_inputs(seed))
    for name, value in second_inputs(seed + 1).items():
        if name != "x":
            out[name + "_2"] = value
    return out


def reference(
    x, c, positions, mod_w, mod_b, norm_g, ffn_w_gate, ffn_w_up, ffn_w_down, fox_w_in, fox_b_f,
    fox_q_g, fox_k_g, fox_w_out, dil_w_in, dil_q_g, dil_k_g, dil_w_out, p_2, w_in_2, na_rpb_2,
    ret_decay_f_2, ret_decay_b_2, w_branch_a_2, w_branch_b_2, w_out_2, ln1_g_2, ln1_b_2, w_up_2,
    conv_w_2, conv_b_2, w_down_2, w_ple_gate_2, w_ple_proj_2, ln2_g_2, ln2_b_2,
):
    x = first_block(
        x, c, positions, mod_w, mod_b, norm_g, ffn_w_gate, ffn_w_up, ffn_w_down, fox_w_in,
        fox_b_f, fox_q_g, fox_k_g, fox_w_out, dil_w_in, dil_q_g, dil_k_g, dil_w_out,
    )
    return second_block(
        x, p_2, w_in_2, na_rpb_2, ret_decay_f_2, ret_decay_b_2, w_branch_a_2, w_branch_b_2,
        w_out_2, ln1_g_2, ln1_b_2, w_up_2, conv_w_2, conv_b_2, w_down_2, w_ple_gate_2,
        w_ple_proj_2, ln2_g_2, ln2_b_2,
    )


_drawn_inputs = setup_inputs


def setup_inputs(seed=0):
    import zlib

    import numpy as np

    out = dict(_drawn_inputs(seed))
    spreads = {}
    factors = {'mod_b': 5.387,
     'norm_g': 8.0,
     'fox_q_g': 8.0,
     'fox_k_g': 8.0,
     'dil_q_g': 8.0,
     'dil_k_g': 8.0,
     'na_rpb_2': 64.0,
     'ret_decay_f_2': 25.376,
     'ret_decay_b_2': 25.632,
     'w_branch_a_2': 3.574,
     'conv_b_2': 8.0}
    for name, (base, spread) in spreads.items():
        noise = np.random.default_rng([zlib.crc32(name.encode()), seed]).standard_normal(out[name].shape)
        drawn = base * np.exp(spread * noise) if base else spread * noise
        out[name] = __import__('jax').numpy.asarray(drawn.astype(out[name].dtype))
    for name, factor in factors.items():
        out[name] = (out[name] * factor).astype(out[name].dtype)
    return out
```

```python
from contextlib import ExitStack

import concourse.bass as bass
from concourse import mybir

F32 = mybir.dt.float32
F32R = mybir.dt.float32r
I32 = mybir.dt.int32
ALU = mybir.AluOpType
ACT = mybir.ActivationFunctionType
AX = mybir.AxisListType

P = 128
T = 256
D = 1024
NC = D // P
F = 2816
FB = F // P
RAW = 7
CONV = 3
PIECE = 2048
BIG = 1e30
ALPHA = 4.0 ** 0.25


class Sync:

    def __init__(self, nc, ctx):
        self.nc = nc
        self.ctx = ctx
        self.sem = {}
        self.count = {}
        self.seen = {}

    def add(self, name):
        self.sem[name] = self.ctx.enter_context(self.nc.semaphore(name))
        self.count[name] = 0

    def done(self, ins, name, n=1):
        self.count[name] += n
        ins.then_inc(self.sem[name], n)
        return (name, self.count[name])

    def wait(self, eng, ename, *tokens):
        for tok in tokens:
            if tok is None:
                continue
            if isinstance(tok, list):
                self.wait(eng, ename, *tok)
                continue
            name, value = tok
            if self.seen.get((ename, name), 0) < value:
                eng.wait_ge(self.sem[name], value)
                self.seen[(ename, name)] = value


def build(nc, a, out):
    root = ExitStack()
    with root:
        sy = Sync(nc, root)
        for n in ("pe", "act", "dve", "pool", "ld", "st"):
            sy.add("s_" + n)
        for i in range(RAW):
            sy.add(f"s_raw{i}")

        class Eng:
            def __init__(self, eng, name):
                self.eng, self.name = eng, name

            def wait(self, *toks):
                sy.wait(self.eng, self.name, *toks)

            def done(self, ins):
                return sy.done(ins, "s_" + self.name)

        pe, act, dve, pool, sp = (Eng(nc.tensor, "pe"), Eng(nc.scalar, "act"), Eng(nc.vector, "dve"),
                                  Eng(nc.gpsimd, "pool"), Eng(nc.sync, "sp"))

        def last(e):
            return ("s_" + e.name, sy.count["s_" + e.name])

        def sb(name, shape, dt, ctx=root):
            return ctx.enter_context(nc.sbuf_tensor(name, shape, dt))

        raw = sb("raw", [P, RAW, PIECE], F32)
        whi = sb("whi", [P, CONV, PIECE], F32R)
        wlo = sb("wlo", [P, CONV, PIECE], F32R)
        x = sb("x", [P, NC, T], F32)
        xhi = sb("xhi", [P, NC, T], F32R)
        xlo = sb("xlo", [P, NC, T], F32R)
        ident = sb("ident", [P, P], F32)
        ones = sb("ones", [P, 1], F32)
        ccol = sb("ccol", [P, NC], F32)
        mod = sb("modc", [P, 72], F32)
        modb = sb("modb", [P, 2, 72], F32)
        ng = sb("ng", [P, 6, NC], F32)
        ascale = sb("ascale", [P, 3, NC], F32)
        gs = sb("gs", [P, 3, NC], F32)
        epst = sb("epst", [P, 3], F32)
        sqb = sb("sqb", [P, 4, T], F32)
        st = sb("st", [P, 8], F32)
        ln = sb("ln", [P, 2, 4, NC], F32)
        ps = root.enter_context(nc.psum_tensor("ps", [P, 8, 512], F32))
        G0, G1, G2, G3, D0, D1, D2, D3 = range(8)
        free = [None] * 8

        def bank_wait(e, *banks):
            for b in banks:
                e.wait(free[b])

        def load(dst, src, *toks):
            pool.wait(*toks)
            return sy.done(nc.gpsimd.dma_start(dst, src), "s_ld", 16)

        def loads_done():
            return ("s_ld", sy.count["s_ld"])

        load(ccol[:, :], a["c"])
        load(ident[:, :], a["k_ident"])
        load(modb[:, :, :], a["mod_b"])
        load(ng[:, :, :], a["norm_g"])
        load(ln[:, :, :, :], a["ln"])
        load(x[:, :, :], a["x"])
        t_small = loads_done()
        t_ones = dve.done(nc.vector.memset(ones[:, :], 1.0))
        dve.done(nc.vector.memset(epst[:, 0:1], 1e-6))
        t_ones = dve.done(nc.vector.memset(epst[:, 1:2], 1e-5))

        pieces = []

        def plan(kind, srcs):
            pieces.append(dict(kind=kind, srcs=srcs))

        def kview(w, k0, k1, c0, c1):
            return w[k0 * P:k1 * P, c0:c1].rearrange("(k p) n -> p k n", p=P)

        def plan_unit(w, c0, c1=None, kind="w", nk=NC):
            for k0 in range(0, nk, 4):
                plan(kind, [((4, 512), 0, 512, kview(w, k0, k0 + 4, c0, c0 + 512))])

        def plan_pair(w0, a0, w1, a1):
            for k0 in (0, 4):
                plan("w", [((4, 512), 0, 256, kview(w0, k0, k0 + 4, a0, a0 + 256)),
                           ((4, 512), 256, 512, kview(w1, k0, k0 + 4, a1, a1 + 256))])

        def plan_down(w):
            for i in range(FB // 2):
                plan("w", [((2, 1024), 0, 1024, kview(w, 2 * i, 2 * i + 2, 0, 1024))])

        mod_at = {}

        def plan_mod(i, u):
            plan_unit(a["mod_w"][i], 512 * u, kind="m")

        fill = {}
        order = []
        for i in range(2):
            seq = [(i, u) for u in range(18)]
            order.append(seq)
        f1 = {("ffn", 0, 0): [(0, u) for u in range(4, 12)], ("mix", 0): [(0, u) for u in range(12, 18)],
              ("ffn", 0, 1): [(1, u) for u in range(0, 6)],
              ("ffn", 1, 0): [(1, u) for u in range(6, 12)], ("mix", 1): [(1, u) for u in range(12, 18)]}

        def spread(units, n):
            at = [[] for _ in range(n)]
            for j, u in enumerate(units):
                at[min(n - 1, (j * n) // len(units))].append(u)
            return at

        steps = []

        def step(kind, **kw):
            steps.append(dict(kind=kind, **kw))

        def plan_first():
            for u in range(4):
                step("mod", i=0, u=u)
            for i in range(2):
                plan_ffn(i, 0)
                plan_mix(i)
                plan_ffn(i, 1)

        def plan_ffn(i, j):
            step("norm", i=i, s=2 * j)
            at = spread(f1.get(("ffn", i, j), []), 16)
            for q in range(11):
                step("gateup", i=i, j=j, q=q)
                for m in at[q]:
                    step("mod", i=m[0], u=m[1])
            for q in range(11):
                step("down", i=i, j=j, q=q)
                if q < 5:
                    for m in at[11 + q]:
                        step("mod", i=m[0], u=m[1], bank=G3)
            step("residual", i=i, s=2 * j)

        def plan_mix(i):
            step("norm", i=i, s=1)
            fl = list(f1[("mix", i)])
            if i == 0:
                step("fox_f")
                for hh in range(2):
                    for r in range(3):
                        step("fox_in", hh=hh, r=r)
                        if fl:
                            m = fl.pop(0)
                            step("mod", i=m[0], u=m[1])
                    step("fox_attn", hh=hh)
            else:
                step("dil_rope")
                for hh in range(2):
                    for g in range(3):
                        for r in range(3):
                            step("dil_in", hh=hh, g=g, r=r)
                        if fl:
                            m = fl.pop(0)
                            step("mod", i=m[0], u=m[1])
                    step("dil_attn", hh=hh)
            step("mix_end")
            for u in range(2):
                step("mix_out", i=i, u=u)
            step("residual", i=i, s=1)

        def plan_second():
            for i in range(2):
                step("sec_begin", i=i)
                for u in range(3):
                    step("na_in", i=i, u=u)
                step("na_attn", i=i)
                for u in range(6):
                    step("ret_in", i=i, u=u)
                step("ret", i=i)
                for u in range(2):
                    step("gate", i=i, u=u, b=0)
                    step("branch", i=i, u=u, b=0)
                for u in range(2):
                    step("gate", i=i, u=u, b=1)
                    step("branch", i=i, u=u, b=1)
                step("merge_end", i=i)
                for u in range(2):
                    step("wout", i=i, u=u)
                step("ln", i=i, j=0)
                for u in range(2):
                    step("plegate", i=i, u=u)
                    step("pleproj", i=i, u=u)
                for q in range(11):
                    step("convup", i=i, q=q)
                for q in range(11):
                    step("down2", i=i, q=q)
                step("ln", i=i, j=1)

        plan_first()
        plan_second()

        def stream(s):
            k = s["kind"]
            if k == "mod":
                plan_mod(s["i"], s["u"])
            elif k == "gateup":
                q = 256 * s["q"]
                plan_pair(a["ffn_w_gate"][s["i"], s["j"]], q, a["ffn_w_up"][s["i"], s["j"]], q)
            elif k == "down":
                w, q = a["ffn_w_down"][s["i"], s["j"]], s["q"]
                plan("w", [((2, 1024), 0, 1024, kview(w, 2 * q, 2 * q + 2, 0, 1024))])
            elif k == "down2":
                w, q = a["w_down_2"][s["i"]], s["q"]
                plan("w", [((2, 1024), 0, 1024, kview(w, 2 * q, 2 * q + 2, 0, 1024))])
            elif k == "fox_f":
                plan("w", [((8, 16), 0, 16, kview(a["fox_w_in"][0], 0, 8, 3072, 3088))])
            elif k == "fox_in":
                plan_unit(a["fox_w_in"][0], 1024 * s["r"] + 512 * s["hh"])
            elif k == "dil_in":
                plan_unit(a["dil_w_in"][0], 3072 * s["g"] + 1024 * s["r"] + 512 * s["hh"])
            elif k == "mix_out":
                plan_unit((a["fox_w_out"] if s["i"] == 0 else a["dil_w_out"])[0], 512 * s["u"])
            elif k == "na_in":
                plan_unit(a["w_in_2"][s["i"]], 512 * s["u"])
            elif k == "ret_in":
                plan_unit(a["w_in_2"][s["i"]], 512 * (3 + s["u"]))
            elif k == "gate":
                plan_unit(a["w_in_2"][s["i"]], 512 * (9 + 2 * s["b"] + s["u"]))
            elif k == "branch":
                if s["b"] == 0:
                    plan_unit(a["w_branch_a_2"][s["i"]], 512 * s["u"], nk=4)
                else:
                    plan_unit(a["w_branch_b_2"][s["i"]], 512 * s["u"])
            elif k == "wout":
                plan_unit(a["w_out_2"][s["i"]], 512 * s["u"])
            elif k == "plegate":
                plan_unit(a["w_ple_gate_2"][s["i"]], 512 * s["u"])
            elif k == "pleproj":
                plan("w", [((2, 512), 0, 512, kview(a["w_ple_proj_2"][s["i"]], 0, 2, 512 * s["u"], 512 * s["u"] + 512))])
            elif k == "convup":
                q = 256 * s["q"]
                plan_pair(a["w_up_2"][s["i"]], q, a["w_up_2"][s["i"]], F + q)

        for s in steps:
            stream(s)

        state = dict(dma=0, conv=0, use=0, cslot=0)
        raw_free = [None] * RAW
        conv_free = [None] * CONV

        def emit_dma(p):
            slot = p % RAW
            sp.wait(raw_free[slot])
            n = 0
            for shape, c0, c1, src in pieces[p]["srcs"]:
                size = shape[0] * shape[1]
                v = raw[:, slot, 0:size].rearrange("p (k n) -> p k n", k=shape[0])[:, :, c0:c1]
                tok = sy.done(nc.sync.dma_start(v, src), f"s_raw{slot}", 16)
                n = size
            pieces[p]["landed"] = tok
            pieces[p]["n"] = n
            pieces[p]["slot"] = slot

        def emit_conv(p):
            pc = pieces[p]
            if pc["kind"] == "m":
                return
            slot, n = pc["slot"], pc["n"]
            c = state["cslot"] % CONV
            state["cslot"] += 1
            pc["c"] = c
            act.wait(pc["landed"], conv_free[c])
            t_hi = act.done(nc.scalar.activation(whi[:, c, 0:n], raw[:, slot, 0:n], ACT.Copy))
            dve.wait(t_hi, pc["landed"], conv_free[c])
            t_lo = dve.done(nc.vector.tensor_tensor(wlo[:, c, 0:n], raw[:, slot, 0:n],
                                                    whi[:, c, 0:n].bitcast(F32), ALU.subtract))
            raw_free[slot] = [t_hi, t_lo]
            pc["conv"] = [t_hi, t_lo]

        def ensure():
            use = state["use"]
            while state["conv"] < len(pieces) and state["conv"] < use + CONV:
                p = state["conv"]
                if state["dma"] <= p:
                    emit_dma(state["dma"])
                    state["dma"] += 1
                    continue
                emit_conv(p)
                state["conv"] += 1
            while state["dma"] < len(pieces) and state["dma"] < use + RAW:
                emit_dma(state["dma"])
                state["dma"] += 1

        def next_piece(k, n):
            ensure()
            p = state["use"]
            pc = pieces[p]
            pe.wait(pc["conv"])
            c = pc["c"]
            vh = whi[:, c, 0:k * n].rearrange("p (k n) -> p k n", k=k)
            vl = wlo[:, c, 0:k * n].rearrange("p (k n) -> p k n", k=k)
            return vh, vl, pc

        def piece_used(pc, tok):
            if pc["kind"] == "m":
                raw_free[pc["slot"]] = tok
            else:
                conv_free[pc["c"]] = tok
            state["use"] += 1

        def raw_piece(k, n):
            ensure()
            pc = pieces[state["use"]]
            pe.wait(pc["landed"])
            return raw[:, pc["slot"], 0:k * n].rearrange("p (k n) -> p k n", k=k), pc

        deferred = []

        def run_deferred():
            while deferred:
                deferred.pop(0)()

        def mm(out_, l, r, start, stop):
            return nc.tensor.matmul(out_, l, r, start=start, stop=stop, skip_group_check=True)

        pair = [0]

        def next_pair():
            pair[0] ^= 1
            return (G2, G3) if pair[0] else (G0, G1)

        def feature_unit(ah, al, need, nk=NC, banks=None):
            b0, b1 = banks or next_pair()
            pe.wait(free[b0], free[b1])
            for k0 in range(0, nk, 4):
                n = min(4, nk - k0)
                vh, vl, pc = next_piece(n, 512)
                for kk in range(n):
                    kc = k0 + kk
                    pe.wait(need(kc))
                    for m in range(4):
                        o = ps[:, b0 if m < 2 else b1, (m % 2) * T:(m % 2 + 1) * T]
                        w, v = vh[:, kk, m * P:(m + 1) * P], vl[:, kk, m * P:(m + 1) * P]
                        mm(o, w, ah[:, kc, :], kc == 0 and m % 2 == 0, False)
                        mm(o, w, al[:, kc, :], False, False)
                        ins = mm(o, v, ah[:, kc, :], False, kc == nk - 1)
                tok = pe.done(ins)
                piece_used(pc, tok)
            return b0, b1, tok

        def token_unit(need, cols=512):
            b0, b1 = next_pair()
            pe.wait(free[b0], free[b1])
            for k0 in range(0, NC, 4 if cols == 512 else NC):
                n = 4 if cols == 512 else NC
                vh, vl, pc = next_piece(n, cols)
                for kk in range(n):
                    kc = k0 + kk
                    pe.wait(need(kc))
                    for t in range(2):
                        o = ps[:, (b0, b1)[t], 0:cols]
                        h, l = xhi[:, kc, t * P:(t + 1) * P], xlo[:, kc, t * P:(t + 1) * P]
                        mm(o, h, vh[:, kk, :], kc == 0, False)
                        mm(o, h, vl[:, kk, :], False, False)
                        ins = mm(o, l, vh[:, kk, :], False, kc == NC - 1)
                tok = pe.done(ins)
                piece_used(pc, tok)
            return b0, b1, tok

        t_c = None
        act.wait(t_small)
        t_c = act.done(nc.scalar.activation(ccol[:, :], ccol[:, :], ACT.Silu))
        mod_tok = {}

        def mod_unit(i, u, bank):
            pe.wait(t_c, free[bank])
            for h in range(2):
                v, pc = raw_piece(4, 512)
                for kk in range(4):
                    for m in range(4):
                        ins = mm(ps[:, bank, m:m + 1], v[:, kk, m * P:(m + 1) * P], ccol[:, 4 * h + kk:4 * h + kk + 1],
                                 h == 0 and kk == 0 and m == 0, h == 1 and kk == 3)
                tok = pe.done(ins)
                piece_used(pc, tok)
            dve.wait(tok, mod_tok.get(("used", u // 2)), t_small)
            t = dve.done(nc.vector.tensor_tensor(mod[:, 4 * u:4 * u + 4], ps[:, bank, 0:4],
                                                 modb[:, i, 4 * u:4 * u + 4], ALU.add))
            free[bank] = t
            s, kind = u // 6, (u % 6) // 2
            if u % 2:
                dve.wait(t)
                c0 = (3 * s + kind) * NC
                if kind == 1:
                    t = dve.done(nc.vector.scalar_tensor_tensor(
                        out=ascale[:, s, :], in0=mod[:, c0:c0 + NC], scalar=1.0, in1=ng[:, 3 * i + s, :],
                        op0=ALU.add, op1=ALU.mult))
                elif kind == 2:
                    t = dve.done(nc.vector.tensor_scalar(gs[:, s, :], mod[:, c0:c0 + NC], 1.0 if s == 1 else 0.5,
                                                         None, ALU.mult))
                mod_tok[(i, s, kind)] = t

        xt = [t_small] * NC
        xn_tok = [None] * NC

        def column_sums(src, toks, col, square):
            for m in range(NC):
                s = m % 4
                if square:
                    act.wait(toks[m], sq_free[s])
                    tk = act.done(nc.scalar.activation(sqb[:, s, :], src[:, m, :], ACT.Square))
                    lhs = sqb[:, s, :]
                else:
                    tk = toks[m]
                    lhs = src[:, m, :]
                pe.wait(tk, t_ones)
                if m == 0:
                    pe.wait(free[G0])
                for t in range(2):
                    ins = mm(ps[:, G0, col + t:col + t + 1], lhs[:, t * P:(t + 1) * P], ones[:, 0:1],
                             m == 0 and t == 0, m == NC - 1)
                tok = pe.done(ins)
                if square:
                    sq_free[s] = tok
            return tok

        sq_free = [None] * 4

        def spread_columns(col, tok, bank):
            pe.wait(tok, free[bank], t_small)
            for t in range(2):
                ins = mm(ps[:, bank, t * P:(t + 1) * P], st[:, col + t:col + t + 1].to_broadcast([P, P]),
                         ident[:, :], t == 0, True)
            return pe.done(ins)

        def rstd_columns(tok, eps):
            act.wait(tok, t_ones)
            ta = act.done(nc.scalar.activation(st[:, 0:2], ps[:, G0, 0:2], ACT.Sqrt, scale=1.0 / D,
                                               bias=epst[:, eps:eps + 1]))
            free[G0] = ta
            dve.wait(ta)
            return dve.done(nc.vector.reciprocal(st[:, 2:4], st[:, 0:2]))

        nb_free = [None] * 4

        def split_chunk(m, src, tok):
            act.wait(tok, last(pe))
            th = act.done(nc.scalar.activation(xhi[:, m, :], src, ACT.Copy))
            dve.wait(th)
            tl = dve.done(nc.vector.tensor_tensor(xlo[:, m, :], src, xhi[:, m, :].bitcast(F32), ALU.subtract))
            xn_tok[m] = [th, tl]
            return tl

        def norm(i, s, nbuf):
            tok = column_sums(x, xt, 0, True)
            tb = spread_columns(2, rstd_columns(tok, 0), G1)
            pend = []
            c0 = 3 * s * NC
            for m in range(NC):
                b = m % 4
                dve.wait(tb, nb_free[b], xt[m])
                t1 = dve.done(nc.vector.tensor_tensor(nbuf[:, b, :], x[:, m, :], ps[:, G1, 0:T], ALU.mult))
                dve.wait(t1, mod_tok[(i, s, 0)], mod_tok[(i, s, 1)])
                t2 = dve.done(nc.vector.tensor_scalar(nbuf[:, b, :], nbuf[:, b, :], ascale[:, s, m:m + 1],
                                                      mod[:, c0 + m:c0 + m + 1], ALU.mult, ALU.add))
                pend.append((m, b, t2))
                if len(pend) > 1:
                    mm_, b_, t_ = pend.pop(0)
                    nb_free[b_] = split_chunk(mm_, nbuf[:, b_, :], t_)
            mm_, b_, t_ = pend.pop(0)
            nb_free[b_] = split_chunk(mm_, nbuf[:, b_, :], t_)
            free[G1] = t1
            mod_tok[("used", 3 * s)] = t2

        def need_x(kc):
            return xn_tok[kc]

        def enter(bar=True):
            c = ExitStack()
            toks = [last(pe), last(act), last(dve), last(pool), loads_done()]
            for e in (act, dve, pool):
                e.wait(toks)
            return c

        wk = {}

        def ffn_begin():
            c = enter()
            wk["ctx"] = c
            wk["nbuf"] = sb("nbuf" + tag(), [P, 4, T], F32, c)
            wk["hhi"] = sb("hhi" + tag(), [P, FB, T], F32R, c)
            wk["hlo"] = sb("hlo" + tag(), [P, FB, T], F32R, c)
            wk["e1"] = sb("e1" + tag(), [P, 2, 512], F32, c)
            wk["e2"] = sb("e2" + tag(), [P, 2, 512], F32, c)
            wk["ht"] = [None] * FB
            wk["ef"] = [None] * 2

        tags = [0]

        def tag():
            tags[0] += 1
            return f"_{tags[0]}"

        def gateup(q):
            b0, b1, tok = feature_unit(xhi, xlo, need_x)
            s = q % 2
            e1, e2 = wk["e1"][:, s, :], wk["e2"][:, s, :]
            act.wait(tok, wk["ef"][s])
            ta = act.done(nc.scalar.activation(e1, ps[:, b0, :], ACT.Silu))
            free[b0] = ta
            dve.wait(ta, tok)
            td = dve.done(nc.vector.tensor_tensor(e2, e1, ps[:, b1, :], ALU.mult))
            free[b1] = td
            hidden_split(q, e2, td, s)

        def hidden_split(q, src, td, s):
            h = wk["hhi"][:, 2 * q:2 * q + 2, :].rearrange("p k n -> p (k n)")
            l = wk["hlo"][:, 2 * q:2 * q + 2, :].rearrange("p k n -> p (k n)")
            act.wait(td)
            th = act.done(nc.scalar.activation(h, src, ACT.Copy))
            dve.wait(th)
            tl = dve.done(nc.vector.tensor_tensor(l, src, h.bitcast(F32), ALU.subtract))
            wk["ef"][s] = tl
            wk["ht"][2 * q] = wk["ht"][2 * q + 1] = [th, tl]

        def down(q):
            if q == 0:
                pe.wait(free[D0], free[D1], free[D2], free[D3])
            vh, vl, pc = next_piece(2, 1024)
            toks = []
            for kk in range(2):
                k = 2 * q + kk
                pe.wait(wk["ht"][k])
                hh, hl = wk["hhi"][:, k, :], wk["hlo"][:, k, :]
                for m in range(NC):
                    o = ps[:, D0 + m // 2, (m % 2) * T:(m % 2 + 1) * T]
                    w, v = vh[:, kk, m * P:(m + 1) * P], vl[:, kk, m * P:(m + 1) * P]
                    mm(o, w, hh, k == 0 and m % 2 == 0, False)
                    mm(o, w, hl, False, False)
                    ins = mm(o, v, hh, False, k == FB - 1)
                    if k == FB - 1 and m % 2:
                        toks += [pe.done(ins)] * 2
            piece_used(pc, toks[-1] if toks else pe.done(ins))
            wk["dt"] = toks

        def dblk(m):
            return ps[:, D0 + m // 2, (m % 2) * T:(m % 2 + 1) * T]

        def residual(i, s):
            for m in range(NC):
                dve.wait(wk["dt"][m], mod_tok[(i, s, 2)], xt[m])
                xt[m] = dve.done(nc.vector.scalar_tensor_tensor(
                    out=x[:, m, :], in0=dblk(m), scalar=gs[:, s, m:m + 1], in1=x[:, m, :],
                    op0=ALU.mult, op1=ALU.add))
                free[D0 + m // 2] = xt[m]

        def out_unit(u, ah, al, need, nk=NC):
            b0, b1, tok = feature_unit(ah, al, need, nk=nk, banks=(D0 + 2 * u, D1 + 2 * u))
            wk["dt"] = (wk["dt"] if u else []) + [tok] * 4

        def attn_scratch(c, n):
            wk["S"] = sb("S" + tag(), [P, 2, n], F32, c)
            wk["PT"] = sb("PT" + tag(), [P, 2, n], F32, c)
            wk["nm"] = sb("nm" + tag(), [P, 2, 8], F32, c)
            wk["rs"] = sb("rs" + tag(), [P, 2, 8], F32, c)
            wk["ri"] = sb("ri" + tag(), [P, 2, 8], F32, c)

        def attention(groups, klen, bias, dst, toks):
            seq = [(h, qt) for h in range(8) for qt in range(2)]
            rec = []
            S, PT, nm, rs, ri = wk["S"], wk["PT"], wk["nm"], wk["rs"], wk["ri"]
            pe.wait(toks)
            pt_free = [None, None]
            s_free = [None, None]

            def scores(j):
                h, qt = seq[j]
                kl = klen(qt)
                b = D0 + 2 * (j % 2)
                pe.wait(free[b], free[b + 1])
                r, c = (h % 2) * 64, h // 2
                for g, (qT, kT, v) in enumerate(groups):
                    bk, off = b + (g * kl) // 512, (g * kl) % 512
                    ins = mm(ps[:, bk, off:off + kl], qT[r:r + 64, c, qt * P:(qt + 1) * P],
                             kT[r:r + 64, c, 0:kl], True, True)
                tok = pe.done(ins)
                n = kl * len(groups)
                s = j % 2
                sv = S[:, s, 0:n]
                pv = ps[:, b:b + 2, :].rearrange("p a n -> p (a n)")[:, 0:n]
                dve.wait(tok, s_free[s])
                td = dve.done(nc.vector.tensor_tensor_reduce(sv, pv, bias(h, qt), 1.0, 3e38, ALU.add, ALU.min,
                                                             nm[:, qt, h:h + 1]))
                free[b] = free[b + 1] = td
                act.wait(td)
                ta = act.done(nc.scalar.activation(sv, sv, ACT.Exp, bias=nm[:, qt, h:h + 1], scale=-1.0,
                                                   accum_out=rs[:, qt, h:h + 1]))
                rec.append((sv, ta, n, kl))

            def turn(j):
                sv, ta, n, kl = rec[j]
                pe.wait(ta, free[G0], free[G1], t_small)
                for b in range(n // P):
                    o = ps[:, G0 + b // 4, (b % 4) * P:(b % 4 + 1) * P]
                    ins = nc.tensor.transpose(o, sv[:, b * P:(b + 1) * P], ident[:, :])
                tok = pe.done(ins)
                s = j % 2
                s_free[s] = tok
                pv = ps[:, G0:G0 + 2, :].rearrange("p a n -> p (a n)")[:, 0:n]
                if j % 2:
                    act.wait(tok, pt_free[s])
                    te = act.done(nc.scalar.activation(PT[:, s, 0:n], pv, ACT.Copy))
                else:
                    dve.wait(tok, pt_free[s])
                    te = dve.done(nc.vector.tensor_copy(PT[:, s, 0:n], pv))
                free[G0] = free[G1] = te
                rec[j] = rec[j] + (te,)

            def values(j):
                h, qt = seq[j]
                sv, ta, n, kl, te = rec[j]
                s = j % 2
                bank = G2 + qt
                if h == 0:
                    pe.wait(free[bank])
                pe.wait(te)
                nb = kl // P
                tot = nb * len(groups)
                for b in range(tot):
                    g, kb = b // nb, b % nb
                    ins = mm(ps[:, bank, h * 64:(h + 1) * 64], PT[:, s, b * P:(b + 1) * P],
                             groups[g][2][:, kb, h * 64:(h + 1) * 64], b == 0, b == tot - 1)
                pt_free[s] = pe.done(ins)

            n = len(seq)
            for j in range(n + 2):
                if j < n:
                    scores(j)
                if 0 <= j - 1 < n:
                    turn(j - 1)
                if 0 <= j - 2 < n:
                    values(j - 2)
            dve.wait(pt_free[0], pt_free[1], last(act))
            tr = dve.done(nc.vector.reciprocal(ri[:, :, :], rs[:, :, :]))
            dve.wait(tr)
            res = []
            for qt in range(2):
                t = dve.done(nc.vector.tensor_tensor(
                    dst(qt), ps[:, G2 + qt, :].rearrange("p (h d) -> p h d", h=8),
                    ri[:, qt, :].unsqueeze(2).to_broadcast([P, 8, 64]), ALU.mult))
                free[G2 + qt] = t
                res.append(t)
            return res

        def turn_chunks(src, n, toks, banks, scale=None):
            pe.wait(toks, t_small)
            for b in banks:
                pe.wait(free[b])
            out_ = []
            for c in range(n):
                for t in range(2):
                    o = ps[:, banks[c // 2], (c % 2) * T + t * P:(c % 2) * T + (t + 1) * P]
                    ins = nc.tensor.transpose(o, src[:, t, c * P:(c + 1) * P], ident[:, :])
                out_.append(pe.done(ins))
            return out_

        def turn_split(src, n, toks, hi, lo, c0=0, banks=(G0, G1, G2, G3)):
            tk = turn_chunks(src, n, toks, banks[:n // 2])
            res = []
            for j in range(n // 2):
                b = banks[j]
                h = hi[:, c0 + 2 * j:c0 + 2 * j + 2, :].rearrange("p k n -> p (k n)")
                l = lo[:, c0 + 2 * j:c0 + 2 * j + 2, :].rearrange("p k n -> p (k n)")
                act.wait(tk[2 * j + 1])
                th = act.done(nc.scalar.activation(h, ps[:, b, :], ACT.Copy))
                dve.wait(th, tk[2 * j + 1])
                tl = dve.done(nc.vector.tensor_tensor(l, ps[:, b, :], h.bitcast(F32), ALU.subtract))
                free[b] = tl
                res += [[th, tl], [th, tl]]
            return res

        def head_norm(b0, b1, tok, gain, dstT, rope=None):
            y = ps[:, b0:b0 + 2, :].rearrange("p t (h d) -> p (t h) d", d=64)
            sq, tm, hs = wk["sq"], wk["tm"], wk["hs"]
            act.wait(tok, wk["tmf"])
            ta = act.done(nc.scalar.activation(sq[:, :, :], ps[:, b0:b0 + 2, :], ACT.Square))
            dve.wait(ta)
            t1 = dve.done(nc.vector.tensor_reduce(hs[:, 0, :], sq[:, :, :].rearrange("p t (h d) -> p (t h) d", d=64),
                                                  AX.X, ALU.add))
            act.wait(t1)
            t2 = act.done(nc.scalar.activation(hs[:, 1, :], hs[:, 0, :], ACT.Sqrt, scale=1.0 / 64,
                                               bias=epst[:, 0:1]))
            dve.wait(t2)
            t3 = dve.done(nc.vector.reciprocal(hs[:, 2, :], hs[:, 1, :]))
            dve.wait(t3, tok, wk["tmf"])
            tv = tm[:, :, :].rearrange("p t (h d) -> p (t h) d", d=64)
            t4 = dve.done(nc.vector.tensor_tensor(tv, y, hs[:, 2, :].unsqueeze(2).to_broadcast([P, 16, 64]),
                                                  ALU.mult))
            free[b0] = free[b1] = [t4, ta]
            dve.wait(t4)
            t5 = dve.done(nc.vector.tensor_tensor(tv, tv, gain.unsqueeze(1).to_broadcast([P, 16, 64]), ALU.mult))
            if rope:
                r4 = tm[:, :, :].rearrange("p t (h d) -> p t h d", d=64)
                ra = wk["ra"][:, :, :, :]
                dve.wait(t5)
                co, si = rope
                for t in range(2):
                    dve.done(nc.vector.tensor_tensor(ra[:, t, :, 0:16], r4[:, t, :, 0:16],
                                                     co[:, t, :].unsqueeze(1).to_broadcast([P, 8, 16]), ALU.mult))
                    dve.done(nc.vector.tensor_tensor(ra[:, t, :, 16:24], r4[:, t, :, 8:16],
                                                     si[:, t, 0:8].unsqueeze(1).to_broadcast([P, 8, 8]), ALU.mult))
                    t6 = dve.done(nc.vector.tensor_tensor(ra[:, t, :, 24:32], r4[:, t, :, 0:8],
                                                          si[:, t, 8:16].unsqueeze(1).to_broadcast([P, 8, 8]),
                                                          ALU.mult))
                dve.wait(t6)
                t5 = dve.done(nc.vector.tensor_tensor(
                    tv[:, :, 0:16], ra[:, :, :, 0:16].rearrange("p t h d -> p (t h) d"),
                    ra[:, :, :, 16:32].rearrange("p t h d -> p (t h) d"), ALU.add))
            deferred.append(lambda: head_turn(t5, dstT))

        def head_turn(t5, dstT):
            tk = turn_chunks(wk["tm"], 4, t5, (D0, D1))
            act.wait(tk[-1])
            te = act.done(nc.scalar.activation(dstT[:, :, :], ps[:, D0:D0 + 2, :].rearrange(
                "p b (c n) -> p (b c) n", c=2), ACT.Copy))
            free[D0] = free[D1] = te
            wk["tmf"] = tk[-1]
            wk["at"].append(te)

        def keep_v(b0, b1, tok, dst):
            act.wait(tok)
            t = act.done(nc.scalar.activation(dst, ps[:, b0:b0 + 2, :], ACT.Copy))
            free[b0] = free[b1] = t
            wk["at"].append(t)

        def fox_begin():
            c = wk["ctx"]
            wk["at"] = []
            wk["tmf"] = None
            wk["qT"] = sb("fqT", [P, 4, T], F32, c)
            wk["kT"] = sb("fkT", [P, 4, T], F32, c)
            wk["v"] = sb("fv", [P, 2, 512], F32, c)
            wk["sq"] = sb("fsq", [P, 2, 512], F32, c)
            wk["tm"] = sb("ftm", [P, 2, 512], F32, c)
            wk["hs"] = sb("fhs", [P, 3, 16], F32, c)
            wk["o"] = sb("fo", [P, 2, 1024], F32, c)
            wk["bias"] = sb("fbias", [P, 8, 384], F32, c)
            wk["tri"] = sb("ftri", [P, 2, T], F32, c)
            wk["cm"] = sb("fcm", [P, T], F32, c)
            wk["gq"] = sb("fgq", [P, 2, 64], F32, c)
            wk["bf"] = sb("fbf", [P, 16], F32, c)
            wk["fl"] = sb("ffl", [P, 4, 2, 16], F32, c)
            wk["cT"] = sb("fcT", [16, T], F32, c)
            attn_scratch(c, T)
            load(wk["tri"][:, :, :], a["k_tri"])
            load(wk["cm"][:, :], a["k_causal"])
            load(wk["gq"][:, 0, :], a["fox_q_g"])
            load(wk["gq"][:, 1, :], a["fox_k_g"])
            load(wk["bf"][:, :], a["fox_b_f"])
            wk["ldt"] = loads_done()
            dve.wait(wk["ldt"])
            wk["gt"] = dve.done(nc.vector.tensor_scalar(wk["gq"][:, 0, :], wk["gq"][:, 0, :], -0.125, None, ALU.mult))

        def fox_f():
            b0, b1, tok = token_unit(need_x, cols=16)
            fl, bf = wk["fl"], wk["bf"]
            dve.wait(tok, wk["ldt"])
            z, t_, e_, l_ = fl[:, 0, :, :], fl[:, 1, :, :], fl[:, 2, :, :], fl[:, 3, :, :]
            t1 = dve.done(nc.vector.tensor_tensor(z, ps[:, b0:b0 + 2, 0:16], bf[:, :].unsqueeze(1).to_broadcast(
                [P, 2, 16]), ALU.add))
            free[b0] = free[b1] = t1
            act.wait(t1)
            t2 = act.done(nc.scalar.activation(t_, z, ACT.Abs))
            act.wait(t2)
            t3 = act.done(nc.scalar.activation(e_, t_, ACT.Exp, scale=-1.0))
            act.wait(t3)
            t4 = act.done(nc.scalar.activation(l_, e_, ACT.Ln, bias=1.0))
            dve.wait(t4)
            t5 = dve.done(nc.vector.scalar_tensor_tensor(out=z, in0=z, scalar=0.0, in1=l_, op0=ALU.min,
                                                         op1=ALU.subtract))
            pe.wait(t5, wk["ldt"], free[D2])
            for s in range(2):
                ins = mm(ps[0:16, D2, 0:T], fl[:, 0, s, :], wk["tri"][:, s, :], s == 0, s == 1)
            t6 = pe.done(ins)
            act.wait(t6)
            wk["ct"] = act.done(nc.scalar.activation(wk["cT"][:, :], ps[0:16, D2, 0:T], ACT.Copy))
            free[D2] = wk["ct"]

        def fox_bias(hh):
            pe.wait(wk["ct"], t_small)
            dve.wait(wk["ldt"], last(pe))
            for h in range(8):
                g = 8 * hh + h
                b = D2 + h % 2
                pe.wait(free[b])
                tok = pe.done(mm(ps[:, b, 0:T], ident[0:16, g:g + 1].to_broadcast([16, P]), wk["cT"][:, :],
                                 True, True))
                dve.wait(tok)
                dve.done(nc.vector.tensor_tensor(wk["bias"][:, h, 0:P], ps[:, b, 0:P], wk["cm"][:, P:T], ALU.add))
                t = dve.done(nc.vector.tensor_tensor(wk["bias"][:, h, P:384], ps[:, b, 0:T], wk["cm"][:, :],
                                                     ALU.add))
                free[b] = t
            wk["at"].append(t)

        def fox_in(hh, r):
            if r == 0:
                wk["at"] = []
            b0, b1, tok = token_unit(need_x)
            run_deferred()
            if r < 2:
                act.wait(wk["gt"])
                dve.wait(wk["gt"], wk["ldt"])
                head_norm(b0, b1, tok, wk["gq"][:, r, :], (wk["qT"], wk["kT"])[r])
            else:
                keep_v(b0, b1, tok, wk["v"][:, :, :])

        def fox_attn(hh):
            run_deferred()
            fox_bias(hh)
            wk["ot"] = attention([(wk["qT"], wk["kT"], wk["v"])], lambda qt: P * (qt + 1),
                                 lambda h, qt: wk["bias"][:, h, 0:P] if qt == 0 else wk["bias"][:, h, P:384],
                                 lambda qt: wk["o"][:, qt, 512 * hh:512 * hh + 512].rearrange(
                                     "p (h d) -> p h d", h=8), wk["at"])

        def dil_begin():
            c = wk["ctx"]
            wk["at"] = []
            wk["tmf"] = None
            for g in range(3):
                wk[f"qT{g}"] = sb(f"dqT{g}", [P, 4, T], F32, c)
                wk[f"kT{g}"] = sb(f"dkT{g}", [P, 4, T], F32, c)
                wk[f"v{g}"] = sb(f"dv{g}", [P, 2, 512], F32, c)
            wk["sq"] = sb("dsq", [P, 2, 512], F32, c)
            wk["tm"] = sb("dtm", [P, 2, 512], F32, c)
            wk["hs"] = sb("dhs", [P, 3, 16], F32, c)
            wk["ra"] = sb("dra", [P, 2, 8, 32], F32, c)
            wk["o"] = sb("do", [P, 2, 1024], F32, c)
            wk["mask"] = sb("dmask", [P, 1152], F32, c)
            wk["gn"] = sb("dgn", [P, 2, 3, 64], F32, c)
            wk["rp"] = sb("drp", [P, 8, 2, 16], F32, c)
            wk["pos"] = sb("dpos", [P, 2], I32, c)
            wk["posf"] = sb("dposf", [P, 2], F32, c)
            wk["inv"] = sb("dinv", [P, 2, 16], F32, c)
            attn_scratch(c, 768)
            load(wk["mask"][:, :], a["k_mask"])
            load(wk["gn"][:, 0, :, :], a["dil_q_g"])
            load(wk["gn"][:, 1, :, :], a["dil_k_g"])
            load(wk["inv"][:, :, :], a["k_inv"])
            load(wk["pos"][:, :], a["positions"])
            wk["ldt"] = loads_done()
            dve.wait(wk["ldt"])
            wk["gt"] = dve.done(nc.vector.tensor_scalar(wk["gn"][:, 0, :, :], wk["gn"][:, 0, :, :], -0.125, None,
                                                        ALU.mult))

        def chain(*fs):
            for f in fs:
                t = dve.done(f())
                dve.wait(t)
            return t

        def dil_rope():
            rp, inv = wk["rp"], wk["inv"]
            V = nc.vector
            import math
            c1 = 6.28125
            c2 = 0.0019350051879882812
            c3 = 2 * math.pi - c1 - c2
            magic = 12582912.0
            ang = rp[:, 0, :, :]
            chain(lambda: V.tensor_copy(wk["posf"][:, :], wk["pos"][:, :]))
            for t in range(2):
                chain(lambda: V.tensor_scalar(rp[:, 0, t, :], inv[:, 0, :], wk["posf"][:, t:t + 1], None, ALU.mult))
            for w, (off, q, r) in enumerate(((0.25, 1, 2), (0.0, 3, 4))):
                n, d = rp[:, q, :, :], rp[:, r, :, :]
                chain(lambda: V.tensor_scalar(n, ang, 1.0 / (2 * math.pi), off, ALU.mult, ALU.add),
                      lambda: V.tensor_scalar(n, n, magic, None, ALU.add),
                      lambda: V.tensor_scalar(n, n, -magic, None, ALU.add),
                      lambda: V.scalar_tensor_tensor(out=d, in0=n, scalar=-c1, in1=ang, op0=ALU.mult, op1=ALU.add),
                      lambda: V.scalar_tensor_tensor(out=d, in0=n, scalar=-c2, in1=d, op0=ALU.mult, op1=ALU.add),
                      lambda: V.scalar_tensor_tensor(out=d, in0=n, scalar=-c3, in1=d, op0=ALU.mult, op1=ALU.add),
                      lambda: V.tensor_scalar(d, d, math.pi / 2 if w == 0 else 0.0, None, ALU.add),
                      lambda: V.tensor_scalar(d, d, 3.1415925, -3.1415925, ALU.min, ALU.max))
            act.wait(last(dve))
            act.done(nc.scalar.activation(rp[:, 5, :, :], rp[:, 2, :, :], ACT.Sin))
            t = act.done(nc.scalar.activation(rp[:, 6, :, :], rp[:, 4, :, :], ACT.Sin))
            dve.wait(t)
            wk["rt"] = dve.done(V.tensor_tensor(rp[:, 7, :, :], rp[:, 6, :, :], inv[:, 1, :].unsqueeze(1)
                                                .to_broadcast([P, 2, 16]), ALU.mult))

        def dil_in(hh, g, r):
            if r == 0 and g == 0:
                wk["at"] = []
            b0, b1, tok = token_unit(need_x)
            run_deferred()
            if r < 2:
                dve.wait(wk["gt"], wk["ldt"], wk["rt"])
                head_norm(b0, b1, tok, wk["gn"][:, r, g, :], wk[f"{'qk'[r]}T{g}"],
                          rope=(wk["rp"][:, 5, :, :], wk["rp"][:, 7, :, :]))
            else:
                keep_v(b0, b1, tok, wk[f"v{g}"][:, :, :])

        def dil_attn(hh):
            run_deferred()
            wk["ot"] = attention([(wk[f"qT{g}"], wk[f"kT{g}"], wk[f"v{g}"]) for g in range(3)],
                                 lambda qt: P * (qt + 1),
                                 lambda h, qt: wk["mask"][:, 0:384] if qt == 0 else wk["mask"][:, 384:1152],
                                 lambda qt: wk["o"][:, qt, 512 * hh:512 * hh + 512].rearrange(
                                     "p (h d) -> p h d", h=8), wk["at"])

        def mix_end():
            act.wait(last(pe))
            dve.wait(last(pe))
            res = turn_split(wk["o"], 8, wk["ot"], xhi, xlo)
            for m in range(NC):
                xn_tok[m] = res[m]

        def split_x(toks, free_last=True):
            for m in range(NC):
                split_chunk(m, x[:, m, :], toks[m])

        def layer_norm(i, j, nxt):
            c = wk["ctx"]
            tok = column_sums(x, xt, 0, False)
            dve.wait(tok)
            t = dve.done(nc.vector.tensor_scalar(st[:, 4:6], ps[:, G0, 0:2], 1.0 / D, None, ALU.mult))
            free[G0] = t
            tb = spread_columns(4, t, G1)
            for m in range(NC):
                dve.wait(tb, xt[m], last(pe))
                xt[m] = dve.done(nc.vector.tensor_tensor(x[:, m, :], x[:, m, :], ps[:, G1, 0:T], ALU.subtract))
            free[G1] = xt[-1]
            tok = column_sums(x, xt, 0, True)
            tb = spread_columns(2, rstd_columns(tok, 1), G1)
            pend = None
            for m in range(NC):
                dve.wait(tb, xt[m])
                t1 = dve.done(nc.vector.tensor_tensor(x[:, m, :], x[:, m, :], ps[:, G1, 0:T], ALU.mult))
                dve.wait(t1)
                xt[m] = dve.done(nc.vector.tensor_scalar(x[:, m, :], x[:, m, :], ln[:, i, 2 * j, m:m + 1],
                                                         ln[:, i, 2 * j + 1, m:m + 1], ALU.mult, ALU.add))
                if nxt:
                    if pend is not None:
                        split_chunk(pend, x[:, pend, :], xt[pend])
                    pend = m
            if nxt:
                split_chunk(pend, x[:, pend, :], xt[pend])
            free[G1] = t1

        def na_begin(i):
            c = enter()
            wk["ctx"] = c
            wk["yahi"] = sb("yahi" + tag(), [P, 4, T], F32R, c)
            wk["yalo"] = sb("yalo" + tag(), [P, 4, T], F32R, c)
            n = ExitStack()
            wk["nctx"] = n
            wk["at"] = []
            wk["qT"] = sb("nqT" + tag(), [P, 4, T], F32, n)
            wk["kT"] = sb("nkT" + tag(), [P, 4, T], F32, n)
            wk["v"] = sb("nv" + tag(), [P, 2, 512], F32, n)
            wk["o"] = sb("no" + tag(), [P, 2, 512], F32, n)
            wk["bias"] = sb("nbias" + tag(), [P, 8, 2, T], F32, n)
            attn_scratch(n, T)
            load(wk["bias"][:, :, :, :], a["na_rpb_2"][i])
            act.wait(loads_done())
            wk["at"].append(act.done(nc.scalar.activation(wk["bias"][:, :, :, :], wk["bias"][:, :, :, :], ACT.Copy,
                                                          scale=-1.0)))

        def na_in(u):
            if u < 2:
                b0, b1, tok = feature_unit(xhi, xlo, need_x)
                dst = (wk["qT"], wk["kT"])[u]
                act.wait(tok)
                t = act.done(nc.scalar.activation(dst[:, :, :], ps[:, b0:b0 + 2, :].rearrange(
                    "p b (c n) -> p (b c) n", c=2), ACT.Copy, scale=-0.125 if u == 0 else 1.0))
                free[b0] = free[b1] = t
                wk["at"].append(t)
            else:
                b0, b1, tok = token_unit(need_x)
                keep_v(b0, b1, tok, wk["v"][:, :, :])

        def na_attn():
            dve.wait(wk["at"])
            ot = attention([(wk["qT"], wk["kT"], wk["v"])], lambda qt: T,
                           lambda h, qt: wk["bias"][:, h, qt, :],
                           lambda qt: wk["o"][:, qt, :].rearrange("p (h d) -> p h d", h=8), wk["at"])
            wk["yat"] = turn_split(wk["o"], 4, ot, wk["yahi"], wk["yalo"], banks=(G0, G1))
            wk["nctx"].close()
            toks = [last(pe), last(act), last(dve), last(pool)]
            for e in (act, dve, pool):
                e.wait(toks)

        def ret_begin(i):
            c = wk["ctx"]
            wk["ybhi"] = sb("ybhi" + tag(), [P, NC, T], F32R, c)
            wk["yblo"] = sb("yblo" + tag(), [P, NC, T], F32R, c)
            n = ExitStack()
            wk["nctx"] = n
            wk["at"] = []
            wk["tmf"] = None
            wk["qT"] = sb("rqT" + tag(), [P, 4, T], F32, n)
            wk["kT"] = sb("rkT" + tag(), [P, 4, T], F32, n)
            wk["v"] = sb("rv" + tag(), [P, 2, 1024], F32, n)
            wk["g"] = sb("rg" + tag(), [P, 2, 1024], F32, n)
            wk["dt4"] = sb("rd" + tag(), [P, 4, 2, T], F32, n)
            wk["tm"] = sb("rtm" + tag(), [P, 2, 512], F32, n)
            wk["cs"] = sb("rcs" + tag(), [P, 2, 2, 64], F32, n)
            wk["rel"] = sb("rrel" + tag(), [P, 2, 2, T], F32, n)
            wk["dk"] = sb("rdk" + tag(), [P, 5, 8], F32, n)
            wk["pt"] = sb("rpt" + tag(), [P, 2, 2, T], F32, n)
            wk["bn"] = sb("rbn" + tag(), [P, 8, 6], F32, n)
            wk["mv"] = sb("rmv" + tag(), [P, 8, 2], F32, n)
            wk["sd"] = sb("rsd" + tag(), [P, 2, 8], F32, n)
            load(wk["cs"][:, :, :, :], a["k_rot"])
            load(wk["rel"][:, :, :, :], a["k_rel"])
            load(wk["dk"][:, 0, :], a["decay"][i])
            wk["ldt"] = loads_done()
            dk = wk["dk"]
            act.wait(wk["ldt"])
            t = act.done(nc.scalar.activation(dk[:, 1, :], dk[:, 0, :], ACT.Abs))
            act.wait(t)
            t = act.done(nc.scalar.activation(dk[:, 2, :], dk[:, 1, :], ACT.Exp, scale=-1.0))
            act.wait(t)
            t = act.done(nc.scalar.activation(dk[:, 3, :], dk[:, 2, :], ACT.Ln, bias=1.0))
            dve.wait(t, wk["ldt"])
            t = dve.done(nc.vector.scalar_tensor_tensor(out=dk[:, 4, :], in0=dk[:, 0, :], scalar=0.0,
                                                        in1=dk[:, 3, :], op0=ALU.min, op1=ALU.subtract))
            dve.wait(t)
            d4, rel = wk["dt4"], wk["rel"]
            for h in range(4):
                dst = d4[:, h, :, :].rearrange("p b n -> p (b n)")
                t = dve.done(nc.vector.tensor_scalar(dst, rel[:, 0, :, :].rearrange("p b n -> p (b n)"),
                                                     dk[:, 4, h:h + 1], None, ALU.mult))
                dve.wait(t)
                t = dve.done(nc.vector.scalar_tensor_tensor(
                    out=dst, in0=rel[:, 1, :, :].rearrange("p b n -> p (b n)"), scalar=dk[:, 4, 4 + h:5 + h],
                    in1=dst, op0=ALU.mult, op1=ALU.add))
            act.wait(t)
            wk["d4t"] = act.done(nc.scalar.activation(d4[:, :, :, :], d4[:, :, :, :], ACT.Exp))

        def ret_in(u):
            b0, b1, tok = token_unit(need_x)
            run_deferred()
            if u < 2:
                tm, cs = wk["tm"], wk["cs"]
                dve.wait(tok, wk["ldt"], wk["tmf"])
                rb = wk["pt"]
                for t in range(2):
                    y = ps[:, (b0, b1)[t], :].rearrange("p (h w d) -> p h w d", h=4, w=2)
                    tv = tm[:, t, :].rearrange("p (h w d) -> p h w d", h=4, w=2)
                    rv = rb[:, t, :, :].rearrange("p a (h w d) -> p (a h) w d", w=2, d=64)
                    co = cs[:, 0, t, :].unsqueeze(1)
                    si = cs[:, 1, t, :].unsqueeze(1).to_broadcast([P, 4, 64])
                    t1 = dve.done(nc.vector.tensor_tensor(
                        tm[:, t, :].rearrange("p (a d) -> p a d", d=64),
                        ps[:, (b0, b1)[t], :].rearrange("p (a d) -> p a d", d=64),
                        co.to_broadcast([P, 8, 64]), ALU.mult))
                    t2 = dve.done(nc.vector.tensor_tensor(rv[:, :, 0, :], y[:, :, 1, :], si, ALU.mult))
                    t3 = dve.done(nc.vector.tensor_tensor(rv[:, :, 1, :], y[:, :, 0, :], si, ALU.mult))
                    dve.wait(t3)
                    dve.done(nc.vector.tensor_tensor(tv[:, :, 0, :], tv[:, :, 0, :], rv[:, :, 0, :], ALU.subtract))
                    t4 = dve.done(nc.vector.tensor_tensor(tv[:, :, 1, :], tv[:, :, 1, :], rv[:, :, 1, :], ALU.add))
                free[b0] = free[b1] = t3
                dst = (wk["qT"], wk["kT"])[u]

                def turn():
                    tk = turn_chunks(wk["tm"], 4, t4, (D0, D1))
                    act.wait(tk[-1])
                    te = act.done(nc.scalar.activation(dst[:, :, :], ps[:, D0:D0 + 2, :].rearrange(
                        "p b (c n) -> p (b c) n", c=2), ACT.Copy, scale=1.0 if u == 0 else 128.0 ** -0.5))
                    free[D0] = free[D1] = te
                    wk["tmf"] = tk[-1]
                    wk["at"].append(te)

                deferred.append(turn)
            elif u < 4:
                keep_v(b0, b1, tok, wk["v"][:, :, 512 * (u - 2):512 * (u - 1)])
            else:
                act.wait(tok)
                t = act.done(nc.scalar.activation(wk["g"][:, :, 512 * (u - 4):512 * (u - 3)], ps[:, b0:b0 + 2, :],
                                                  ACT.Silu))
                free[b0] = free[b1] = t
                wk["gt"] = t

        def ret():
            run_deferred()
            qT, kT, v, d4, pt, g = wk["qT"], wk["kT"], wk["v"], wk["dt4"], wk["pt"], wk["g"]
            pe.wait(wk["at"])
            ptf = [None, None]
            bn, mv, sd = wk["bn"], wk["mv"], wk["sd"]
            tps = []
            bnt = []

            def ret_out(h, nt):
                return ps[:, D0 + 2 * (h % 2) + nt, (h // 2) * T:(h // 2 + 1) * T]

            def scores(h):
                b = G0 + h
                pe.wait(free[b])
                for mb in range(2):
                    ins = mm(ps[:, b, mb * T:(mb + 1) * T], kT[:, h, mb * P:(mb + 1) * P], qT[:, h, :], mb == 0, True)
                tok = pe.done(ins)
                dve.wait(tok, wk["d4t"], ptf[h % 2])
                tp = dve.done(nc.vector.tensor_tensor(pt[:, h % 2, :, :].rearrange("p b n -> p (b n)"), ps[:, b, :],
                                                      d4[:, h, :, :].rearrange("p b n -> p (b n)"), ALU.mult))
                free[b] = tp
                tps.append(tp)

            for h in range(4):
                if h == 0:
                    scores(0)
                    scores(1)
                elif h < 3:
                    scores(h + 1)
                pe.wait(tps[h])
                for nt in range(2):
                    pe.wait(free[D0 + 2 * (h % 2) + nt], bnt[h - 2] if h > 1 else None)
                    o = ret_out(h, nt)
                    for mb in range(2):
                        ins = mm(o, pt[:, h % 2, mb, nt * P:(nt + 1) * P], v[:, mb, h * T:(h + 1) * T], mb == 0,
                                 mb == 1)
                tok = pe.done(ins)
                ptf[h % 2] = tok
                dve.wait(tok)
                for nt in range(2):
                    t = dve.done(nc.vector.bn_stats(bn[:, 2 * h + nt, :], ret_out(h, nt)))
                bnt.append(t)
                dve.wait(t)
                for nt in range(2):
                    t = dve.done(nc.vector.bn_aggr(mv[:, 2 * h + nt, :], bn[:, 2 * h + nt, :]))
            act.wait(t, t_ones)
            t = act.done(nc.scalar.activation(sd[:, 0, :], mv[:, :, 1], ACT.Sqrt, bias=epst[:, 0:1]))
            dve.wait(t)
            t = dve.done(nc.vector.reciprocal(sd[:, 1, :], sd[:, 0, :]))
            dve.wait(t, wk["gt"])
            e = wk["tm"]
            for h in range(4):
                for nt in range(2):
                    j = 2 * h + nt
                    o = ret_out(h, nt)
                    tmp = e[:, j % 2, 0:T]
                    t = dve.done(nc.vector.tensor_scalar(tmp, o, mv[:, j, 0:1], sd[:, 1, j:j + 1], ALU.subtract,
                                                         ALU.mult))
                    free[D0 + 2 * (h % 2) + nt] = t
                    dve.wait(t)
                    t = dve.done(nc.vector.tensor_tensor(g[:, nt, h * T:(h + 1) * T], g[:, nt, h * T:(h + 1) * T],
                                                         tmp, ALU.mult))
            wk["ybt"] = turn_split(g, 8, t, wk["ybhi"], wk["yblo"])
            n = wk["nctx"]
            n.close()
            c = wk["ctx"]
            toks = [last(pe), last(act), last(dve), last(pool)]
            for e_ in (act, dve, pool):
                e_.wait(toks)
            wk["sg"] = sb("sg" + tag(), [P, 2, 1024], F32, c)
            wk["m32"] = sb("m32" + tag(), [P, NC, T], F32, c)
            wk["mhi"] = sb("mhi" + tag(), [P, NC, T], F32R, c)
            wk["mlo"] = sb("mlo" + tag(), [P, NC, T], F32R, c)
            wk["sgf"] = [None, None]
            wk["mt"] = [None] * NC
            wk["m32t"] = [None, None]

        def gate(u, b):
            b0, b1, tok = feature_unit(xhi, xlo, need_x)
            act.wait(tok, wk["sgf"][u])
            wk["sgt"] = act.done(nc.scalar.activation(wk["sg"][:, u, :], ps[:, b0:b0 + 2, :].rearrange(
                "p b n -> p (b n)"), ACT.Sigmoid))
            free[b0] = free[b1] = wk["sgt"]

        def branch(u, b):
            if b == 0:
                b0, b1, tok = feature_unit(wk["yahi"], wk["yalo"], lambda kc: wk["yat"][kc], nk=4)
            else:
                b0, b1, tok = feature_unit(wk["ybhi"], wk["yblo"], lambda kc: wk["ybt"][kc])
            pv = ps[:, b0:b0 + 2, :].rearrange("p b n -> p (b n)")
            m = wk["m32"][:, 4 * u:4 * u + 4, :].rearrange("p k n -> p (k n)")
            sg = wk["sg"][:, u, :]
            dve.wait(tok, wk["sgt"])
            if b == 0:
                t = dve.done(nc.vector.tensor_tensor(m, sg, pv, ALU.mult))
                free[b0] = free[b1] = wk["sgf"][u] = wk["m32t"][u] = t
                return
            t = dve.done(nc.vector.tensor_tensor(sg, sg, pv, ALU.mult))
            free[b0] = free[b1] = t
            dve.wait(t, wk["m32t"][u])
            t = dve.done(nc.vector.tensor_tensor(m, m, sg, ALU.add))
            act.wait(t)
            h = wk["mhi"][:, 4 * u:4 * u + 4, :].rearrange("p k n -> p (k n)")
            l = wk["mlo"][:, 4 * u:4 * u + 4, :].rearrange("p k n -> p (k n)")
            th = act.done(nc.scalar.activation(h, m, ACT.Copy))
            dve.wait(th)
            tl = dve.done(nc.vector.tensor_tensor(l, m, h.bitcast(F32), ALU.subtract))
            for k in range(4):
                wk["mt"][4 * u + k] = [th, tl]

        def residual_ln():
            for m in range(NC):
                dve.wait(wk["dt"][m], xt[m])
                xt[m] = dve.done(nc.vector.scalar_tensor_tensor(
                    out=x[:, m, :], in0=x[:, m, :], scalar=ALPHA, in1=dblk(m), op0=ALU.mult, op1=ALU.add))
                free[D0 + m // 2] = xt[m]

        def residual_plain():
            for m in range(NC):
                dve.wait(wk["dt"][m], xt[m])
                xt[m] = dve.done(nc.vector.tensor_tensor(x[:, m, :], x[:, m, :], dblk(m), ALU.add))
                free[D0 + m // 2] = xt[m]

        def second_ffn_begin(i):
            wk["ctx"].close()
            ffn_begin()
            c = wk["ctx"]
            wk["cw"] = sb("cw" + tag(), [P, 4, 44], F32, c)
            wk["pT"] = sb("pT" + tag(), [P, 2, T], F32, c)
            wk["phi"] = sb("phi" + tag(), [P, 2, T], F32R, c)
            wk["plo"] = sb("plo" + tag(), [P, 2, T], F32R, c)
            wk["pg"] = sb("pg" + tag(), [P, 1024], F32, c)
            load(wk["cw"][:, :, :], a["conv"][i])
            load(wk["pT"][:, :, :], a["p_2"][i])
            wk["ldt"] = loads_done()
            act.wait(wk["ldt"])
            th = act.done(nc.scalar.activation(wk["phi"][:, :, :], wk["pT"][:, :, :], ACT.Copy))
            dve.wait(th, wk["ldt"])
            tl = dve.done(nc.vector.tensor_tensor(wk["plo"][:, :, :], wk["pT"][:, :, :],
                                                  wk["phi"][:, :, :].bitcast(F32), ALU.subtract))
            wk["pt_"] = [th, tl]
            wk["pgf"] = None

        def plegate(u):
            b0, b1, tok = feature_unit(xhi, xlo, need_x)
            act.wait(tok, wk["pgf"])
            wk["pgt"] = act.done(nc.scalar.activation(wk["pg"][:, :], ps[:, b0:b0 + 2, :].rearrange(
                "p b n -> p (b n)"), ACT.Sigmoid))
            free[b0] = free[b1] = wk["pgt"]

        def pleproj(u):
            b0, b1, tok = feature_unit(wk["phi"], wk["plo"], lambda kc: wk["pt_"], nk=2)
            dve.wait(tok, wk["pgt"])
            t = dve.done(nc.vector.tensor_tensor(wk["pg"][:, :], wk["pg"][:, :], ps[:, b0:b0 + 2, :].rearrange(
                "p b n -> p (b n)"), ALU.mult))
            free[b0] = free[b1] = t
            dve.wait(t, *[xn_tok[m] for m in range(4 * u, 4 * u + 4)])
            xv = x[:, 4 * u:4 * u + 4, :].rearrange("p k n -> p (k n)")
            t = dve.done(nc.vector.scalar_tensor_tensor(out=xv, in0=xv, scalar=ALPHA, in1=wk["pg"][:, :],
                                                        op0=ALU.mult, op1=ALU.add))
            wk["pgf"] = t
            for m in range(4 * u, 4 * u + 4):
                xt[m] = t

        def convup(q):
            b0, b1, tok = feature_unit(xhi, xlo, need_x)
            s = q % 2
            cw = wk["cw"]
            e = (wk["e1"], wk["e2"])
            res = []
            for side, b in ((0, b0), (1, b1)):
                act.wait(tok, wk["ef"][s], wk["ldt"])
                for k in range(2):
                    blk = 22 * side + 2 * q + k
                    ta = act.done(nc.scalar.activation(
                        e[side][:, s, k * T:(k + 1) * T], ps[:, b, k * T:(k + 1) * T], ACT.Identity,
                        scale=cw[:, 1, blk:blk + 1], bias=cw[:, 3, blk:blk + 1]))
                for k in range(2):
                    blk = 22 * side + 2 * q + k
                    y = ps[:, b, k * T:(k + 1) * T]
                    o = e[side][:, s, k * T:(k + 1) * T]
                    dve.wait(ta, tok)
                    t = dve.done(nc.vector.scalar_tensor_tensor(
                        out=o[:, 1:T], in0=y[:, 0:T - 1], scalar=cw[:, 0, blk:blk + 1], in1=o[:, 1:T],
                        op0=ALU.mult, op1=ALU.add))
                    dve.wait(t)
                    t = dve.done(nc.vector.scalar_tensor_tensor(
                        out=o[:, 0:T - 1], in0=y[:, 1:T], scalar=cw[:, 2, blk:blk + 1], in1=o[:, 0:T - 1],
                        op0=ALU.mult, op1=ALU.add))
                free[b] = t
                res.append(t)
            act.wait(res[0])
            ta = act.done(nc.scalar.activation(e[0][:, s, :], e[0][:, s, :], ACT.Gelu_apprx_tanh))
            dve.wait(ta, res[1])
            td = dve.done(nc.vector.tensor_tensor(e[1][:, s, :], e[0][:, s, :], e[1][:, s, :], ALU.mult))
            hidden_split(q, e[1][:, s, :], td, s)

        for s in steps:
            k = s["kind"]
            if k == "mod":
                mod_unit(s["i"], s["u"], s.get("bank", D3))
            elif k == "norm":
                if "ctx" in wk:
                    wk["ctx"].close()
                if s["s"] != 1:
                    ffn_begin()
                else:
                    wk["ctx"] = enter()
                    if s["i"] == 0:
                        fox_begin()
                    else:
                        dil_begin()
                    wk["nbuf"] = wk["bias" if s["i"] == 0 else "v0"]
                    wk["nbuf"] = (wk["bias"][:, :, :].rearrange("p h n -> p (h n)")[:, 0:1024] if s["i"] == 0
                                  else wk["v0"][:, :, :].rearrange("p t n -> p (t n)")).rearrange(
                                      "p (k n) -> p k n", k=4)
                nb = wk["nbuf"]
                norm(s["i"], s["s"], nb)
            elif k == "gateup":
                gateup(s["q"])
            elif k == "down":
                down(s["q"])
            elif k == "residual":
                residual(s["i"], s["s"])
            elif k == "fox_f":
                fox_f()
            elif k == "fox_in":
                fox_in(s["hh"], s["r"])
            elif k == "fox_attn":
                fox_attn(s["hh"])
            elif k == "dil_rope":
                dil_rope()
            elif k == "dil_in":
                dil_in(s["hh"], s["g"], s["r"])
            elif k == "dil_attn":
                dil_attn(s["hh"])
            elif k == "mix_end":
                mix_end()
            elif k == "mix_out":
                out_unit(s["u"], xhi, xlo, need_x)
            elif k == "sec_begin":
                wk["ctx"].close()
                if s["i"] == 0:
                    split_x(xt)
                na_begin(s["i"])
            elif k == "na_in":
                na_in(s["u"])
            elif k == "na_attn":
                na_attn()
                ret_begin(s["i"])
            elif k == "ret_in":
                ret_in(s["u"])
            elif k == "ret":
                ret()
            elif k == "gate":
                gate(s["u"], s["b"])
            elif k == "branch":
                branch(s["u"], s["b"])
            elif k == "merge_end":
                pass
            elif k == "wout":
                out_unit(s["u"], wk["mhi"], wk["mlo"], lambda kc: wk["mt"][kc])
            elif k == "ln":
                if s["j"] == 0:
                    residual_ln()
                    layer_norm(s["i"], 0, True)
                    second_ffn_begin(s["i"])
                else:
                    residual_plain()
                    layer_norm(s["i"], 1, s["i"] == 0)
            elif k == "plegate":
                plegate(s["u"])
            elif k == "pleproj":
                pleproj(s["u"])
            elif k == "convup":
                convup(s["q"])
            elif k == "down2":
                down(s["q"])
        wk["ctx"].close()
        for m in range(NC):
            sp.wait(xt[m])
            t = sy.done(nc.sync.dma_start(out[:, m, :], x[:, m, :]), "s_st", 16)
        sp.wait(t)


def constants():
    import numpy as np
    k = {}
    k["k_ident"] = np.eye(P, dtype=np.float32)
    s = np.arange(T)
    tri = (s[:, None] <= s[None, :]).astype(np.float32).reshape(2, P, T)
    k["k_tri"] = np.ascontiguousarray(tri.transpose(1, 0, 2))
    q = np.arange(P)
    k["k_causal"] = np.where(s[None, :] <= q[:, None] + P, 0.0, BIG).astype(np.float32)
    parts = []
    for qt in range(2):
        for window, dil in ((128, 1), (512, 4), (2048, 16)):
            d = (q[:, None] + P * qt) - np.arange(P * (qt + 1))[None, :]
            parts.append(np.where((d >= 0) & (d <= window) & (d % dil == 0), 0.0, BIG).astype(np.float32))
    k["k_mask"] = np.ascontiguousarray(np.concatenate(parts, axis=1))
    inv = (np.float32(500000.0) ** (-(np.arange(8, dtype=np.float32) * 2.0 / 16))).astype(np.float32)
    sign = np.concatenate([-np.ones(8), np.ones(8)]).astype(np.float32)
    k["k_inv"] = np.ascontiguousarray(np.broadcast_to(np.stack([np.concatenate([inv, inv]), sign]), (P, 2, 16)))
    inv = (np.float32(10000.0) ** (-np.arange(64, dtype=np.float32) / 64)).astype(np.float32)
    ang = (s.astype(np.float32)[:, None] * inv[None, :]).astype(np.float64)
    rot = np.stack([np.cos(ang), np.sin(ang)]).astype(np.float32).reshape(2, 2, P, 64)
    k["k_rot"] = np.ascontiguousarray(rot.transpose(2, 0, 1, 3))
    m = (np.arange(2)[None, :, None] * P + q[:, None, None])
    n = s[None, None, :]
    k["k_rel"] = np.ascontiguousarray(np.stack([np.maximum(n - m, 0), np.maximum(m - n, 0)], axis=1).astype(np.float32))
    return k


def layout(inp):
    import numpy as np
    g = {n: np.asarray(v) for n, v in inp.items()}

    def col(v, n):
        return np.ascontiguousarray(v.reshape(v.shape[:-1] + (n, P)))

    r = {}
    for n in ("mod_w", "ffn_w_gate", "ffn_w_up", "ffn_w_down", "fox_w_in", "fox_w_out", "dil_w_in", "dil_w_out",
              "w_in_2", "w_branch_a_2", "w_branch_b_2", "w_out_2", "w_up_2", "w_down_2", "w_ple_gate_2",
              "w_ple_proj_2"):
        r[n] = np.ascontiguousarray(g[n])
    r["x"] = np.ascontiguousarray(g["x"][0].T.reshape(NC, P, T).transpose(1, 0, 2))
    r["c"] = np.ascontiguousarray(g["c"].reshape(NC, P).T)
    r["mod_b"] = np.ascontiguousarray(g["mod_b"].reshape(2, 72, P).transpose(2, 0, 1))
    r["norm_g"] = np.ascontiguousarray(g["norm_g"].reshape(6, NC, P).transpose(2, 0, 1))
    r["ln"] = np.ascontiguousarray(np.stack([g["ln1_g_2"], g["ln1_b_2"], g["ln2_g_2"], g["ln2_b_2"]], axis=1)
                                   .reshape(2, 4, NC, P).transpose(3, 0, 1, 2))
    r["fox_q_g"] = np.ascontiguousarray(np.broadcast_to(g["fox_q_g"], (P, 64)))
    r["fox_k_g"] = np.ascontiguousarray(np.broadcast_to(g["fox_k_g"], (P, 64)))
    r["fox_b_f"] = np.ascontiguousarray(np.broadcast_to(g["fox_b_f"], (P, 16)))
    r["dil_q_g"] = np.ascontiguousarray(np.broadcast_to(g["dil_q_g"][0], (P, 3, 64)))
    r["dil_k_g"] = np.ascontiguousarray(np.broadcast_to(g["dil_k_g"][0], (P, 3, 64)))
    r["positions"] = np.ascontiguousarray(g["positions"].reshape(2, P).T)
    q = np.arange(T)
    rr, cc = q // 64, q % 64
    start = np.clip(cc - 8, 0, 48)
    dr = rr[None, :] - rr[:, None] + 7
    inside = (cc[None, :] >= start[:, None]) & (cc[None, :] < start[:, None] + 16)
    dc = np.where(inside, cc[None, :] - cc[:, None] + 15, 31)
    padded = np.pad(g["na_rpb_2"], ((0, 0), (0, 0), (0, 0), (0, 1)), constant_values=-BIG)
    b = padded[:, :, dr, dc]
    r["na_rpb_2"] = np.ascontiguousarray(b.reshape(2, 8, 2, P, T).transpose(0, 3, 1, 2, 4))
    dec = np.concatenate([g["ret_decay_f_2"], g["ret_decay_b_2"]], axis=1)
    r["decay"] = np.ascontiguousarray(np.broadcast_to(dec[:, None, :], (2, P, 8)))
    cw = np.concatenate([g["conv_w_2"], g["conv_b_2"][:, None, :]], axis=1)
    r["conv"] = np.ascontiguousarray(cw.reshape(2, 4, 44, P).transpose(0, 3, 1, 2))
    r["p_2"] = np.ascontiguousarray(g["p_2"][:, 0].transpose(0, 2, 1).reshape(2, 2, P, T).transpose(0, 2, 1, 3))
    r.update(constants())
    return r


def kernel(**inputs):
    import concourse.bacc as bacc
    import numpy as np
    from concourse.bass_utils import run_bass_kernel_spmd

    nc = bacc.Bacc("TRN2", target_bir_lowering=False, num_devices=1)
    arrays = {f"in_{n}": v for n, v in layout(inputs).items()}
    args = {n[3:]: nc.dram_tensor(n, v.shape, mybir.dt.from_np(v.dtype), kind="ExternalInput").ap()
            for n, v in arrays.items()}
    out = nc.dram_tensor("out_x", (P, NC, T), F32, kind="ExternalOutput").ap()
    build(nc, args, out)
    r = run_bass_kernel_spmd(nc, [arrays], core_ids=[0])
    y = r.results[0]["out_x"]
    return np.ascontiguousarray(np.asarray(y).transpose(1, 0, 2).reshape(1, D, T).transpose(0, 2, 1))
```

```python
import math
from contextlib import ExitStack

import concourse.bass as bass
from concourse import mybir

F32 = mybir.dt.float32
F32R = mybir.dt.float32r
I32 = mybir.dt.int32
ALU = mybir.AluOpType
ACT = mybir.ActivationFunctionType
AX = mybir.AxisListType

P = 128
T = 256
D = 1024
NC = D // P
F = 2816
FB = F // P
RAW = 6
CONV = 3
PIECE = 2048
BIG = 1e30
ALPHA = 4.0 ** 0.25


class Sync:

    def __init__(self, nc, ctx):
        self.nc = nc
        self.ctx = ctx
        self.sem = {}
        self.count = {}
        self.seen = {}

    def add(self, name):
        self.sem[name] = self.ctx.enter_context(self.nc.semaphore(name))
        self.count[name] = 0

    def done(self, ins, name, n=1):
        self.count[name] += n
        ins.then_inc(self.sem[name], n)
        return (name, self.count[name])

    def wait(self, eng, ename, *tokens):
        for tok in tokens:
            if tok is None:
                continue
            if isinstance(tok, list):
                self.wait(eng, ename, *tok)
                continue
            name, value = tok
            if self.seen.get((ename, name), 0) < value:
                eng.wait_ge(self.sem[name], value)
                self.seen[(ename, name)] = value


def build(nc, a, out):
    root = ExitStack()
    with root:
        sy = Sync(nc, root)
        for n in ("pe", "act", "dve", "pool", "ld", "st", "c", "a"):
            sy.add("s_" + n)
        for i in range(RAW):
            sy.add(f"s_raw{i}")

        class Eng:
            def __init__(self, eng, name):
                self.eng, self.name = eng, name

            def wait(self, *toks):
                sy.wait(self.eng, self.name, *toks)

            def done(self, ins):
                return sy.done(ins, "s_" + self.name)

        pe, act, dve, pool, sp = (Eng(nc.tensor, "pe"), Eng(nc.scalar, "act"), Eng(nc.vector, "dve"),
                                  Eng(nc.gpsimd, "pool"), Eng(nc.sync, "sp"))

        def last(e):
            return ("s_" + e.name, sy.count["s_" + e.name])

        def sb(name, shape, dt, ctx=root):
            return ctx.enter_context(nc.sbuf_tensor(name, shape, dt))

        raw = sb("raw", [P, RAW, PIECE], F32)
        whi = sb("whi", [P, CONV, PIECE], F32R)
        wlo = sb("wlo", [P, CONV, PIECE], F32R)
        x = sb("x", [P, NC, T], F32)
        xhi = sb("xhi", [P, NC, T], F32R)
        xlo = sb("xlo", [P, NC, T], F32R)
        ident = sb("ident", [P, P], F32)
        mean = sb("mean", [P, P], F32)
        ccol = sb("ccol", [P, NC], F32)
        csil = sb("csil", [P, NC, 32], F32)
        mrow = sb("mrow", [P, 512], F32)
        rope = sb("rope", [P, 2, 2, 16], F32)
        inv = sb("inv", [P, 2, 16], F32)
        pos = sb("pos", [P, 2], I32)
        cw = sb("cw", [P, 2, 4, 44], F32)
        rot = sb("rot", [P, 2, 2, 64], F32)
        mod = sb("modc", [P, 72], F32)
        modb = sb("modb", [P, 2, 72], F32)
        ng = sb("ng", [P, 6, NC], F32)
        ascale = sb("ascale", [P, 3, NC], F32)
        gs = sb("gs", [P, 3, NC], F32)
        epst = sb("epst", [P, 3], F32)
        sqb = sb("sqb", [P, 4, T], F32)
        st = sb("st", [P, 8], F32)
        ln = sb("ln", [P, 2, 4, NC], F32)
        ps = root.enter_context(nc.psum_tensor("ps", [P, 8, 512], F32))
        G0, G1, G2, G3, D0, D1, D2, D3 = range(8)
        free = [None] * 8

        def bank_wait(e, *banks):
            for b in banks:
                e.wait(free[b])

        def load(dst, src, *toks):
            pool.wait(*toks)
            return sy.done(nc.gpsimd.dma_start(dst, src), "s_ld", 16)

        def loads_done():
            return ("s_ld", sy.count["s_ld"])

        t_ccol = sy.done(nc.sync.dma_start(ccol[:, :], a["c"]), "s_c", 16)
        for dst, src in ((modb[:, :, :], a["mod_b"]), (ng[:, :, :], a["norm_g"]), (ident[:, :], a["k_ident"]),
                         (x[:, :, :], a["x"]), (inv[:, :, :], a["k_inv"]), (pos[:, :], a["positions"]),
                         (cw[:, :, :, :], a["conv"]), (rot[:, :, :, :], a["k_rot"]), (ln[:, :, :, :], a["ln"])):
            t_small = sy.done(nc.scalar.dma_start(dst, src), "s_a", 16)
        dve.done(nc.vector.memset(csil[:, :, :], 0.0))
        dve.done(nc.vector.memset(mean[:, :], 1.0 / D))
        dve.done(nc.vector.memset(epst[:, 0:1], 1e-6))
        t_ones = dve.done(nc.vector.memset(epst[:, 1:2], 1e-5))

        pieces = []

        def plan(kind, srcs):
            pieces.append(dict(kind=kind, srcs=srcs))

        def kview(w, k0, k1, c0, c1):
            return w[k0 * P:k1 * P, c0:c1].rearrange("(k p) n -> p k n", p=P)

        def plan_unit(w, c0, c1=None, kind="w", nk=NC):
            for k0 in range(0, nk, 4):
                plan(kind, [((4, 512), 0, 512, kview(w, k0, k0 + 4, c0, c0 + 512))])

        def plan_pair(w0, a0, w1, a1):
            for k0 in (0, 4):
                plan("w", [((4, 512), 0, 256, kview(w0, k0, k0 + 4, a0, a0 + 256)),
                           ((4, 512), 256, 512, kview(w1, k0, k0 + 4, a1, a1 + 256))])

        def plan_down(w):
            for i in range(FB // 2):
                plan("w", [((2, 1024), 0, 1024, kview(w, 2 * i, 2 * i + 2, 0, 1024))])

        mod_at = {}

        def plan_mod(i, u):
            plan_unit(a["mod_w"][i], 512 * u, kind="m")

        fill = {}
        order = []
        for i in range(2):
            seq = [(i, u) for u in range(18)]
            order.append(seq)
        f1 = {("ffn", 0, 0): [(0, u) for u in range(4, 12)], ("mix", 0): [(0, u) for u in range(12, 18)],
              ("ffn", 0, 1): [(1, u) for u in range(0, 6)],
              ("ffn", 1, 0): [(1, u) for u in range(6, 12)], ("mix", 1): [(1, u) for u in range(12, 18)]}

        def spread(units, n):
            at = [[] for _ in range(n)]
            for j, u in enumerate(units):
                at[min(n - 1, (j * n) // len(units))].append(u)
            return at

        steps = []

        def step(kind, **kw):
            steps.append(dict(kind=kind, **kw))

        def plan_first():
            for u in range(4):
                step("mod", i=0, u=u)
            for i in range(2):
                plan_ffn(i, 0)
                plan_mix(i)
                plan_ffn(i, 1)

        def plan_ffn(i, j):
            fl = list(f1.get(("ffn", i, j), []))
            step("norm", i=i, s=2 * j, m=fl.pop(0) if fl else None)
            at = spread(fl, 16)
            for q in range(11):
                step("gateup", i=i, j=j, q=q)
                for m in at[q]:
                    step("mod", i=m[0], u=m[1])
            for q in range(11):
                step("down", i=i, j=j, q=q)
                if q < 5:
                    for m in at[11 + q]:
                        step("mod", i=m[0], u=m[1], bank=G3)

        def plan_mix(i):
            fl = list(f1[("mix", i)])
            step("norm", i=i, s=1, m=fl.pop(0))
            if i == 0:
                for hh in range(2):
                    for r in range(3):
                        step("fox_in", hh=hh, r=r)
                        if hh == 0 and r == 0:
                            step("fox_f")
                        if fl:
                            m = fl.pop(0)
                            step("mod", i=m[0], u=m[1])
                    step("fox_attn", hh=hh)
            else:
                for hh in range(2):
                    for g in range(3):
                        for r in range(3):
                            step("dil_in", hh=hh, g=g, r=r)
                        if fl:
                            m = fl.pop(0)
                            step("mod", i=m[0], u=m[1])
                    step("dil_attn", hh=hh)
            for u in range(2):
                step("mix_out", i=i, u=u)

        def plan_second():
            for i in range(2):
                step("sec_begin", i=i)
                for u in range(3):
                    step("na_in", i=i, u=u)
                step("na_attn", i=i)
                for u in range(6):
                    step("ret_in", i=i, u=u)
                step("gate", i=i, u=0, b=0)
                for h, (u, b) in enumerate(((1, 0), (0, 1), (1, 1))):
                    step("ret", i=i, h=h)
                    step("gate", i=i, u=u, b=b)
                step("ret", i=i, h=3)
                for u, b in ((0, 0), (1, 0), (0, 1), (1, 1)):
                    step("branch", i=i, u=u, b=b)
                    if (u, b) == (1, 0):
                        step("ret_end", i=i)
                for u in range(2):
                    step("wout", i=i, u=u)
                step("ln", i=i, j=0)
                for u in range(2):
                    step("plegate", i=i, u=u)
                    step("pleproj", i=i, u=u)
                for q in range(11):
                    step("convup", i=i, q=q)
                for q in range(11):
                    step("down2", i=i, q=q)
                step("ln", i=i, j=1)

        plan_first()
        plan_second()

        def stream(s):
            k = s["kind"]
            if k == "norm" and s["m"]:
                plan_mod(*s["m"])
            elif k == "mod":
                plan_mod(s["i"], s["u"])
            elif k == "gateup":
                q = 256 * s["q"]
                plan_pair(a["ffn_w_gate"][s["i"], s["j"]], q, a["ffn_w_up"][s["i"], s["j"]], q)
            elif k == "down":
                w, q = a["ffn_w_down"][s["i"], s["j"]], s["q"]
                plan("w", [((2, 1024), 0, 1024, kview(w, 2 * q, 2 * q + 2, 0, 1024))])
            elif k == "down2":
                w, q = a["w_down_2"][s["i"]], s["q"]
                plan("w", [((2, 1024), 0, 1024, kview(w, 2 * q, 2 * q + 2, 0, 1024))])
            elif k == "fox_f":
                plan("w", [((8, 16), 0, 16, kview(a["fox_w_in"][0], 0, 8, 3072, 3088))])
            elif k == "fox_in":
                plan_unit(a["fox_w_in"][0], 1024 * s["r"] + 512 * s["hh"])
            elif k == "dil_in":
                plan_unit(a["dil_w_in"][0], 3072 * s["g"] + 1024 * s["r"] + 512 * s["hh"])
            elif k == "mix_out":
                plan_unit((a["fox_w_out"] if s["i"] == 0 else a["dil_w_out"])[0], 512 * s["u"])
            elif k == "na_in":
                plan_unit(a["w_in_2"][s["i"]], 512 * s["u"])
            elif k == "ret_in":
                plan_unit(a["w_in_2"][s["i"]], 512 * (3 + s["u"]))
            elif k == "gate":
                plan_unit(a["w_in_2"][s["i"]], 512 * (9 + 2 * s["b"] + s["u"]))
            elif k == "branch":
                if s["b"] == 0:
                    plan_unit(a["w_branch_a_2"][s["i"]], 512 * s["u"], nk=4)
                else:
                    plan_unit(a["w_branch_b_2"][s["i"]], 512 * s["u"])
            elif k == "wout":
                plan_unit(a["w_out_2"][s["i"]], 512 * s["u"])
            elif k == "plegate":
                plan_unit(a["w_ple_gate_2"][s["i"]], 512 * s["u"])
            elif k == "pleproj":
                plan("w", [((2, 512), 0, 512, kview(a["w_ple_proj_2"][s["i"]], 0, 2, 512 * s["u"], 512 * s["u"] + 512))])
            elif k == "convup":
                q = 256 * s["q"]
                plan_pair(a["w_up_2"][s["i"]], q, a["w_up_2"][s["i"]], F + q)

        for s in steps:
            stream(s)

        state = dict(dma=0, conv=0, use=0, cslot=0)
        raw_free = [None] * RAW
        conv_free = [None] * CONV

        def emit_dma(p):
            slot = p % RAW
            sp.wait(raw_free[slot])
            n = 0
            for shape, c0, c1, src in pieces[p]["srcs"]:
                size = shape[0] * shape[1]
                v = raw[:, slot, 0:size].rearrange("p (k n) -> p k n", k=shape[0])[:, :, c0:c1]
                tok = sy.done(nc.sync.dma_start(v, src), f"s_raw{slot}", 16)
                n = size
            pieces[p]["landed"] = tok
            pieces[p]["n"] = n
            pieces[p]["slot"] = slot

        def emit_conv(p):
            pc = pieces[p]
            if pc["kind"] == "m":
                return
            slot, n = pc["slot"], pc["n"]
            c = state["cslot"] % CONV
            state["cslot"] += 1
            pc["c"] = c
            act.wait(pc["landed"], conv_free[c])
            t_hi = act.done(nc.scalar.activation(whi[:, c, 0:n], raw[:, slot, 0:n], ACT.Copy))
            dve.wait(t_hi, pc["landed"], conv_free[c])
            t_lo = dve.done(nc.vector.tensor_tensor(wlo[:, c, 0:n], raw[:, slot, 0:n],
                                                    whi[:, c, 0:n].bitcast(F32), ALU.subtract))
            raw_free[slot] = [t_hi, t_lo]
            pc["conv"] = [t_hi, t_lo]

        def ensure(ahead=CONV):
            use = state["use"]
            while state["conv"] < len(pieces):
                p = state["conv"]
                if p >= use + RAW or (pieces[p]["kind"] != "m" and
                                      sum(pieces[j]["kind"] != "m" for j in range(use, p)) >= ahead):
                    break
                if state["dma"] <= p:
                    emit_dma(state["dma"])
                    state["dma"] += 1
                    continue
                emit_conv(p)
                state["conv"] += 1
            while state["dma"] < len(pieces) and state["dma"] < use + RAW:
                emit_dma(state["dma"])
                state["dma"] += 1

        def next_piece(k, n, ahead=CONV):
            ensure(ahead)
            p = state["use"]
            pc = pieces[p]
            pe.wait(pc["conv"])
            c = pc["c"]
            vh = whi[:, c, 0:k * n].rearrange("p (k n) -> p k n", k=k)
            vl = wlo[:, c, 0:k * n].rearrange("p (k n) -> p k n", k=k)
            return vh, vl, pc

        def piece_used(pc, tok):
            if pc["kind"] == "m":
                raw_free[pc["slot"]] = tok
            else:
                conv_free[pc["c"]] = tok
            state["use"] += 1

        def raw_piece(k, n):
            ensure()
            pc = pieces[state["use"]]
            pe.wait(pc["landed"])
            return raw[:, pc["slot"], 0:k * n].rearrange("p (k n) -> p k n", k=k), pc

        deferred = []

        def run_deferred():
            while deferred:
                deferred.pop(0)()

        def mm(out_, l, r, start, stop):
            return nc.tensor.matmul(out_, l, r, start=start, stop=stop, skip_group_check=True)

        pair = [0]

        def next_pair():
            pair[0] ^= 1
            return (G2, G3) if pair[0] else (G0, G1)

        def triple(o, w, v, h, l, first, final):
            mm(o, w, h, first, False)
            mm(o, v, h, False, False)
            return mm(o, w, l, False, final)

        def feature_unit(ah, al, need, nk=NC, banks=None, tail=None):
            b0, b1 = banks or next_pair()
            pe.wait(free[b0], free[b1])
            for k0 in range(0, nk, 4):
                n = min(4, nk - k0)
                end = tail and k0 + 4 >= nk
                vh, vl, pc = next_piece(n, 512, 2 if end else CONV)

                def block(m, kk):
                    o = ps[:, b0 if m < 2 else b1, (m % 2) * T:(m % 2 + 1) * T]
                    return triple(o, vh[:, kk, m * P:(m + 1) * P], vl[:, kk, m * P:(m + 1) * P], ah[:, k0 + kk, :],
                                  al[:, k0 + kk, :], k0 + kk == 0 and m % 2 == 0, k0 + kk == nk - 1)

                if end:
                    for kk in range(n):
                        pe.wait(need(k0 + kk))
                    for b in range(2):
                        for kk in range(n):
                            for m in (2 * b, 2 * b + 1):
                                ins = block(m, kk)
                        tok = pe.done(ins)
                        if b == 1:
                            piece_used(pc, tok)
                            xread[0] = tok
                        tail(b, tok)
                    return b0, b1, tok
                for kk in range(n):
                    kc = k0 + kk
                    nd = need(kc)
                    pe.wait(nd[0])
                    for m in range(4):
                        o = ps[:, b0 if m < 2 else b1, (m % 2) * T:(m % 2 + 1) * T]
                        w, v = vh[:, kk, m * P:(m + 1) * P], vl[:, kk, m * P:(m + 1) * P]
                        mm(o, w, ah[:, kc, :], kc == 0 and m % 2 == 0, False)
                        mm(o, v, ah[:, kc, :], False, False)
                    pe.wait(nd[1])
                    for m in range(4):
                        o = ps[:, b0 if m < 2 else b1, (m % 2) * T:(m % 2 + 1) * T]
                        ins = mm(o, vh[:, kk, m * P:(m + 1) * P], al[:, kc, :], False, kc == nk - 1)
                tok = pe.done(ins)
                piece_used(pc, tok)
            xread[0] = tok
            run_deferred()
            return b0, b1, tok

        def token_unit(need):
            b0, b1 = next_pair()
            pe.wait(free[b0], free[b1])
            for k0 in range(0, NC, 4):
                vh, vl, pc = next_piece(4, 512)
                for kk in range(4):
                    kc = k0 + kk
                    nd = need(kc)
                    pe.wait(nd[0])
                    for t in range(2):
                        o, h = ps[:, (b0, b1)[t], :], xhi[:, kc, t * P:(t + 1) * P]
                        mm(o, h, vh[:, kk, :], kc == 0, False)
                        mm(o, h, vl[:, kk, :], False, False)
                    pe.wait(nd[1])
                    for t in range(2):
                        ins = mm(ps[:, (b0, b1)[t], :], xlo[:, kc, t * P:(t + 1) * P], vh[:, kk, :], False,
                                 kc == NC - 1)
                tok = pe.done(ins)
                piece_used(pc, tok)
            xread[0] = tok
            run_deferred()
            return b0, b1, tok

        act.wait(t_ccol, t_ones)
        t_c = act.done(nc.scalar.activation(csil[:, :, 0], ccol[:, :], ACT.Silu))
        mod_tok = {}
        mrow_free = [None]

        def mod_unit(i, u, bank):
            pe.wait(t_c, free[bank])
            for h in range(2):
                v, pc = raw_piece(4, 512)
                for kk in range(4):
                    ins = mm(ps[32 * kk:32 * kk + 32, bank, :], csil[:, 4 * h + kk, :], v[:, kk, :], h == 0, h == 1)
                tok = pe.done(ins)
                piece_used(pc, tok)
            run_deferred()
            act.wait(tok, mrow_free[0])
            t = act.done(nc.scalar.activation(mrow[:, :], ps[:, bank, :], ACT.Copy))
            free[bank] = t
            deferred.append(lambda: mod_turn(i, u, bank, t))

        def mod_turn(i, u, bank, t):
            pe.wait(t, free[bank], t_small)
            for m in range(4):
                ins = nc.tensor.transpose(ps[:, bank, m * P:(m + 1) * P], mrow[:, m * P:(m + 1) * P], ident[:, :])
            tok = pe.done(ins)
            mrow_free[0] = tok
            c0 = mod[:, 4 * u:4 * u + 4]
            dve.wait(tok, mod_tok.get(("used", u // 2)), t_small)
            t = dve.done(nc.vector.tensor_reduce(
                c0, ps[:, bank, :].rearrange("p (m g n) -> p m g n", m=4, g=4)[:, :, :, 0], AX.X, ALU.add))
            free[bank] = t
            dve.wait(t)
            t = dve.done(nc.vector.tensor_tensor(c0, c0, modb[:, i, 4 * u:4 * u + 4], ALU.add))
            s, kind = u // 6, (u % 6) // 2
            if u % 2:
                dve.wait(t)
                c0 = (3 * s + kind) * NC
                if kind == 1:
                    t = dve.done(nc.vector.scalar_tensor_tensor(
                        out=ascale[:, s, :], in0=mod[:, c0:c0 + NC], scalar=1.0, in1=ng[:, 3 * i + s, :],
                        op0=ALU.add, op1=ALU.mult))
                elif kind == 2:
                    t = dve.done(nc.vector.tensor_scalar(gs[:, s, :], mod[:, c0:c0 + NC], 1.0 if s == 1 else 0.5,
                                                         None, ALU.mult))
                mod_tok[(i, s, kind)] = t

        xt = [t_small] * NC
        xn_tok = [None] * NC

        def spread_columns(tok, bank):
            pe.wait(tok, free[bank], t_small)
            for t in range(2):
                ins = mm(ps[:, bank, t * P:(t + 1) * P], st[:, 2 + t:3 + t].to_broadcast([P, P]),
                         ident[:, :], t == 0, True)
            return pe.done(ins)

        def preload(func):
            act.wait(t_ones)
            act.done(nc.scalar.activation(st[:, 6:7], epst[:, 0:1], func))

        def square(m, tok):
            s = m % 4
            act.wait(tok, sq_free[s])
            return act.done(nc.scalar.activation(sqb[:, s, :], x[:, m, :], ACT.Square))

        def stat(m, tok, squares):
            pe.wait(tok, t_ones)
            if m == 0:
                pe.wait(free[G0])
            t = pe.done(mm(ps[:, G0, 0:T], mean[:, :], sqb[:, m % 4, :] if squares else x[:, m, :], m == 0,
                           m == NC - 1))
            if squares:
                sq_free[m % 4] = t
            return t

        def rstd_row(tok, eps, src=G0, dst=G1, between=None):
            dve.wait(tok, t_small)
            for t in range(2):
                td = dve.done(nc.vector.tensor_tensor_reduce(
                    junk[:, t, :], ps[:, src, t * P:(t + 1) * P], ident[:, :], 1.0, 0.0, ALU.mult, ALU.add,
                    st[:, 4 + t:5 + t]))
            free[src] = td
            act.wait(td, t_ones)
            ta = act.done(nc.scalar.activation(st[:, 0:2], st[:, 4:6], ACT.Sqrt, bias=epst[:, eps:eps + 1]))
            dve.wait(ta)
            tr = dve.done(nc.vector.reciprocal(st[:, 2:4], st[:, 0:2]))
            if between:
                between()
            return spread_columns(tr, dst)

        sq_free = [None] * 4
        junk = sb("junk", [P, 2, P], F32)
        nb_free = [None] * 4
        xread = [None]

        def split_chunk(m, src, tok):
            act.wait(tok, xread[0])
            th = act.done(nc.scalar.activation(xhi[:, m, :], src, ACT.Copy))
            dve.wait(th)
            tl = dve.done(nc.vector.tensor_tensor(xlo[:, m, :], src, xhi[:, m, :].bitcast(F32), ALU.subtract))
            xn_tok[m] = [th, tl]
            return tl

        class Tail:

            def __init__(self, update, mode, lag=2):
                self.update, self.mode, self.lag = update, mode, lag
                self.queue = []
                self.tok = None
                run_deferred()
                if mode == "square":
                    preload(ACT.Sqrt)

            def add(self, chunks):
                for m in chunks:
                    self.update(m)
                    if self.mode == "split":
                        split_chunk(m, x[:, m, :], xt[m])
                if self.mode != "split":
                    self.queue.append([(m, square(m, xt[m]) if self.mode == "square" else xt[m]) for m in chunks])

            def flush(self, left):
                while len(self.queue) > left:
                    for m, tok in self.queue.pop(0):
                        self.tok = stat(m, tok, self.mode == "square")

            def step(self, chunks):
                if self.mode == "square":
                    self.flush(1)
                self.add(chunks)
                self.flush(self.lag)

        def norm(i, s, nbuf, tok, between=None):
            tb = rstd_row(tok, 0, between=between)
            pend = []
            c0 = 3 * s * NC
            am, bm = mod_tok[(i, s, 0)], mod_tok[(i, s, 1)]

            def low(m, b, th, tv):
                dve.wait(th, tv)
                tl = dve.done(nc.vector.tensor_tensor(xlo[:, m, :], nbuf[:, b, :], xhi[:, m, :].bitcast(F32),
                                                      ALU.subtract))
                xn_tok[m] = [th, tl]
                nb_free[b] = tl

            for m in range(NC):
                b = m % 4
                if m == 4:
                    ensure(2)
                dve.wait(tb, nb_free[b], xt[m])
                t1 = dve.done(nc.vector.tensor_tensor(nbuf[:, b, :], x[:, m, :], ps[:, G1, 0:T], ALU.mult))
                act.wait(t1, am, bm, xread[0])
                sc, bi = ascale[:, s, m:m + 1], mod[:, c0 + m:c0 + m + 1]
                th = act.done(nc.scalar.activation(xhi[:, m, :], nbuf[:, b, :], ACT.Identity, scale=sc, bias=bi))
                tv = act.done(nc.scalar.activation(nbuf[:, b, :], nbuf[:, b, :], ACT.Identity, scale=sc, bias=bi))
                pend.append((m, b, th, tv))
                if len(pend) > 1:
                    low(*pend.pop(0))
            low(*pend.pop(0))
            free[G1] = t1
            mod_tok[("used", 3 * s)] = tv
            ensure()

        def need_x(kc):
            return xn_tok[kc]

        def enter(bar=True):
            c = ExitStack()
            toks = [last(pe), last(act), last(dve), last(pool), loads_done()]
            for e in (act, dve, pool):
                e.wait(toks)
            return c

        wk = {}

        def ffn_begin():
            c = enter()
            wk["ctx"] = c
            wk["nbuf"] = sb("nbuf" + tag(), [P, 4, T], F32, c)
            wk["hhi"] = sb("hhi" + tag(), [P, FB, T], F32R, c)
            wk["hlo"] = sb("hlo" + tag(), [P, FB, T], F32R, c)
            wk["e1"] = sb("e1" + tag(), [P, 2, 512], F32, c)
            wk["e2"] = sb("e2" + tag(), [P, 2, 512], F32, c)
            wk["ht"] = [None] * FB
            wk["dt"] = [None] * NC
            wk["ef"] = [None] * 2

        tags = [0]

        def tag():
            tags[0] += 1
            return f"_{tags[0]}"

        def gateup(q):
            b0, b1, tok = feature_unit(xhi, xlo, need_x)
            s = q % 2
            e1, e2 = wk["e1"][:, s, :], wk["e2"][:, s, :]
            act.wait(tok, wk["ef"][s])
            ta = act.done(nc.scalar.activation(e1, ps[:, b0, :], ACT.Silu))
            free[b0] = ta
            dve.wait(ta, tok)
            td = dve.done(nc.vector.tensor_tensor(e2, e1, ps[:, b1, :], ALU.mult))
            free[b1] = td
            hidden_split(q, e2, td, s)

        def hidden_split(q, src, td, s):
            h = wk["hhi"][:, 2 * q:2 * q + 2, :].rearrange("p k n -> p (k n)")
            l = wk["hlo"][:, 2 * q:2 * q + 2, :].rearrange("p k n -> p (k n)")
            act.wait(td)
            th = act.done(nc.scalar.activation(h, src, ACT.Copy))
            dve.wait(th)
            tl = dve.done(nc.vector.tensor_tensor(l, src, h.bitcast(F32), ALU.subtract))
            wk["ef"][s] = tl
            wk["ht"][2 * q] = wk["ht"][2 * q + 1] = [th, tl]

        def down(q, tail=None):
            if q == 0:
                pe.wait(free[D0], free[D1], free[D2], free[D3])
            end = q == FB // 2 - 1
            vh, vl, pc = next_piece(2, 1024, 2 if end else CONV)
            hh, hl = wk["hhi"], wk["hlo"]

            def block(k, m):
                kk = k - 2 * q
                return triple(ps[:, D0 + m // 2, (m % 2) * T:(m % 2 + 1) * T], vh[:, kk, m * P:(m + 1) * P],
                              vl[:, kk, m * P:(m + 1) * P], hh[:, k, :], hl[:, k, :], k == 0 and m % 2 == 0,
                              k == FB - 1)

            if not end:
                for k in (2 * q, 2 * q + 1):
                    pe.wait(wk["ht"][k])
                    for m in range(NC):
                        ins = block(k, m)
                piece_used(pc, pe.done(ins))
                run_deferred()
                return
            pe.wait(wk["ht"][2 * q], wk["ht"][2 * q + 1])
            for b in range(4):
                for k in (2 * q, 2 * q + 1):
                    for m in (2 * b, 2 * b + 1):
                        ins = block(k, m)
                tok = pe.done(ins)
                wk["dt"][2 * b] = wk["dt"][2 * b + 1] = tok
                if b == 3:
                    piece_used(pc, tok)
                tail.step((2 * b, 2 * b + 1))
            tail.flush(0)

        def dblk(m):
            return ps[:, D0 + m // 2, (m % 2) * T:(m % 2 + 1) * T]

        def residual(i, s):
            def update(m):
                dve.wait(wk["dt"][m], mod_tok[(i, s, 2)], xt[m])
                xt[m] = dve.done(nc.vector.scalar_tensor_tensor(
                    out=x[:, m, :], in0=dblk(m), scalar=gs[:, s, m:m + 1], in1=x[:, m, :],
                    op0=ALU.mult, op1=ALU.add))
                free[D0 + m // 2] = xt[m]
            return update

        def out_unit(u, ah, al, need, tail=None):
            wk.setdefault("dt", [None] * NC)
            if u == 0:
                _, _, tok = feature_unit(ah, al, need, banks=(D0, D1))
                wk["dt"][0:4] = [tok] * 4
                return
            first = [True]

            def on_bank(b, tok):
                wk["dt"][4 + 2 * b] = wk["dt"][5 + 2 * b] = tok
                if first[0]:
                    first[0] = False
                    tail.step((0, 1))
                    tail.step((2, 3))
                tail.step((4 + 2 * b, 5 + 2 * b))

            feature_unit(ah, al, need, banks=(D2, D3), tail=on_bank)
            tail.flush(0)

        def attn_scratch(c, n):
            wk["S"] = sb("S" + tag(), [P, 3, n], F32, c)
            wk["PT"] = sb("PT" + tag(), [P, 4, n], F32, c)
            wk["nm"] = sb("nm" + tag(), [P, 16], F32, c)
            wk["rs"] = sb("rs" + tag(), [P, 16], F32, c)
            wk["ri"] = sb("ri" + tag(), [P, 16], F32, c)
            wk["afree"] = dict(s=[None] * 3, pt=[None] * 4)

        def attention(groups, klen, bias, emit, toks):
            seq = [(2 * c + w, qt) for c in range(4) for qt in range(2) for w in range(2)]
            rec = []
            S, PT, nm, rs, ri = wk["S"], wk["PT"], wk["nm"], wk["rs"], wk["ri"]
            pe.wait(toks)
            s_free, pt_free = wk["afree"]["s"], wk["afree"]["pt"]

            def scores(j):
                h, qt = seq[j]
                kl = klen(qt)
                b = D0 + 2 * (j % 2)
                pe.wait(free[b], free[b + 1])
                r, c = (h % 2) * 64, h // 2
                for g, (qT, kT, v) in enumerate(groups):
                    bk, off = b + (g * kl) // 512, (g * kl) % 512
                    ins = mm(ps[:, bk, off:off + kl], qT[r:r + 64, c, qt * P:(qt + 1) * P],
                             kT[r:r + 64, c, 0:kl], True, True)
                tok = pe.done(ins)
                n = kl * len(groups)
                s = j % 3
                sv = S[:, s, 0:n]
                pv = ps[:, b:b + 2, :].rearrange("p a n -> p (a n)")[:, 0:n]
                dve.wait(tok, s_free[s])
                td = dve.done(nc.vector.tensor_tensor_reduce(sv, pv, bias(h, qt), 1.0, 3e38, ALU.add, ALU.min,
                                                             nm[:, j:j + 1]))
                free[b] = free[b + 1] = td
                act.wait(td)
                ta = act.done(nc.scalar.activation(sv, sv, ACT.Exp, bias=nm[:, j:j + 1], scale=-1.0,
                                                   accum_out=rs[:, j:j + 1]))
                rec.append((sv, ta, n, kl))

            def weigh(j):
                sv, ta, n, kl = rec[j]
                dve.wait(ta)
                tr = dve.done(nc.vector.reciprocal(ri[:, j:j + 1], rs[:, j:j + 1]))
                dve.wait(tr)
                tn = dve.done(nc.vector.tensor_scalar(sv, sv, ri[:, j:j + 1], None, ALU.mult))
                rec[j] = (sv, tn, n, kl)

            def turn(j):
                sv, ta, n, kl = rec[j]
                bt = G0 if n > 512 else G0 + j % 2
                banks = (G0, G1) if n > 512 else (bt,)
                pe.wait(ta, t_small)
                bank_wait(pe, *banks)
                for b in range(n // P):
                    o = ps[:, bt + b // 4, (b % 4) * P:(b % 4 + 1) * P]
                    ins = nc.tensor.transpose(o, sv[:, b * P:(b + 1) * P], ident[:, :])
                tok = pe.done(ins)
                s_free[j % 3] = tok
                s = j % 4
                pv = ps[:, bt:bt + len(banks), :].rearrange("p a n -> p (a n)")[:, 0:n]
                act.wait(tok, pt_free[s])
                te = act.done(nc.scalar.activation(PT[:, s, 0:n], pv, ACT.Copy))
                for b in banks:
                    free[b] = te
                rec[j] = rec[j] + (te,)

            def values(j):
                h, qt = seq[j]
                c = h // 2
                bank = G2 + c % 2
                if qt == 0:
                    pe.wait(free[bank])
                pe.wait(rec[j - 1][4], rec[j][4])
                kl = rec[j][3]
                nb = kl // P
                tot = nb * len(groups)
                for b in range(tot):
                    g, kb = b // nb, b % nb
                    for w in range(2):
                        hd = 2 * c + w
                        ins = mm(ps[64 * w:64 * w + 64, bank, qt * P:(qt + 1) * P],
                                 groups[g][2][:, kb, hd * 64:(hd + 1) * 64],
                                 PT[:, (j - 1 + w) % 4, b * P:(b + 1) * P], b == 0, b == tot - 1)
                tok = pe.done(ins)
                pt_free[(j - 1) % 4] = pt_free[j % 4] = tok
                if qt == 1:
                    emit(c, bank, tok)

            n = len(seq)
            for j in range(n + 3):
                if j < n:
                    scores(j)
                if 0 <= j - 1 < n:
                    weigh(j - 1)
                if 0 <= j - 2 < n:
                    turn(j - 2)
                if j >= 4 and j % 2 == 0:
                    values(j - 3)

        def emit_split(hi, lo, res):
            def emit(c, bank, tok):
                act.wait(tok)
                th = act.done(nc.scalar.activation(hi[:, c, :], ps[:, bank, 0:T], ACT.Copy))
                dve.wait(th, tok)
                tl = dve.done(nc.vector.tensor_tensor(lo[:, c, :], ps[:, bank, 0:T], hi[:, c, :].bitcast(F32),
                                                      ALU.subtract))
                free[bank] = tl
                res[c] = [th, tl]
            return emit

        def emit_keep(dst, res):
            def emit(c, bank, tok):
                act.wait(tok)
                res[c] = act.done(nc.scalar.activation(dst[:, c, :], ps[:, bank, 0:T], ACT.Copy))
                free[bank] = res[c]
            return emit

        def mix_attention(hh, *args):
            if hh == 0:
                wk["ores"] = [None] * 4
                attention(*args[:-1], emit_keep(wk["oT"], wk["ores"]), args[-1])
                return
            dve.wait(xread[0])
            for c in range(4):
                split_chunk(c, wk["oT"][:, c, :], wk["ores"][c])
            res = [None] * 4
            attention(*args[:-1], emit_split(xhi[:, 4:8, :], xlo[:, 4:8, :], res), args[-1])
            xn_tok[4:8] = res

        def turn_chunks(src, n, toks, banks, scale=None):
            pe.wait(toks, t_small)
            for b in banks:
                pe.wait(free[b])
            out_ = []
            for c in range(n):
                for t in range(2):
                    o = ps[:, banks[c // 2], (c % 2) * T + t * P:(c % 2) * T + (t + 1) * P]
                    ins = nc.tensor.transpose(o, src[:, t, c * P:(c + 1) * P], ident[:, :])
                out_.append(pe.done(ins))
            return out_

        def turn_split(src, n, toks, hi, lo, c0=0, banks=(G0, G1, G2, G3)):
            tk = turn_chunks(src, n, toks, banks[:n // 2])
            res = []
            for j in range(n // 2):
                b = banks[j]
                h = hi[:, c0 + 2 * j:c0 + 2 * j + 2, :].rearrange("p k n -> p (k n)")
                l = lo[:, c0 + 2 * j:c0 + 2 * j + 2, :].rearrange("p k n -> p (k n)")
                act.wait(tk[2 * j + 1])
                th = act.done(nc.scalar.activation(h, ps[:, b, :], ACT.Copy))
                dve.wait(th, tk[2 * j + 1])
                tl = dve.done(nc.vector.tensor_tensor(l, ps[:, b, :], h.bitcast(F32), ALU.subtract))
                free[b] = tl
                res += [[th, tl], [th, tl]]
            return res

        def head_norm(b0, b1, tok, gain, dstT, turned=False):
            y = ps[:, b0:b0 + 2, :].rearrange("p t (h d) -> p (t h) d", d=64)
            tm, hs = wk["tm"], wk["hs"]
            act.wait(tok, wk["tmf"])
            ta = act.done(nc.scalar.activation(tm[:, :, :], ps[:, b0:b0 + 2, :], ACT.Square))
            dve.wait(ta)
            t1 = dve.done(nc.vector.tensor_reduce(hs[:, 0, :], tm[:, :, :].rearrange("p t (h d) -> p (t h) d", d=64),
                                                  AX.X, ALU.add))
            act.wait(t1)
            t2 = act.done(nc.scalar.activation(hs[:, 1, :], hs[:, 0, :], ACT.Sqrt, scale=1.0 / 64,
                                               bias=epst[:, 0:1]))
            dve.wait(t2)
            t3 = dve.done(nc.vector.reciprocal(hs[:, 2, :], hs[:, 1, :]))
            dve.wait(t3, tok, wk["tmf"])
            tv = tm[:, :, :].rearrange("p t (h d) -> p (t h) d", d=64)
            t4 = dve.done(nc.vector.tensor_tensor(tv, y, hs[:, 2, :].unsqueeze(2).to_broadcast([P, 16, 64]),
                                                  ALU.mult))
            free[b0] = free[b1] = [t4, ta]
            dve.wait(t4)
            t5 = dve.done(nc.vector.tensor_tensor(tv, tv, gain.unsqueeze(1).to_broadcast([P, 16, 64]), ALU.mult))
            if turned:
                r4 = tm[:, :, :].rearrange("p t (h d) -> p t h d", d=64)
                ra = wk["ra"][:, :, :, :]
                dve.wait(t5)
                co, si = rope[:, 0, :, :], rope[:, 1, :, :]
                for t in range(2):
                    dve.done(nc.vector.tensor_tensor(ra[:, t, :, 0:16], r4[:, t, :, 0:16],
                                                     co[:, t, :].unsqueeze(1).to_broadcast([P, 8, 16]), ALU.mult))
                    dve.done(nc.vector.tensor_tensor(ra[:, t, :, 16:24], r4[:, t, :, 8:16],
                                                     si[:, t, 0:8].unsqueeze(1).to_broadcast([P, 8, 8]), ALU.mult))
                    t6 = dve.done(nc.vector.tensor_tensor(ra[:, t, :, 24:32], r4[:, t, :, 0:8],
                                                          si[:, t, 8:16].unsqueeze(1).to_broadcast([P, 8, 8]),
                                                          ALU.mult))
                dve.wait(t6)
                t5 = dve.done(nc.vector.tensor_tensor(
                    tv[:, :, 0:16], ra[:, :, :, 0:16].rearrange("p t h d -> p (t h) d"),
                    ra[:, :, :, 16:32].rearrange("p t h d -> p (t h) d"), ALU.add))
            deferred.append(lambda: head_turn(t5, dstT))

        def head_turn(t5, dstT):
            tk = turn_chunks(wk["tm"], 4, t5, (D0, D1))
            act.wait(tk[-1])
            te = act.done(nc.scalar.activation(dstT[:, :, :], ps[:, D0:D0 + 2, :].rearrange(
                "p b (c n) -> p (b c) n", c=2), ACT.Copy))
            free[D0] = free[D1] = te
            wk["tmf"] = tk[-1]
            wk["at"].append(te)

        def keep_v(b0, b1, tok, dst):
            act.wait(tok)
            t = act.done(nc.scalar.activation(dst, ps[:, b0:b0 + 2, :], ACT.Copy))
            free[b0] = free[b1] = t
            wk["at"].append(t)

        def fox_begin():
            c = wk["ctx"]
            wk["at"] = []
            wk["tmf"] = None
            wk["qT"] = sb("fqT", [P, 4, T], F32, c)
            wk["kT"] = sb("fkT", [P, 4, T], F32, c)
            wk["v"] = sb("fv", [P, 2, 512], F32, c)
            wk["tm"] = sb("ftm", [P, 2, 512], F32, c)
            wk["hs"] = sb("fhs", [P, 3, 16], F32, c)
            wk["oT"] = sb("foT", [P, 4, T], F32, c)
            wk["bias"] = sb("fbias", [P, 8, 384], F32, c)
            wk["cm"] = sb("fcm", [P, T], F32, c)
            wk["gq"] = sb("fgq", [P, 2, 64], F32, c)
            wk["nbuf"] = sb("fnb", [P, 4, T], F32, c)
            wk["bf"] = sb("fbf", [16, 1], F32, c)
            wk["fl"] = sb("ffl", [16, 4, T], F32, c)
            wk["cT"] = sb("fcT", [P, T], F32, c)
            attn_scratch(c, T)
            load(wk["cm"][:, :], a["k_causal"])
            load(wk["gq"][:, 0, :], a["fox_q_g"])
            load(wk["gq"][:, 1, :], a["fox_k_g"])
            load(wk["bf"][:, :], a["fox_b_f"])
            wk["ldt"] = loads_done()

        def fox_gain():
            dve.wait(wk["ldt"])
            wk["gt"] = dve.done(nc.vector.tensor_scalar(wk["gq"][:, 0, :], wk["gq"][:, 0, :], -0.125, None, ALU.mult))

        def fox_f():
            b, _ = next_pair()
            pe.wait(free[b])
            vh, vl, pc = next_piece(NC, 16)
            for kc in range(NC):
                pe.wait(xn_tok[kc])
                ins = triple(ps[0:16, b, 0:T], vh[:, kc, :], vl[:, kc, :], xhi[:, kc, :], xlo[:, kc, :], kc == 0,
                             kc == NC - 1)
            tok = pe.done(ins)
            piece_used(pc, tok)
            fl = wk["fl"]
            z, t_, l_, o_ = fl[:, 0, :], fl[:, 1, :], fl[:, 2, :], fl[:, 3, :]
            act.wait(tok, wk["ldt"])
            t1 = act.done(nc.scalar.activation(z, ps[0:16, b, 0:T], ACT.Identity, bias=wk["bf"][:, 0:1]))
            free[b] = t1
            act.wait(t1)
            t2 = act.done(nc.scalar.activation(t_, z, ACT.Abs))
            act.wait(t2)
            t3 = act.done(nc.scalar.activation(t_, t_, ACT.Exp, scale=-1.0))
            act.wait(t3)
            t4 = act.done(nc.scalar.activation(l_, t_, ACT.Ln, bias=1.0))
            t0 = dve.done(nc.vector.memset(wk["cT"][:, :], 0.0))
            dve.wait(t4)
            t5 = dve.done(nc.vector.scalar_tensor_tensor(out=z, in0=z, scalar=0.0, in1=l_, op0=ALU.min,
                                                         op1=ALU.subtract))
            t6 = dve.done(nc.vector.memset(o_, 1.0))
            dve.wait(t5, t6, t0)
            wk["ct"] = dve.done(nc.vector.tensor_tensor_scan(wk["cT"][0:16, :], o_, z, 0.0, ALU.mult, ALU.add))

        def fox_bias(hh):
            pe.wait(wk["ct"], t_small)
            dve.wait(wk["ldt"], last(pe))
            for h in range(8):
                g = 8 * hh + h
                b = D2 + h % 2
                pe.wait(free[b])
                tok = pe.done(mm(ps[:, b, 0:T], ident[:, g:g + 1].to_broadcast([P, P]), wk["cT"][:, :],
                                 True, True))
                dve.wait(tok)
                dve.done(nc.vector.tensor_tensor(wk["bias"][:, h, 0:P], ps[:, b, 0:P], wk["cm"][:, P:T], ALU.add))
                t = dve.done(nc.vector.tensor_tensor(wk["bias"][:, h, P:384], ps[:, b, 0:T], wk["cm"][:, :],
                                                     ALU.add))
                free[b] = t
            wk["at"].append(t)

        def fox_in(hh, r):
            if r == 0:
                wk["at"] = []
            b0, b1, tok = token_unit(need_x)
            if r < 2:
                act.wait(wk["gt"])
                dve.wait(wk["gt"], wk["ldt"])
                head_norm(b0, b1, tok, wk["gq"][:, r, :], (wk["qT"], wk["kT"])[r])
            else:
                keep_v(b0, b1, tok, wk["v"][:, :, :])

        def fox_attn(hh):
            fox_bias(hh)
            mix_attention(hh, [(wk["qT"], wk["kT"], wk["v"])], lambda qt: P * (qt + 1),
                          lambda h, qt: wk["bias"][:, h, 0:P] if qt == 0 else wk["bias"][:, h, P:384], wk["at"])

        def dil_begin():
            c = wk["ctx"]
            wk["at"] = []
            wk["tmf"] = None
            for g in range(3):
                wk[f"qT{g}"] = sb(f"dqT{g}", [P, 4, T], F32, c)
                wk[f"kT{g}"] = sb(f"dkT{g}", [P, 4, T], F32, c)
                wk[f"v{g}"] = sb(f"dv{g}", [P, 2, 512], F32, c)
            wk["tm"] = sb("dtm", [P, 2, 512], F32, c)
            wk["hs"] = sb("dhs", [P, 3, 16], F32, c)
            wk["ra"] = sb("dra", [P, 2, 8, 32], F32, c)
            wk["oT"] = sb("doT", [P, 4, T], F32, c)
            wk["mask"] = sb("dmask", [P, 1152], F32, c)
            wk["gn"] = sb("dgn", [P, 2, 3, 64], F32, c)
            attn_scratch(c, 768)
            load(wk["mask"][:, :], a["k_mask"])
            load(wk["gn"][:, 0, :, :], a["dil_q_g"])
            load(wk["gn"][:, 1, :, :], a["dil_k_g"])
            wk["ldt"] = loads_done()

        def dil_gain():
            dve.wait(wk["ldt"])
            wk["gt"] = dve.done(nc.vector.tensor_scalar(wk["gn"][:, 0, :, :], wk["gn"][:, 0, :, :], -0.125, None,
                                                        ALU.mult))

        def chain(*fs):
            for f in fs:
                t = dve.done(f())
                dve.wait(t)
            return t

        def make_rope():
            tmp = ExitStack()
            rp = sb("rp", [P, 5, 2, 16], F32, tmp)
            posf = sb("posf", [P, 2], F32, tmp)
            V = nc.vector
            c1 = 6.28125
            c2 = 0.0019350051879882812
            c3 = 2 * math.pi - c1 - c2
            magic = 12582912.0
            ang = rp[:, 0, :, :]
            dve.wait(t_small)
            chain(lambda: V.tensor_copy(posf[:, :], pos[:, :]))
            for t in range(2):
                chain(lambda: V.tensor_scalar(rp[:, 0, t, :], inv[:, 0, :], posf[:, t:t + 1], None, ALU.mult))
            for w, (off, q, r) in enumerate(((0.25, 1, 2), (0.0, 3, 4))):
                n, d = rp[:, q, :, :], rp[:, r, :, :]
                chain(lambda: V.tensor_scalar(n, ang, 1.0 / (2 * math.pi), off, ALU.mult, ALU.add),
                      lambda: V.tensor_scalar(n, n, magic, None, ALU.add),
                      lambda: V.tensor_scalar(n, n, -magic, None, ALU.add),
                      lambda: V.scalar_tensor_tensor(out=d, in0=n, scalar=-c1, in1=ang, op0=ALU.mult, op1=ALU.add),
                      lambda: V.scalar_tensor_tensor(out=d, in0=n, scalar=-c2, in1=d, op0=ALU.mult, op1=ALU.add),
                      lambda: V.scalar_tensor_tensor(out=d, in0=n, scalar=-c3, in1=d, op0=ALU.mult, op1=ALU.add),
                      lambda: V.tensor_scalar(d, d, math.pi / 2 if w == 0 else 0.0, None, ALU.add),
                      lambda: V.tensor_scalar(d, d, 3.1415925, -3.1415925, ALU.min, ALU.max))
            act.wait(last(dve))
            act.done(nc.scalar.activation(rope[:, 0, :, :], rp[:, 2, :, :], ACT.Sin))
            t = act.done(nc.scalar.activation(rp[:, 0, :, :], rp[:, 4, :, :], ACT.Sin))
            dve.wait(t)
            wk["rt"] = dve.done(V.tensor_tensor(rope[:, 1, :, :], rp[:, 0, :, :], inv[:, 1, :].unsqueeze(1)
                                                .to_broadcast([P, 2, 16]), ALU.mult))
            tmp.close()

        def dil_in(hh, g, r):
            if r == 0 and g == 0:
                wk["at"] = []
            b0, b1, tok = token_unit(need_x)
            if r < 2:
                dve.wait(wk["gt"], wk["ldt"], wk["rt"])
                head_norm(b0, b1, tok, wk["gn"][:, r, g, :], wk[f"{'qk'[r]}T{g}"], turned=True)
            else:
                keep_v(b0, b1, tok, wk[f"v{g}"][:, :, :])

        def dil_attn(hh):
            mix_attention(hh, [(wk[f"qT{g}"], wk[f"kT{g}"], wk[f"v{g}"]) for g in range(3)],
                          lambda qt: P * (qt + 1),
                          lambda h, qt: wk["mask"][:, 0:384] if qt == 0 else wk["mask"][:, 384:1152], wk["at"])

        def split_x(toks, free_last=True):
            for m in range(NC):
                split_chunk(m, x[:, m, :], toks[m])

        def layer_norm(i, j, nxt, tok):
            preload(ACT.Sqrt)
            for m in range(NC):
                dve.wait(tok, xt[m])
                xt[m] = dve.done(nc.vector.tensor_tensor(x[:, m, :], x[:, m, :], ps[:, G0, 0:T], ALU.subtract))
                pe.wait(square(m, xt[m]))
                if m == 0:
                    pe.wait(free[G1])
                tk = pe.done(mm(ps[:, G1, 0:T], mean[:, :], sqb[:, m % 4, :], m == 0, m == NC - 1))
                sq_free[m % 4] = tk
            free[G0] = xt[-1]
            tb = rstd_row(tk, 1, G1, G0)
            pend = []

            def low(m, th):
                dve.wait(th, xt[m])
                xn_tok[m] = [th, dve.done(nc.vector.tensor_tensor(xlo[:, m, :], x[:, m, :],
                                                                  xhi[:, m, :].bitcast(F32), ALU.subtract))]

            for m in range(NC):
                if m == 4:
                    ensure(2)
                dve.wait(tb, xt[m])
                t1 = dve.done(nc.vector.tensor_tensor(x[:, m, :], x[:, m, :], ps[:, G0, 0:T], ALU.mult))
                act.wait(t1, t_small)
                g, b = ln[:, i, 2 * j, m:m + 1], ln[:, i, 2 * j + 1, m:m + 1]
                if nxt:
                    act.wait(xread[0])
                    th = act.done(nc.scalar.activation(xhi[:, m, :], x[:, m, :], ACT.Identity, scale=g, bias=b))
                xt[m] = act.done(nc.scalar.activation(x[:, m, :], x[:, m, :], ACT.Identity, scale=g, bias=b))
                if nxt:
                    pend.append((m, th))
                    if len(pend) > 1:
                        low(*pend.pop(0))
            if nxt:
                low(*pend.pop(0))
            free[G0] = t1
            ensure()

        def na_begin(i):
            c = enter()
            wk["ctx"] = c
            wk["yahi"] = sb("yahi" + tag(), [P, 4, T], F32R, c)
            wk["yalo"] = sb("yalo" + tag(), [P, 4, T], F32R, c)
            wk["sg"] = sb("sg" + tag(), [P, 2, 2, 1024], F32, c)
            wk["sgt"] = [[None, None], [None, None]]
            n = ExitStack()
            wk["nctx"] = n
            wk["at"] = []
            wk["qT"] = sb("nqT" + tag(), [P, 4, T], F32, n)
            wk["kT"] = sb("nkT" + tag(), [P, 4, T], F32, n)
            wk["v"] = sb("nv" + tag(), [P, 2, 512], F32, n)
            wk["bias"] = sb("nbias" + tag(), [P, 8, 2, T], F32, n)
            attn_scratch(n, T)
            load(wk["bias"][:, :, :, :], a["na_rpb_2"][i])
            pool.wait(loads_done())
            wk["at"].append(pool.done(nc.gpsimd.tensor_scalar(wk["bias"][:, :, :, :], wk["bias"][:, :, :, :], -1.0,
                                                              None, ALU.mult)))

        def na_in(u):
            if u < 2:
                b0, b1, tok = feature_unit(xhi, xlo, need_x)
                dst = (wk["qT"], wk["kT"])[u]
                act.wait(tok)
                t = act.done(nc.scalar.activation(dst[:, :, :], ps[:, b0:b0 + 2, :].rearrange(
                    "p b (c n) -> p (b c) n", c=2), ACT.Copy, scale=-0.125 if u == 0 else 1.0))
                free[b0] = free[b1] = t
                wk["at"].append(t)
            else:
                b0, b1, tok = token_unit(need_x)
                keep_v(b0, b1, tok, wk["v"][:, :, :])

        def na_attn():
            dve.wait(wk["at"])
            wk["yat"] = [None] * 4
            attention([(wk["qT"], wk["kT"], wk["v"])], lambda qt: T, lambda h, qt: wk["bias"][:, h, qt, :],
                      emit_split(wk["yahi"], wk["yalo"], wk["yat"]), wk["at"])
            wk["nctx"].close()
            toks = [last(pe), last(act), last(dve), last(pool)]
            for e in (act, dve, pool):
                e.wait(toks)

        def ret_begin(i):
            n = ExitStack()
            wk["nctx"] = n
            wk["at"] = []
            wk["tmf"] = None
            wk["qT"] = sb("rqT" + tag(), [P, 4, T], F32, n)
            wk["kT"] = sb("rkT" + tag(), [P, 4, T], F32, n)
            wk["v"] = sb("rv" + tag(), [P, 2, 1024], F32, n)
            wk["g"] = sb("rg" + tag(), [P, 2, 1024], F32, n)
            wk["dt4"] = sb("rd" + tag(), [P, 4, 2, T], F32, n)
            wk["tm"] = sb("rtm" + tag(), [P, 2, 512], F32, n)
            wk["dk"] = sb("rdk" + tag(), [P, 5, 8], F32, n)
            wk["pt"] = sb("rpt" + tag(), [P, 2, 2, T], F32, n)
            wk["rel"] = wk["pt"]
            wk["cs"] = rot
            wk["ptf"] = [None, None]
            wk["rt3"] = []
            wk["bn"] = sb("rbn" + tag(), [P, 8, 6], F32, n)
            wk["mv"] = sb("rmv" + tag(), [P, 8, 2], F32, n)
            wk["sd"] = sb("rsd" + tag(), [P, 2, 8], F32, n)
            load(wk["rel"][:, :, :, :], a["k_rel"])
            load(wk["dk"][:, 0, :], a["decay"][i])
            wk["ldt"] = loads_done()
            dk = wk["dk"]
            act.wait(wk["ldt"])
            t = act.done(nc.scalar.activation(dk[:, 1, :], dk[:, 0, :], ACT.Abs))
            act.wait(t)
            t = act.done(nc.scalar.activation(dk[:, 2, :], dk[:, 1, :], ACT.Exp, scale=-1.0))
            act.wait(t)
            t = act.done(nc.scalar.activation(dk[:, 3, :], dk[:, 2, :], ACT.Ln, bias=1.0))
            dve.wait(t, wk["ldt"])
            t = dve.done(nc.vector.scalar_tensor_tensor(out=dk[:, 4, :], in0=dk[:, 0, :], scalar=0.0,
                                                        in1=dk[:, 3, :], op0=ALU.min, op1=ALU.subtract))
            dve.wait(t)
            d4, rel = wk["dt4"], wk["rel"]
            for h in range(4):
                dst = d4[:, h, :, :].rearrange("p b n -> p (b n)")
                t = dve.done(nc.vector.tensor_scalar(dst, rel[:, 0, :, :].rearrange("p b n -> p (b n)"),
                                                     dk[:, 4, h:h + 1], None, ALU.mult))
                dve.wait(t)
                t = dve.done(nc.vector.scalar_tensor_tensor(
                    out=dst, in0=rel[:, 1, :, :].rearrange("p b n -> p (b n)"), scalar=dk[:, 4, 4 + h:5 + h],
                    in1=dst, op0=ALU.mult, op1=ALU.add))
            act.wait(t)
            wk["d4t"] = act.done(nc.scalar.activation(d4[:, :, :, :], d4[:, :, :, :], ACT.Exp))

        def ret_in(u):
            b0, b1, tok = token_unit(need_x)
            if u < 2:
                tm, cs = wk["tm"], wk["cs"]
                dve.wait(tok, wk["ldt"], wk["tmf"], wk["d4t"])
                rb = wk["pt"]
                for t in range(2):
                    y = ps[:, (b0, b1)[t], :].rearrange("p (h w d) -> p h w d", h=4, w=2)
                    tv = tm[:, t, :].rearrange("p (h w d) -> p h w d", h=4, w=2)
                    rv = rb[:, t, :, :].rearrange("p a (h w d) -> p (a h) w d", w=2, d=64)
                    co = cs[:, 0, t, :].unsqueeze(1)
                    si = cs[:, 1, t, :].unsqueeze(1).to_broadcast([P, 4, 64])
                    t1 = dve.done(nc.vector.tensor_tensor(
                        tm[:, t, :].rearrange("p (a d) -> p a d", d=64),
                        ps[:, (b0, b1)[t], :].rearrange("p (a d) -> p a d", d=64),
                        co.to_broadcast([P, 8, 64]), ALU.mult))
                    t2 = dve.done(nc.vector.tensor_tensor(rv[:, :, 0, :], y[:, :, 1, :], si, ALU.mult))
                    t3 = dve.done(nc.vector.tensor_tensor(rv[:, :, 1, :], y[:, :, 0, :], si, ALU.mult))
                    dve.wait(t3)
                    dve.done(nc.vector.tensor_tensor(tv[:, :, 0, :], tv[:, :, 0, :], rv[:, :, 0, :], ALU.subtract))
                    t4 = dve.done(nc.vector.tensor_tensor(tv[:, :, 1, :], tv[:, :, 1, :], rv[:, :, 1, :], ALU.add))
                free[b0] = free[b1] = t3
                dst = (wk["qT"], wk["kT"])[u]

                def turn():
                    tk = turn_chunks(wk["tm"], 4, t4, (D0, D1))
                    act.wait(tk[-1])
                    te = act.done(nc.scalar.activation(dst[:, :, :], ps[:, D0:D0 + 2, :].rearrange(
                        "p b (c n) -> p (b c) n", c=2), ACT.Copy, scale=1.0 if u == 0 else 128.0 ** -0.5))
                    free[D0] = free[D1] = te
                    wk["tmf"] = tk[-1]
                    wk["at"].append(te)

                deferred.append(turn)
            elif u < 4:
                keep_v(b0, b1, tok, wk["v"][:, :, 512 * (u - 2):512 * (u - 1)])
            else:
                act.wait(tok)
                t = act.done(nc.scalar.activation(wk["g"][:, :, 512 * (u - 4):512 * (u - 3)], ps[:, b0:b0 + 2, :],
                                                  ACT.Silu))
                free[b0] = free[b1] = t
                wk["gt"] = t

        def ret_out(h, nt):
            return ps[:, D2 + h % 2, nt * T:(nt + 1) * T]

        def ret(h):
            qT, kT, d4, pt = wk["qT"], wk["kT"], wk["dt4"], wk["pt"]
            b = D0 + h % 2
            pe.wait(wk["at"], free[b])
            for mb in range(2):
                ins = mm(ps[:, b, mb * T:(mb + 1) * T], kT[:, h, mb * P:(mb + 1) * P], qT[:, h, :], mb == 0, True)
            tok = pe.done(ins)
            dve.wait(tok, wk["d4t"], wk["ptf"][h % 2], wk["at"])
            tp = dve.done(nc.vector.tensor_tensor(pt[:, h % 2, :, :].rearrange("p b n -> p (b n)"), ps[:, b, :],
                                                  d4[:, h, :, :].rearrange("p b n -> p (b n)"), ALU.mult))
            free[b] = tp
            deferred.append(lambda: ret_values(h, tp))

        def ret_values(h, tp):
            v, pt, g = wk["v"], wk["pt"], wk["g"]
            bn, mv, sd, e = wk["bn"], wk["mv"], wk["sd"], wk["tm"]
            bo = D2 + h % 2
            pe.wait(tp, free[bo])
            for nt in range(2):
                for mb in range(2):
                    ins = mm(ret_out(h, nt), pt[:, h % 2, mb, nt * P:(nt + 1) * P], v[:, mb, h * T:(h + 1) * T],
                             mb == 0, mb == 1)
            tok = pe.done(ins)
            wk["ptf"][h % 2] = tok
            dve.wait(tok)
            for nt in range(2):
                t = dve.done(nc.vector.bn_stats(bn[:, 2 * h + nt, :], ret_out(h, nt)))
            dve.wait(t)
            for nt in range(2):
                t = dve.done(nc.vector.bn_aggr(mv[:, 2 * h + nt, :], bn[:, 2 * h + nt, :]))
            act.wait(t, t_ones)
            t = act.done(nc.scalar.activation(sd[:, 0, 2 * h:2 * h + 2], mv[:, 2 * h:2 * h + 2, 1], ACT.Sqrt,
                                              bias=epst[:, 0:1]))
            dve.wait(t)
            t = dve.done(nc.vector.reciprocal(sd[:, 1, 2 * h:2 * h + 2], sd[:, 0, 2 * h:2 * h + 2]))
            dve.wait(t, wk["gt"])
            for nt in range(2):
                j = 2 * h + nt
                tmp = e[:, nt, 0:T]
                t = dve.done(nc.vector.tensor_scalar(tmp, ret_out(h, nt), mv[:, j, 0:1], sd[:, 1, j:j + 1],
                                                     ALU.subtract, ALU.mult))
            free[bo] = t
            dve.wait(t)
            for nt in range(2):
                t = dve.done(nc.vector.tensor_tensor(g[:, nt, h * T:(h + 1) * T], g[:, nt, h * T:(h + 1) * T],
                                                     e[:, nt, 0:T], ALU.mult))
            wk["rt3"].append(t)

        def ret_end():
            act.wait(xread[0])
            dve.wait(xread[0])
            wk["ybt"] = turn_split(wk["g"], 8, wk["rt3"], xhi, xlo, banks=(D0, D1, D2, D3))
            wk["nctx"].close()
            c = wk["ctx"]
            toks = [last(pe), last(act), last(dve), last(pool)]
            for e_ in (act, dve, pool):
                e_.wait(toks)
            wk["mhi"] = sb("mhi" + tag(), [P, NC, T], F32R, c)
            wk["mlo"] = sb("mlo" + tag(), [P, NC, T], F32R, c)
            wk["mt"] = [None] * NC

        def gate(u, b):
            b0, b1, tok = feature_unit(xhi, xlo, need_x)
            act.wait(tok)
            wk["sgt"][b][u] = act.done(nc.scalar.activation(wk["sg"][:, b, u, :], ps[:, b0:b0 + 2, :].rearrange(
                "p b n -> p (b n)"), ACT.Sigmoid))
            free[b0] = free[b1] = wk["sgt"][b][u]

        def branch(u, b):
            if b == 0:
                b0, b1, tok = feature_unit(wk["yahi"], wk["yalo"], lambda kc: wk["yat"][kc], nk=4)
            else:
                b0, b1, tok = feature_unit(xhi, xlo, lambda kc: wk["ybt"][kc])
            pv = ps[:, b0:b0 + 2, :].rearrange("p b n -> p (b n)")
            sg, m = wk["sg"][:, b, u, :], wk["sg"][:, 0, u, :]
            dve.wait(tok, wk["sgt"][b][u])
            t = dve.done(nc.vector.tensor_tensor(sg, sg, pv, ALU.mult))
            free[b0] = free[b1] = wk["sgt"][b][u] = t
            if b == 0:
                return
            h = wk["mhi"][:, 4 * u:4 * u + 4, :].rearrange("p k n -> p (k n)")
            l = wk["mlo"][:, 4 * u:4 * u + 4, :].rearrange("p k n -> p (k n)")
            dve.wait(t, wk["sgt"][0][u])
            for k in range(2):
                c = slice(512 * k, 512 * k + 512)
                t = dve.done(nc.vector.tensor_tensor(m[:, c], m[:, c], sg[:, c], ALU.add))
                act.wait(t)
                th = act.done(nc.scalar.activation(h[:, c], m[:, c], ACT.Copy))
                dve.wait(th)
                tl = dve.done(nc.vector.tensor_tensor(l[:, c], m[:, c], h[:, c].bitcast(F32), ALU.subtract))
                wk["mt"][4 * u + 2 * k] = wk["mt"][4 * u + 2 * k + 1] = [th, tl]

        def update_ln(m):
            dve.wait(wk["dt"][m], xt[m])
            xt[m] = dve.done(nc.vector.scalar_tensor_tensor(
                out=x[:, m, :], in0=x[:, m, :], scalar=ALPHA, in1=dblk(m), op0=ALU.mult, op1=ALU.add))
            free[D0 + m // 2] = xt[m]

        def update_plain(m):
            dve.wait(wk["dt"][m], xt[m])
            xt[m] = dve.done(nc.vector.tensor_tensor(x[:, m, :], x[:, m, :], dblk(m), ALU.add))
            free[D0 + m // 2] = xt[m]

        def second_ffn_begin(i):
            wk["ctx"].close()
            ffn_begin()
            c = wk["ctx"]
            wk["cw"] = cw[:, i, :, :]
            wk["pT"] = sb("pT" + tag(), [P, 2, T], F32, c)
            wk["phi"] = sb("phi" + tag(), [P, 2, T], F32R, c)
            wk["plo"] = sb("plo" + tag(), [P, 2, T], F32R, c)
            wk["pg"] = sb("pg" + tag(), [P, 1024], F32, c)
            load(wk["pT"][:, :, :], a["p_2"][i])
            wk["ldt"] = loads_done()
            act.wait(wk["ldt"])
            th = act.done(nc.scalar.activation(wk["phi"][:, :, :], wk["pT"][:, :, :], ACT.Copy))
            dve.wait(th, wk["ldt"])
            tl = dve.done(nc.vector.tensor_tensor(wk["plo"][:, :, :], wk["pT"][:, :, :],
                                                  wk["phi"][:, :, :].bitcast(F32), ALU.subtract))
            wk["pt_"] = [th, tl]
            wk["pgf"] = None

        def plegate(u):
            b0, b1, tok = feature_unit(xhi, xlo, need_x)
            act.wait(tok, wk["pgf"])
            wk["pgt"] = act.done(nc.scalar.activation(wk["pg"][:, :], ps[:, b0:b0 + 2, :].rearrange(
                "p b n -> p (b n)"), ACT.Sigmoid))
            free[b0] = free[b1] = wk["pgt"]

        def pleproj(u):
            b0, b1, tok = feature_unit(wk["phi"], wk["plo"], lambda kc: wk["pt_"], nk=2)
            dve.wait(tok, wk["pgt"])
            t = dve.done(nc.vector.tensor_tensor(wk["pg"][:, :], wk["pg"][:, :], ps[:, b0:b0 + 2, :].rearrange(
                "p b n -> p (b n)"), ALU.mult))
            free[b0] = free[b1] = t
            dve.wait(t, *[xn_tok[m] for m in range(4 * u, 4 * u + 4)])
            xv = x[:, 4 * u:4 * u + 4, :].rearrange("p k n -> p (k n)")
            t = dve.done(nc.vector.scalar_tensor_tensor(out=xv, in0=xv, scalar=ALPHA, in1=wk["pg"][:, :],
                                                        op0=ALU.mult, op1=ALU.add))
            wk["pgf"] = t
            for m in range(4 * u, 4 * u + 4):
                xt[m] = t

        def convup(q):
            b0, b1, tok = feature_unit(xhi, xlo, need_x)
            s = q % 2
            cw = wk["cw"]
            e = (wk["e1"], wk["e2"])
            res = []
            for side, b in ((0, b0), (1, b1)):
                act.wait(tok, wk["ef"][s], wk["ldt"])
                for k in range(2):
                    blk = 22 * side + 2 * q + k
                    ta = act.done(nc.scalar.activation(
                        e[side][:, s, k * T:(k + 1) * T], ps[:, b, k * T:(k + 1) * T], ACT.Identity,
                        scale=cw[:, 1, blk:blk + 1], bias=cw[:, 3, blk:blk + 1]))
                for k in range(2):
                    blk = 22 * side + 2 * q + k
                    y = ps[:, b, k * T:(k + 1) * T]
                    o = e[side][:, s, k * T:(k + 1) * T]
                    dve.wait(ta, tok)
                    t = dve.done(nc.vector.scalar_tensor_tensor(
                        out=o[:, 1:T], in0=y[:, 0:T - 1], scalar=cw[:, 0, blk:blk + 1], in1=o[:, 1:T],
                        op0=ALU.mult, op1=ALU.add))
                    dve.wait(t)
                    t = dve.done(nc.vector.scalar_tensor_tensor(
                        out=o[:, 0:T - 1], in0=y[:, 1:T], scalar=cw[:, 2, blk:blk + 1], in1=o[:, 0:T - 1],
                        op0=ALU.mult, op1=ALU.add))
                free[b] = t
                res.append(t)
            act.wait(res[0])
            ta = act.done(nc.scalar.activation(e[0][:, s, :], e[0][:, s, :], ACT.Gelu_apprx_tanh))
            dve.wait(ta, res[1])
            td = dve.done(nc.vector.tensor_tensor(e[1][:, s, :], e[0][:, s, :], e[1][:, s, :], ALU.mult))
            hidden_split(q, e[1][:, s, :], td, s)

        make_rope()
        tail = None
        for s in steps:
            k = s["kind"]
            i, u = s.get("i"), s.get("u")
            if k == "mod":
                mod_unit(i, u, s.get("bank", D3) - u % 2)
            elif k == "norm":
                run_deferred()
                if tail is None:
                    tail = Tail(lambda m: None, "square")
                    for m in range(0, NC, 2):
                        tail.step((m, m + 1))
                    tail.flush(0)
                if "ctx" in wk:
                    wk["ctx"].close()
                if s["s"] != 1:
                    ffn_begin()
                else:
                    wk["ctx"] = enter()
                    (dil_begin if i else fox_begin)()
                    if i:
                        wk["nbuf"] = wk["v0"][:, :, :].rearrange("p t n -> p (t n)").rearrange("p (k n) -> p k n", k=4)
                md = s["m"]
                norm(i, s["s"], wk["nbuf"], tail.tok, (lambda: mod_unit(*md, D3 - md[1] % 2)) if md else None)
                if s["s"] == 1:
                    (dil_gain if i else fox_gain)()
            elif k == "gateup":
                gateup(s["q"])
            elif k == "down":
                if s["q"] == FB // 2 - 1:
                    tail = Tail(residual(i, 2 * s["j"]), "split" if (i, s["j"]) == (1, 1) else "square")
                down(s["q"], tail)
            elif k == "fox_f":
                fox_f()
            elif k == "fox_in":
                fox_in(s["hh"], s["r"])
            elif k == "fox_attn":
                fox_attn(s["hh"])
            elif k == "dil_in":
                dil_in(s["hh"], s["g"], s["r"])
            elif k == "dil_attn":
                dil_attn(s["hh"])
            elif k == "mix_out":
                if u == 1:
                    tail = Tail(residual(i, 1), "square")
                out_unit(u, xhi, xlo, need_x, tail)
            elif k == "sec_begin":
                wk["ctx"].close()
                na_begin(i)
            elif k == "na_in":
                na_in(u)
            elif k == "na_attn":
                na_attn()
                ret_begin(i)
            elif k == "ret_in":
                ret_in(u)
            elif k == "ret":
                ret(s["h"])
            elif k == "ret_end":
                ret_end()
            elif k == "gate":
                gate(u, s["b"])
            elif k == "branch":
                branch(u, s["b"])
            elif k == "wout":
                if u == 1:
                    tail = Tail(update_ln, "mean")
                out_unit(u, wk["mhi"], wk["mlo"], lambda kc: wk["mt"][kc], tail)
            elif k == "ln":
                layer_norm(i, s["j"], s["j"] == 0 or i == 0, tail.tok)
                if s["j"] == 0:
                    second_ffn_begin(i)
            elif k == "plegate":
                plegate(u)
            elif k == "pleproj":
                pleproj(u)
            elif k == "convup":
                convup(s["q"])
            elif k == "down2":
                if s["q"] == FB // 2 - 1:
                    tail = Tail(update_plain, "mean")
                down(s["q"], tail)
        wk["ctx"].close()
        for m in range(NC):
            sp.wait(xt[m])
            t = sy.done(nc.sync.dma_start(out[:, m, :], x[:, m, :]), "s_st", 16)
        sp.wait(t)


def constants():
    import numpy as np
    k = {}
    k["k_ident"] = np.eye(P, dtype=np.float32)
    s = np.arange(T)
    q = np.arange(P)
    k["k_causal"] = np.where(s[None, :] <= q[:, None] + P, 0.0, BIG).astype(np.float32)
    parts = []
    for qt in range(2):
        for window, dil in ((128, 1), (512, 4), (2048, 16)):
            d = (q[:, None] + P * qt) - np.arange(P * (qt + 1))[None, :]
            parts.append(np.where((d >= 0) & (d <= window) & (d % dil == 0), 0.0, BIG).astype(np.float32))
    k["k_mask"] = np.ascontiguousarray(np.concatenate(parts, axis=1))
    inv = (np.float32(500000.0) ** (-(np.arange(8, dtype=np.float32) * 2.0 / 16))).astype(np.float32)
    sign = np.concatenate([-np.ones(8), np.ones(8)]).astype(np.float32)
    k["k_inv"] = np.ascontiguousarray(np.broadcast_to(np.stack([np.concatenate([inv, inv]), sign]), (P, 2, 16)))
    inv = (np.float32(10000.0) ** (-np.arange(64, dtype=np.float32) / 64)).astype(np.float32)
    ang = (s.astype(np.float32)[:, None] * inv[None, :]).astype(np.float64)
    rot = np.stack([np.cos(ang), np.sin(ang)]).astype(np.float32).reshape(2, 2, P, 64)
    k["k_rot"] = np.ascontiguousarray(rot.transpose(2, 0, 1, 3))
    m = (np.arange(2)[None, :, None] * P + q[:, None, None])
    n = s[None, None, :]
    k["k_rel"] = np.ascontiguousarray(np.stack([np.maximum(n - m, 0), np.maximum(m - n, 0)], axis=1).astype(np.float32))
    return k


def layout(inp):
    import numpy as np
    g = {n: np.asarray(v) for n, v in inp.items()}

    def col(v, n):
        return np.ascontiguousarray(v.reshape(v.shape[:-1] + (n, P)))

    r = {}
    for n in ("mod_w", "ffn_w_gate", "ffn_w_up", "ffn_w_down", "fox_w_in", "fox_w_out", "dil_w_in", "dil_w_out",
              "w_in_2", "w_branch_a_2", "w_branch_b_2", "w_out_2", "w_up_2", "w_down_2", "w_ple_gate_2",
              "w_ple_proj_2"):
        r[n] = np.ascontiguousarray(g[n])
    r["x"] = np.ascontiguousarray(g["x"][0].T.reshape(NC, P, T).transpose(1, 0, 2))
    r["c"] = np.ascontiguousarray(g["c"].reshape(NC, P).T)
    r["mod_b"] = np.ascontiguousarray(g["mod_b"].reshape(2, 72, P).transpose(2, 0, 1))
    r["norm_g"] = np.ascontiguousarray(g["norm_g"].reshape(6, NC, P).transpose(2, 0, 1))
    r["ln"] = np.ascontiguousarray(np.stack([g["ln1_g_2"], g["ln1_b_2"], g["ln2_g_2"], g["ln2_b_2"]], axis=1)
                                   .reshape(2, 4, NC, P).transpose(3, 0, 1, 2))
    r["fox_q_g"] = np.ascontiguousarray(np.broadcast_to(g["fox_q_g"], (P, 64)))
    r["fox_k_g"] = np.ascontiguousarray(np.broadcast_to(g["fox_k_g"], (P, 64)))
    r["fox_b_f"] = np.ascontiguousarray(g["fox_b_f"].reshape(16, 1))
    r["dil_q_g"] = np.ascontiguousarray(np.broadcast_to(g["dil_q_g"][0], (P, 3, 64)))
    r["dil_k_g"] = np.ascontiguousarray(np.broadcast_to(g["dil_k_g"][0], (P, 3, 64)))
    r["positions"] = np.ascontiguousarray(g["positions"].reshape(2, P).T)
    q = np.arange(T)
    rr, cc = q // 64, q % 64
    start = np.clip(cc - 8, 0, 48)
    dr = rr[None, :] - rr[:, None] + 7
    inside = (cc[None, :] >= start[:, None]) & (cc[None, :] < start[:, None] + 16)
    dc = np.where(inside, cc[None, :] - cc[:, None] + 15, 31)
    padded = np.pad(g["na_rpb_2"], ((0, 0), (0, 0), (0, 0), (0, 1)), constant_values=-BIG)
    b = padded[:, :, dr, dc]
    r["na_rpb_2"] = np.ascontiguousarray(b.reshape(2, 8, 2, P, T).transpose(0, 3, 1, 2, 4))
    dec = np.concatenate([g["ret_decay_f_2"], g["ret_decay_b_2"]], axis=1)
    r["decay"] = np.ascontiguousarray(np.broadcast_to(dec[:, None, :], (2, P, 8)))
    cw = np.concatenate([g["conv_w_2"], g["conv_b_2"][:, None, :]], axis=1)
    r["conv"] = np.ascontiguousarray(cw.reshape(2, 4, 44, P).transpose(3, 0, 1, 2))
    r["p_2"] = np.ascontiguousarray(g["p_2"][:, 0].transpose(0, 2, 1).reshape(2, 2, P, T).transpose(0, 2, 1, 3))
    r.update(constants())
    return r


def kernel(**inputs):
    import concourse.bacc as bacc
    import numpy as np
    from concourse.bass_utils import run_bass_kernel_spmd

    nc = bacc.Bacc("TRN2", target_bir_lowering=False, num_devices=1)
    arrays = {f"in_{n}": v for n, v in layout(inputs).items()}
    args = {n[3:]: nc.dram_tensor(n, v.shape, mybir.dt.from_np(v.dtype), kind="ExternalInput").ap()
            for n, v in arrays.items()}
    out = nc.dram_tensor("out_x", (P, NC, T), F32, kind="ExternalOutput").ap()
    build(nc, args, out)
    r = run_bass_kernel_spmd(nc, [arrays], core_ids=[0])
    y = r.results[0]["out_x"]
    return np.ascontiguousarray(np.asarray(y).transpose(1, 0, 2).reshape(1, D, T).transpose(0, 2, 1))
```

```python
import math
from contextlib import ExitStack

import concourse.bass as bass
from concourse import mybir

F32 = mybir.dt.float32
F32R = mybir.dt.float32r
I32 = mybir.dt.int32
ALU = mybir.AluOpType
ACT = mybir.ActivationFunctionType
AX = mybir.AxisListType

P = 128
T = 256
D = 1024
NC = D // P
F = 2816
FB = F // P
RAW = 6
CONV = 3
PIECE = 2048
BIG = 1e30
ALPHA = 4.0 ** 0.25


class Sync:

    def __init__(self, nc, ctx):
        self.nc = nc
        self.ctx = ctx
        self.sem = {}
        self.count = {}
        self.seen = {}

    def add(self, name):
        self.sem[name] = self.ctx.enter_context(self.nc.semaphore(name))
        self.count[name] = 0

    def done(self, ins, name, n=1):
        self.count[name] += n
        ins.then_inc(self.sem[name], n)
        return (name, self.count[name])

    def wait(self, eng, ename, *tokens):
        for tok in tokens:
            if tok is None:
                continue
            if isinstance(tok, list):
                self.wait(eng, ename, *tok)
                continue
            name, value = tok
            if self.seen.get((ename, name), 0) < value:
                eng.wait_ge(self.sem[name], value)
                self.seen[(ename, name)] = value


def build(nc, a, out):
    root = ExitStack()
    with root:
        sy = Sync(nc, root)
        for n in ("pe", "act", "dve", "pool", "ld", "st", "c", "a", "i", "x"):
            sy.add("s_" + n)
        for i in range(RAW):
            sy.add(f"s_raw{i}")

        class Eng:
            def __init__(self, eng, name):
                self.eng, self.name = eng, name

            def wait(self, *toks):
                sy.wait(self.eng, self.name, *toks)

            def done(self, ins):
                return sy.done(ins, "s_" + self.name)

        pe, act, dve, pool, sp = (Eng(nc.tensor, "pe"), Eng(nc.scalar, "act"), Eng(nc.vector, "dve"),
                                  Eng(nc.gpsimd, "pool"), Eng(nc.sync, "sp"))

        def last(e):
            return ("s_" + e.name, sy.count["s_" + e.name])

        def sb(name, shape, dt, ctx=root):
            return ctx.enter_context(nc.sbuf_tensor(name, shape, dt))

        raw = sb("raw", [P, RAW, PIECE], F32)
        whi = sb("whi", [P, CONV, PIECE], F32R)
        wlo = sb("wlo", [P, CONV, PIECE], F32R)
        x = sb("x", [P, NC, T], F32)
        xhi = sb("xhi", [P, NC, T], F32R)
        xlo = sb("xlo", [P, NC, T], F32R)
        ident = sb("ident", [P, P], F32)
        mean = sb("mean", [P, P], F32)
        ccol = sb("ccol", [P, NC], F32)
        csil = sb("csil", [P, NC, 32], F32)
        mrow = sb("mrow", [P, 512], F32)
        rope = sb("rope", [P, 2, 2, 16], F32)
        inv = sb("inv", [P, 2, 16], F32)
        pos = sb("pos", [P, 2], I32)
        cw = sb("cw", [P, 2, 4, 44], F32)
        rot = sb("rot", [P, 2, 2, 64], F32)
        mod = sb("modc", [P, 72], F32)
        modb = sb("modb", [P, 2, 72], F32)
        ng = sb("ng", [P, 6, NC], F32)
        ascale = sb("ascale", [P, 3, NC], F32)
        gs = sb("gs", [P, 3, NC], F32)
        epst = sb("epst", [P, 3], F32)
        sqb = sb("sqb", [P, 4, T], F32)
        st = sb("st", [P, 8], F32)
        pT = sb("pT", [P, 2, T], F32)
        ln = sb("ln", [P, 2, 4, NC], F32)
        ps = root.enter_context(nc.psum_tensor("ps", [P, 8, 512], F32))
        G0, G1, G2, G3, D0, D1, D2, D3 = range(8)
        free = [None] * 8

        def bank_wait(e, *banks):
            for b in banks:
                e.wait(free[b])

        def load(dst, src, *toks):
            pool.wait(*toks)
            return sy.done(nc.gpsimd.dma_start(dst, src), "s_ld", 16)

        def loads_done():
            return ("s_ld", sy.count["s_ld"])

        t_ccol = sy.done(nc.sync.dma_start(ccol[:, :], a["c"]), "s_c", 16)
        for dst, src in ((modb[:, :, :], a["mod_b"]), (ng[:, :, :], a["norm_g"])):
            t_mb = sy.done(nc.sync.dma_start(dst, src), "s_a", 16)
        t_zero = dve.done(nc.vector.memset(csil[:, :, :], 0.0))
        act.wait(t_ccol, t_zero)
        t_c = act.done(nc.scalar.activation(csil[:, :, 0], ccol[:, :], ACT.Silu))
        t_id = sy.done(nc.scalar.dma_start(ident[:, :], a["k_ident"]), "s_i", 16)
        t_x = sy.done(nc.scalar.dma_start(x[:, :, :], a["x"]), "s_x", 16)
        for dst, src in ((inv[:, :, :], a["k_inv"]), (pos[:, :], a["positions"]), (cw[:, :, :, :], a["conv"]),
                         (rot[:, :, :, :], a["k_rot"]), (ln[:, :, :, :], a["ln"])):
            t_small = load(dst, src)
        dve.done(nc.vector.memset(mean[:, :], 1.0 / D))
        dve.done(nc.vector.memset(epst[:, 0:1], 1e-6))
        t_ones = dve.done(nc.vector.memset(epst[:, 1:2], 1e-5))

        pieces = []

        def plan(kind, srcs):
            pieces.append(dict(kind=kind, srcs=srcs))

        def kview(w, k0, k1, c0, c1):
            return w[k0 * P:k1 * P, c0:c1].rearrange("(k p) n -> p k n", p=P)

        def plan_unit(w, c0, c1=None, kind="w", nk=NC):
            for k0 in range(0, nk, 4):
                plan(kind, [((4, 512), 0, 512, kview(w, k0, k0 + 4, c0, c0 + 512))])

        def plan_pair(w0, a0, w1, a1):
            for k0 in (0, 4):
                plan("w", [((4, 512), 0, 256, kview(w0, k0, k0 + 4, a0, a0 + 256)),
                           ((4, 512), 256, 512, kview(w1, k0, k0 + 4, a1, a1 + 256))])

        def plan_down(w):
            for i in range(FB // 2):
                plan("w", [((2, 1024), 0, 1024, kview(w, 2 * i, 2 * i + 2, 0, 1024))])

        def plan_mod(i, u):
            plan_unit(a["mod_w"][i], 512 * u, kind="m")

        f1 = {("ffn", 0, 0): [(0, u) for u in range(4, 11)], ("mix", 0): [(0, u) for u in range(11, 16)],
              ("ffn", 0, 1): [(0, 16), (0, 17)] + [(1, u) for u in range(4)],
              ("ffn", 1, 0): [(1, u) for u in range(4, 10)], ("mix", 1): [(1, u) for u in range(10, 16)],
              ("ffn", 1, 1): [(1, 16), (1, 17)]}

        def spread(units, n):
            at = [[] for _ in range(n)]
            for j, u in enumerate(units):
                at[min(n - 1, (j * n) // len(units))].append(u)
            return at

        steps = []

        def step(kind, **kw):
            steps.append(dict(kind=kind, **kw))

        def plan_first():
            for u in range(4):
                step("mod", i=0, u=u)
            for i in range(2):
                plan_ffn(i, 0)
                plan_mix(i)
                plan_ffn(i, 1)

        def plan_ffn(i, j):
            fl = list(f1.get(("ffn", i, j), []))
            step("norm", i=i, s=2 * j, m=fl.pop(0) if fl and (i, j) != (0, 0) else None)
            at = spread(fl, 16)
            for q in range(11):
                step("gateup", i=i, j=j, q=q)
                for m in at[q]:
                    step("mod", i=m[0], u=m[1])
            for q in range(11):
                step("down", i=i, j=j, q=q)
                if q < 5:
                    for m in at[11 + q]:
                        step("mod", i=m[0], u=m[1], bank=G3)

        def plan_mix(i):
            fl = list(f1[("mix", i)])
            step("norm", i=i, s=1, m=fl.pop(0))
            if i == 0:
                for hh in range(2):
                    for r in range(3):
                        step("fox_in", hh=hh, r=r)
                        if hh == 0 and r == 0:
                            step("fox_f")
                        for m in fl[:2 if r == 1 else 1] if hh == 0 else ():
                            fl.remove(m)
                            step("mod", i=m[0], u=m[1])
                    step("fox_attn", hh=hh)
            else:
                for hh in range(2):
                    for g in range(3):
                        for r in range(3):
                            step("dil_in", hh=hh, g=g, r=r)
                        if fl:
                            m = fl.pop(0)
                            step("mod", i=m[0], u=m[1])
                    step("dil_attn", hh=hh)
            for u in range(2):
                step("mix_out", i=i, u=u)

        def plan_second():
            for i in range(2):
                step("sec_begin", i=i)
                for u in range(3):
                    step("na_in", i=i, u=u)
                step("na_attn", i=i)
                for u in (2, 3, 4, 5):
                    step("ret_in", i=i, u=u)
                step("gate", i=i, u=0, b=0)
                for u in (0, 1):
                    step("ret_in", i=i, u=u)
                for h, (u, b) in enumerate(((1, 0), (0, 1), (1, 1))):
                    step("gate", i=i, u=u, b=b)
                    step("ret", i=i, h=h)
                step("ret", i=i, h=3)
                step("branch", i=i, u=0, b=0)
                step("branch", i=i, u=1, b=0)
                step("ret_end", i=i)
                for u in range(2):
                    step("branch", i=i, u=u, b=1)
                for u in range(2):
                    step("wout", i=i, u=u)
                step("ln", i=i, j=0)
                for u in range(2):
                    step("plegate", i=i, u=u)
                    step("pleproj", i=i, u=u)
                for q in range(11):
                    step("convup", i=i, q=q)
                for q in range(11):
                    step("down2", i=i, q=q)
                step("ln", i=i, j=1)

        plan_first()
        plan_second()

        def stream(s):
            k = s["kind"]
            if k == "norm" and s["m"]:
                plan_mod(*s["m"])
            elif k == "mod":
                plan_mod(s["i"], s["u"])
            elif k == "gateup":
                q = 256 * s["q"]
                plan_pair(a["ffn_w_gate"][s["i"], s["j"]], q, a["ffn_w_up"][s["i"], s["j"]], q)
            elif k == "down":
                w, q = a["ffn_w_down"][s["i"], s["j"]], s["q"]
                plan("w", [((2, 1024), 0, 1024, kview(w, 2 * q, 2 * q + 2, 0, 1024))])
            elif k == "down2":
                w, q = a["w_down_2"][s["i"]], s["q"]
                plan("w", [((2, 1024), 0, 1024, kview(w, 2 * q, 2 * q + 2, 0, 1024))])
            elif k == "fox_f":
                plan("w", [((8, 16), 0, 16, kview(a["fox_w_in"][0], 0, 8, 3072, 3088))])
            elif k == "fox_in":
                plan_unit(a["fox_w_in"][0], 1024 * s["r"] + 512 * s["hh"])
            elif k == "dil_in":
                plan_unit(a["dil_w_in"][0], 3072 * s["g"] + 1024 * s["r"] + 512 * s["hh"])
            elif k == "mix_out":
                plan_unit((a["fox_w_out"] if s["i"] == 0 else a["dil_w_out"])[0], 512 * s["u"])
            elif k == "na_in":
                plan_unit(a["w_in_2"][s["i"]], 512 * s["u"])
            elif k == "ret_in":
                plan_unit(a["w_in_2"][s["i"]], 512 * (3 + s["u"]))
            elif k == "gate":
                plan_unit(a["w_in_2"][s["i"]], 512 * (9 + 2 * s["b"] + s["u"]))
            elif k == "branch":
                if s["b"] == 0:
                    plan_unit(a["w_branch_a_2"][s["i"]], 512 * s["u"], nk=4)
                else:
                    plan_unit(a["w_branch_b_2"][s["i"]], 512 * s["u"])
            elif k == "wout":
                plan_unit(a["w_out_2"][s["i"]], 512 * s["u"])
            elif k == "plegate":
                plan_unit(a["w_ple_gate_2"][s["i"]], 512 * s["u"])
            elif k == "pleproj":
                plan("w", [((2, 512), 0, 512, kview(a["w_ple_proj_2"][s["i"]], 0, 2, 512 * s["u"], 512 * s["u"] + 512))])
            elif k == "convup":
                q = 256 * s["q"]
                plan_pair(a["w_up_2"][s["i"]], q, a["w_up_2"][s["i"]], F + q)

        for s in steps:
            stream(s)

        state = dict(dma=0, conv=0, use=0, cslot=0)
        raw_free = [None] * RAW
        conv_free = [None] * CONV

        def emit_dma(p):
            slot = p % RAW
            sp.wait(raw_free[slot])
            n = 0
            for shape, c0, c1, src in pieces[p]["srcs"]:
                size = shape[0] * shape[1]
                v = raw[:, slot, 0:size].rearrange("p (k n) -> p k n", k=shape[0])[:, :, c0:c1]
                tok = sy.done(nc.sync.dma_start(v, src), f"s_raw{slot}", 16)
                n = size
            pieces[p]["landed"] = tok
            pieces[p]["n"] = n
            pieces[p]["slot"] = slot

        def emit_conv(p):
            pc = pieces[p]
            if pc["kind"] == "m":
                return
            slot, n = pc["slot"], pc["n"]
            c = state["cslot"] % CONV
            state["cslot"] += 1
            pc["c"] = c
            act.wait(pc["landed"], conv_free[c])
            t_hi = act.done(nc.scalar.activation(whi[:, c, 0:n], raw[:, slot, 0:n], ACT.Copy))
            dve.wait(t_hi, pc["landed"], conv_free[c])
            t_lo = dve.done(nc.vector.tensor_tensor(wlo[:, c, 0:n], raw[:, slot, 0:n],
                                                    whi[:, c, 0:n].bitcast(F32), ALU.subtract))
            raw_free[slot] = [t_hi, t_lo]
            pc["conv"] = [t_hi, t_lo]

        def ensure(ahead=CONV):
            use = state["use"]
            while state["conv"] < len(pieces):
                p = state["conv"]
                if p >= use + RAW or (pieces[p]["kind"] != "m" and
                                      sum(pieces[j]["kind"] != "m" for j in range(use, p)) >= ahead):
                    break
                if state["dma"] <= p:
                    emit_dma(state["dma"])
                    state["dma"] += 1
                    continue
                emit_conv(p)
                state["conv"] += 1
            while state["dma"] < len(pieces) and state["dma"] < use + RAW:
                emit_dma(state["dma"])
                state["dma"] += 1

        def next_piece(k, n, ahead=CONV):
            ensure(ahead)
            p = state["use"]
            pc = pieces[p]
            pe.wait(pc["conv"])
            c = pc["c"]
            vh = whi[:, c, 0:k * n].rearrange("p (k n) -> p k n", k=k)
            vl = wlo[:, c, 0:k * n].rearrange("p (k n) -> p k n", k=k)
            return vh, vl, pc

        def piece_used(pc, tok):
            if pc["kind"] == "m":
                raw_free[pc["slot"]] = tok
            else:
                conv_free[pc["c"]] = tok
            state["use"] += 1

        def raw_piece(k, n, ahead):
            ensure(ahead)
            pc = pieces[state["use"]]
            pe.wait(pc["landed"])
            return raw[:, pc["slot"], 0:k * n].rearrange("p (k n) -> p k n", k=k), pc

        deferred = []
        deferred_mod = []
        beside = []

        def run_deferred(mod_only=False):
            while deferred and not mod_only:
                deferred.pop(0)()
            while deferred_mod:
                deferred_mod.pop(0)()

        def mm(out_, l, r, start, stop):
            return nc.tensor.matmul(out_, l, r, start=start, stop=stop, skip_group_check=True)

        pair = [0]

        def next_pair():
            pair[0] ^= 1
            return (G2, G3) if pair[0] else (G0, G1)

        def triple(o, w, v, h, l, first, final):
            mm(o, w, h, first, False)
            mm(o, v, h, False, False)
            return mm(o, w, l, False, final)

        def feature_unit(ah, al, need, nk=NC, banks=None, tail=None):
            b0, b1 = banks or next_pair()
            pe.wait(free[b0], free[b1])
            for k0 in range(0, nk, 4):
                n = min(4, nk - k0)
                end = tail and k0 + 4 >= nk
                vh, vl, pc = next_piece(n, 512, 2 if end else CONV)

                def block(m, kk):
                    o = ps[:, b0 if m < 2 else b1, (m % 2) * T:(m % 2 + 1) * T]
                    return triple(o, vh[:, kk, m * P:(m + 1) * P], vl[:, kk, m * P:(m + 1) * P], ah[:, k0 + kk, :],
                                  al[:, k0 + kk, :], k0 + kk == 0 and m % 2 == 0, k0 + kk == nk - 1)

                if end:
                    for kk in range(n):
                        pe.wait(need(k0 + kk))
                    for b in range(2):
                        for kk in range(n):
                            for m in (2 * b, 2 * b + 1):
                                ins = block(m, kk)
                        tok = pe.done(ins)
                        if b == 1:
                            piece_used(pc, tok)
                            xread[0] = tok
                        tail(b, tok)
                    return b0, b1, tok
                for kk in range(n):
                    kc = k0 + kk
                    nd = need(kc)
                    pe.wait(nd[0])
                    for m in range(4):
                        o = ps[:, b0 if m < 2 else b1, (m % 2) * T:(m % 2 + 1) * T]
                        w, v = vh[:, kk, m * P:(m + 1) * P], vl[:, kk, m * P:(m + 1) * P]
                        mm(o, w, ah[:, kc, :], kc == 0 and m % 2 == 0, False)
                        mm(o, v, ah[:, kc, :], False, False)
                    pe.wait(nd[1])
                    for m in range(4):
                        o = ps[:, b0 if m < 2 else b1, (m % 2) * T:(m % 2 + 1) * T]
                        ins = mm(o, vh[:, kk, m * P:(m + 1) * P], al[:, kc, :], False, kc == nk - 1)
                tok = pe.done(ins)
                piece_used(pc, tok)
                if beside:
                    beside.pop(0)()
            xread[0] = tok
            run_deferred()
            return b0, b1, tok

        def token_unit(need):
            b0, b1 = next_pair()
            pe.wait(free[b0], free[b1])
            for k0 in range(0, NC, 4):
                vh, vl, pc = next_piece(4, 512)
                for kk in range(4):
                    kc = k0 + kk
                    nd = need(kc)
                    pe.wait(nd[0])
                    for t in range(2):
                        o, h = ps[:, (b0, b1)[t], :], xhi[:, kc, t * P:(t + 1) * P]
                        mm(o, h, vh[:, kk, :], kc == 0, False)
                        mm(o, h, vl[:, kk, :], False, False)
                    pe.wait(nd[1])
                    for t in range(2):
                        ins = mm(ps[:, (b0, b1)[t], :], xlo[:, kc, t * P:(t + 1) * P], vh[:, kk, :], False,
                                 kc == NC - 1)
                tok = pe.done(ins)
                piece_used(pc, tok)
                if beside:
                    beside.pop(0)()
            xread[0] = tok
            run_deferred()
            return b0, b1, tok

        mod_tok = {}
        mrow_free = [None]

        def mod_unit(i, u, bank, ahead=CONV):
            pe.wait(t_c, free[bank])
            for h in range(2):
                v, pc = raw_piece(4, 512, ahead)
                for kk in range(4):
                    ins = mm(ps[32 * kk:32 * kk + 32, bank, :], csil[:, 4 * h + kk, :], v[:, kk, :], h == 0, h == 1)
                tok = pe.done(ins)
                piece_used(pc, tok)
            run_deferred(True)
            act.wait(tok, mrow_free[0])
            t = act.done(nc.scalar.activation(mrow[:, :], ps[:, bank, :], ACT.Copy))
            free[bank] = t
            deferred_mod.append(lambda: mod_turn(i, u, bank, t))

        def mod_turn(i, u, bank, t):
            pe.wait(t, free[bank], t_id)
            for m in range(4):
                ins = nc.tensor.transpose(ps[:, bank, m * P:(m + 1) * P], mrow[:, m * P:(m + 1) * P], ident[:, :])
            tok = pe.done(ins)
            mrow_free[0] = tok
            c0 = mod[:, 4 * u:4 * u + 4]
            dve.wait(tok, mod_tok.get(("used", u // 2)), t_mb)
            t = dve.done(nc.vector.tensor_reduce(
                c0, ps[:, bank, :].rearrange("p (m g n) -> p m g n", m=4, g=4)[:, :, :, 0], AX.X, ALU.add))
            free[bank] = t
            dve.wait(t)
            t = dve.done(nc.vector.tensor_tensor(c0, c0, modb[:, i, 4 * u:4 * u + 4], ALU.add))
            s, kind = u // 6, (u % 6) // 2
            if u % 2:
                dve.wait(t)
                c0 = (3 * s + kind) * NC
                if kind == 1:
                    t = dve.done(nc.vector.scalar_tensor_tensor(
                        out=ascale[:, s, :], in0=mod[:, c0:c0 + NC], scalar=1.0, in1=ng[:, 3 * i + s, :],
                        op0=ALU.add, op1=ALU.mult))
                elif kind == 2:
                    t = dve.done(nc.vector.tensor_scalar(gs[:, s, :], mod[:, c0:c0 + NC], 1.0 if s == 1 else 0.5,
                                                         None, ALU.mult))
                mod_tok[(i, s, kind)] = t

        xt = [t_x] * NC
        xn_tok = [None] * NC

        def spread_columns(tok, bank):
            pe.wait(tok, free[bank], t_id)
            for t in range(2):
                ins = mm(ps[:, bank, t * P:(t + 1) * P], st[:, 2 + t:3 + t].to_broadcast([P, P]),
                         ident[:, :], t == 0, True)
            return pe.done(ins)

        def preload(func):
            act.wait(t_ones)
            act.done(nc.scalar.activation(st[:, 6:7], epst[:, 0:1], func))

        def square(m, tok):
            s = m % 4
            act.wait(tok, sq_free[s])
            return act.done(nc.scalar.activation(sqb[:, s, :], x[:, m, :], ACT.Square))

        def stat(m, tok, squares):
            pe.wait(tok, t_ones)
            if m == 0:
                pe.wait(free[G0])
            t = pe.done(mm(ps[:, G0, 0:T], mean[:, :], sqb[:, m % 4, :] if squares else x[:, m, :], m == 0,
                           m == NC - 1))
            if squares:
                sq_free[m % 4] = t
            return t

        def rstd_row(tok, eps, src=G0, dst=G1, between=None):
            dve.wait(tok, t_id)
            junk = sqb[:, 0, :].rearrange("p (t n) -> p t n", t=2)
            td = dve.done(nc.vector.tensor_tensor(
                junk, ps[:, src, 0:T].rearrange("p (t n) -> p t n", t=2),
                ident[:, :].unsqueeze(1).to_broadcast([P, 2, P]), ALU.mult))
            free[src] = td
            dve.wait(td)
            td = dve.done(nc.vector.tensor_reduce(st[:, 4:6], junk, AX.X, ALU.add))
            sq_free[0] = td
            act.wait(td, t_ones)
            ta = act.done(nc.scalar.activation(st[:, 0:2], st[:, 4:6], ACT.Sqrt, bias=epst[:, eps:eps + 1]))
            dve.wait(ta)
            tr = dve.done(nc.vector.reciprocal(st[:, 2:4], st[:, 0:2]))
            if between:
                between()
            return spread_columns(tr, dst)

        sq_free = [None] * 4
        nb_free = [None] * 4
        xread = [None]

        def split_chunk(m, src, tok):
            act.wait(tok, xread[0])
            th = act.done(nc.scalar.activation(xhi[:, m, :], src, ACT.Copy))
            dve.wait(th)
            tl = dve.done(nc.vector.tensor_tensor(xlo[:, m, :], src, xhi[:, m, :].bitcast(F32), ALU.subtract))
            xn_tok[m] = [th, tl]
            return tl

        class Tail:

            def __init__(self, update, mode, lag=2):
                self.update, self.mode, self.lag = update, mode, lag
                self.queue = []
                self.tok = None
                self.started = False
                run_deferred()
                if mode == "square":
                    preload(ACT.Sqrt)

            def add(self, chunks):
                for m in chunks:
                    self.update(m)
                    if self.mode == "split":
                        split_chunk(m, x[:, m, :], xt[m])
                if self.mode != "split":
                    self.queue.append([(m, square(m, xt[m]) if self.mode == "square" else xt[m]) for m in chunks])

            def flush(self, left):
                while len(self.queue) > left:
                    for m, tok in self.queue.pop(0):
                        self.tok = stat(m, tok, self.mode == "square")

            def step(self, chunks):
                if self.mode == "square":
                    self.flush(1)
                self.add(chunks)
                if not self.started and wk:
                    ensure()
                self.started = True
                self.flush(self.lag)

        def norm(i, s, nbuf, tok, between=None):
            tb = rstd_row(tok, 0, between=between)
            if (i, s) == (0, 0):
                ensure(1)
            pend = []
            pair[0] = 0
            c0 = 3 * s * NC
            am, bm = mod_tok[(i, s, 0)], mod_tok[(i, s, 1)]

            def low(m, b, th, tv):
                dve.wait(th, tv)
                tl = dve.done(nc.vector.tensor_tensor(xlo[:, m, :], nbuf[:, b, :], xhi[:, m, :].bitcast(F32),
                                                      ALU.subtract))
                xn_tok[m] = [th, tl]
                nb_free[b] = tl

            for m in range(NC):
                b = m % 4
                if m == 4:
                    ensure(2)
                dve.wait(tb, nb_free[b], xt[m])
                t1 = dve.done(nc.vector.tensor_tensor(nbuf[:, b, :], x[:, m, :], ps[:, G1, 0:T], ALU.mult))
                act.wait(t1, am, bm, xread[0])
                sc, bi = ascale[:, s, m:m + 1], mod[:, c0 + m:c0 + m + 1]
                th = act.done(nc.scalar.activation(xhi[:, m, :], nbuf[:, b, :], ACT.Identity, scale=sc, bias=bi))
                tv = act.done(nc.scalar.activation(nbuf[:, b, :], nbuf[:, b, :], ACT.Identity, scale=sc, bias=bi))
                pend.append((m, b, th, tv))
                if len(pend) > 1:
                    low(*pend.pop(0))
            low(*pend.pop(0))
            free[G1] = t1
            mod_tok[("used", 3 * s)] = tv
            ensure()

        def need_x(kc):
            return xn_tok[kc]

        def enter(bar=True):
            c = ExitStack()
            toks = [last(pe), last(act), last(dve), last(pool), loads_done()]
            for e in (act, dve, pool):
                e.wait(toks)
            return c

        wk = {}

        def ffn_begin():
            c = enter()
            wk["ctx"] = c
            wk["nbuf"] = sb("nbuf" + tag(), [P, 4, T], F32, c)
            wk["hhi"] = sb("hhi" + tag(), [P, FB, T], F32R, c)
            wk["hlo"] = sb("hlo" + tag(), [P, FB, T], F32R, c)
            wk["e1"] = sb("e1" + tag(), [P, 2, 512], F32, c)
            wk["e2"] = sb("e2" + tag(), [P, 2, 512], F32, c)
            wk["ht"] = [None] * FB
            wk["dt"] = [None] * NC
            wk["ef"] = [None] * 2

        tags = [0]

        def tag():
            tags[0] += 1
            return f"_{tags[0]}"

        def gateup(q):
            b0, b1, tok = feature_unit(xhi, xlo, need_x)
            s = q % 2
            e1, e2 = wk["e1"][:, s, :], wk["e2"][:, s, :]
            act.wait(tok, wk["ef"][s])
            ta = act.done(nc.scalar.activation(e1, ps[:, b0, :], ACT.Silu))
            free[b0] = ta
            dve.wait(ta, tok)
            td = dve.done(nc.vector.tensor_tensor(e2, e1, ps[:, b1, :], ALU.mult))
            free[b1] = td
            hidden_split(q, e2, td, s)

        def hidden_split(q, src, td, s):
            h = wk["hhi"][:, 2 * q:2 * q + 2, :].rearrange("p k n -> p (k n)")
            l = wk["hlo"][:, 2 * q:2 * q + 2, :].rearrange("p k n -> p (k n)")
            act.wait(td)
            th = act.done(nc.scalar.activation(h, src, ACT.Copy))
            dve.wait(th)
            tl = dve.done(nc.vector.tensor_tensor(l, src, h.bitcast(F32), ALU.subtract))
            wk["ef"][s] = tl
            wk["ht"][2 * q] = wk["ht"][2 * q + 1] = [th, tl]

        def down(q, tail=None):
            if q == 0:
                run_deferred()
                pe.wait(free[D0], free[D1], free[D2], free[D3])
            end = q == FB // 2 - 1
            vh, vl, pc = next_piece(2, 1024, 2 if end else CONV)
            hh, hl = wk["hhi"], wk["hlo"]

            def block(k, m):
                kk = k - 2 * q
                return triple(ps[:, D0 + m // 2, (m % 2) * T:(m % 2 + 1) * T], vh[:, kk, m * P:(m + 1) * P],
                              vl[:, kk, m * P:(m + 1) * P], hh[:, k, :], hl[:, k, :], k == 0 and m % 2 == 0,
                              k == FB - 1)

            if not end:
                for k in (2 * q, 2 * q + 1):
                    pe.wait(wk["ht"][k])
                    for m in range(NC):
                        ins = block(k, m)
                piece_used(pc, pe.done(ins))
                run_deferred()
                return
            pe.wait(wk["ht"][2 * q], wk["ht"][2 * q + 1])
            for b in range(4):
                for k in (2 * q, 2 * q + 1):
                    for m in (2 * b, 2 * b + 1):
                        ins = block(k, m)
                tok = pe.done(ins)
                wk["dt"][2 * b] = wk["dt"][2 * b + 1] = tok
                if b == 3:
                    piece_used(pc, tok)
                tail.step((2 * b, 2 * b + 1))
            tail.flush(0)

        def dblk(m):
            return ps[:, D0 + m // 2, (m % 2) * T:(m % 2 + 1) * T]

        def residual(i, s):
            def update(m):
                dve.wait(wk["dt"][m], mod_tok[(i, s, 2)], xt[m])
                xt[m] = dve.done(nc.vector.scalar_tensor_tensor(
                    out=x[:, m, :], in0=dblk(m), scalar=gs[:, s, m:m + 1], in1=x[:, m, :],
                    op0=ALU.mult, op1=ALU.add))
                free[D0 + m // 2] = xt[m]
            return update

        def out_unit(u, ah, al, need, tail=None):
            wk.setdefault("dt", [None] * NC)
            if u == 0:
                _, _, tok = feature_unit(ah, al, need, banks=(D0, D1))
                wk["dt"][0:4] = [tok] * 4
                return
            first = [True]

            def on_bank(b, tok):
                wk["dt"][4 + 2 * b] = wk["dt"][5 + 2 * b] = tok
                if first[0]:
                    first[0] = False
                    tail.step((0, 1))
                    tail.step((2, 3))
                tail.step((4 + 2 * b, 5 + 2 * b))

            feature_unit(ah, al, need, banks=(D2, D3), tail=on_bank)
            tail.flush(0)

        def attn_scratch(c, n):
            wk["S"] = sb("S" + tag(), [P, 4, n], F32, c)
            wk["PT"] = sb("PT" + tag(), [P, 2, n], F32, c)
            wk["dg"] = sb("dg" + tag(), [P, 4, P], F32, c)
            wk["nm"] = sb("nm" + tag(), [P, 16], F32, c)
            wk["rs"] = sb("rs" + tag(), [P, 16], F32, c)
            wk["ri"] = sb("ri" + tag(), [P, 16], F32, c)
            wk["afree"] = dict(s=[None] * 4, pt=[None] * 2)

        def attention(groups, klen, bias, row, toks, emit, compact=False):
            rec = []
            dg = wk["dg"]
            S, PT, nm, rs, ri = wk["S"], wk["PT"], wk["nm"], wk["rs"], wk["ri"]
            pe.wait(toks[:-1], t_id)
            s_free, pt_free = wk["afree"]["s"], wk["afree"]["pt"]

            def score_bank(p, w):
                if compact:
                    return D0 + w
                return D0 + 2 * w if len(groups) > 1 else D0 + 2 * (p % 2) + w

            def scores(p):
                c, qt = p // 2, p % 2
                kl = klen(qt)
                n = kl * len(groups)
                nb = -(-n // 512)
                for w in range(2):
                    for b in range(nb):
                        pe.wait(free[score_bank(p, w) + b])
                for g, (qT, kT, v) in enumerate(groups):
                    for w in range(2):
                        bk, off = score_bank(p, w) + (g * kl) // 512, (g * kl) % 512
                        ins = mm(ps[:, bk, off:off + kl], qT[64 * w:64 * w + 64, c, qt * P:(qt + 1) * P],
                                 kT[64 * w:64 * w + 64, c, 0:kl], True, row is None)
                if row:
                    for w in range(2):
                        lhs, rhs = row(2 * c + w, kl)
                        ins = mm(ps[:, score_bank(p, w), 0:kl], lhs, rhs, False, True)
                tok = pe.done(ins)
                for w in range(2):
                    j, b = 2 * p + w, score_bank(p, w)
                    sv = S[:, j % 4, 0:n]
                    pv = ps[:, b:b + nb, :].rearrange("p a n -> p (a n)")[:, 0:n]
                    dve.wait(tok, s_free[j % 4])
                    td = dve.done(nc.vector.tensor_tensor_reduce(sv, pv, bias(2 * c + w, qt), 1.0, 3e38, ALU.add,
                                                                 ALU.min, nm[:, j:j + 1]))
                    for k in range(nb):
                        free[b + k] = td
                    rec.append([sv, td, n, kl])

            def exps(j):
                sv, td = rec[j][:2]
                act.wait(td)
                rec[j][1] = act.done(nc.scalar.activation(sv, sv, ACT.Exp, bias=nm[:, j:j + 1], scale=-1.0,
                                                          accum_out=rs[:, j:j + 1]))

            def weigh(j):
                dve.wait(rec[j][1])
                tr = dve.done(nc.vector.reciprocal(ri[:, j:j + 1], rs[:, j:j + 1]))
                dve.wait(tr, s_free[j % 4], t_id)
                rec[j][1] = dve.done(nc.vector.tensor_scalar(dg[:, j % 4, :], ident[:, :], ri[:, j:j + 1], None,
                                                             ALU.mult))

            def turn(j):
                sv, ta, n, kl = rec[j]
                bt = G0 if n > 512 else G0 + j % 2
                banks = (G0, G1) if n > 512 else (bt,)
                pe.wait(ta, t_id)
                bank_wait(pe, *banks)
                for b in range(n // P):
                    o = ps[:, bt + b // 4, (b % 4) * P:(b % 4 + 1) * P]
                    ins = mm(o, sv[:, b * P:(b + 1) * P], dg[:, j % 4, :], b % 4 == 0, True)
                tok = pe.done(ins)
                s_free[j % 4] = tok
                pv = ps[:, bt:bt + len(banks), :].rearrange("p a n -> p (a n)")[:, 0:n]
                act.wait(tok, pt_free[j % 2])
                te = act.done(nc.scalar.activation(PT[:, j % 2, 0:n], pv, ACT.Copy))
                for b in banks:
                    free[b] = te
                rec[j].append(te)

            def turn_pair(p):
                n = rec[2 * p][2]
                pe.wait(rec[2 * p][1], rec[2 * p + 1][1], free[D2])
                for w in range(2):
                    j = 2 * p + w
                    for b in range(n // P):
                        ins = mm(ps[:, D2, w * T + b * P:w * T + (b + 1) * P], rec[j][0][:, b * P:(b + 1) * P],
                                 dg[:, j % 4, :], w == 0 and b == 0, True)
                tok = pe.done(ins)
                act.wait(tok, pt_free[0], pt_free[1])
                te = act.done(nc.scalar.activation(
                    PT[:, :, 0:n], ps[:, D2, :].rearrange("p (w n) -> p w n", w=2)[:, :, 0:n], ACT.Copy))
                free[D2] = te
                for j in (2 * p, 2 * p + 1):
                    s_free[j % 4] = tok
                    rec[j].append(te)

            def values(p):
                c, qt = p // 2, p % 2
                bank = D3 if compact else G2 + c % 2
                if qt == 0:
                    pe.wait(free[bank])
                pe.wait(rec[2 * p][4], rec[2 * p + 1][4], toks[-1])
                kl = rec[2 * p][3]
                nb = kl // P
                tot = nb * len(groups)
                for b in range(tot):
                    g, kb = b // nb, b % nb
                    for w in range(2):
                        hd = 2 * c + w
                        ins = mm(ps[64 * w:64 * w + 64, bank, qt * P:(qt + 1) * P],
                                 groups[g][2][:, kb, hd * 64:(hd + 1) * 64],
                                 PT[:, w, b * P:(b + 1) * P], b == 0, b == tot - 1)
                tok = pe.done(ins)
                pt_free[0] = pt_free[1] = tok
                if qt == 1:
                    emit(c, bank, tok)

            def step_of(p):
                if p < 8:
                    scores(p)
                if p >= 2:
                    values(p - 2)
                if compact and 0 < p < 9:
                    turn_pair(p - 1)
                for w in range(2):
                    if 0 < p < 9 and not compact:
                        turn(2 * p - 2 + w)
                    if p < 8:
                        exps(2 * p + w)
                if p < 8:
                    weigh(2 * p)
                    weigh(2 * p + 1)

            if compact:
                return [lambda p=p: step_of(p) for p in range(10)]
            for p in range(10):
                step_of(p)

        def emit_split(hi, lo, res):
            def emit(c, bank, tok):
                act.wait(tok)
                th = act.done(nc.scalar.activation(hi[:, c, :], ps[:, bank, 0:T], ACT.Copy))
                dve.wait(th, tok)
                tl = dve.done(nc.vector.tensor_tensor(lo[:, c, :], ps[:, bank, 0:T], hi[:, c, :].bitcast(F32),
                                                      ALU.subtract))
                free[bank] = tl
                res[c] = [th, tl]
            return emit

        def emit_keep(dst, res):
            def emit(c, bank, tok):
                act.wait(tok)
                res[c] = act.done(nc.scalar.activation(dst[:, c, :], ps[:, bank, 0:T], ACT.Copy))
                free[bank] = res[c]
            return emit

        def mix_attention(hh, *args, compact=False):
            if hh == 0:
                wk["ores"] = [None] * 4
                beside.extend(attention(*args, emit_keep(wk["oT"], wk["ores"]), compact=compact) or ())
                return
            dve.wait(xread[0])
            for c in range(4):
                split_chunk(c, wk["oT"][:, c, :], wk["ores"][c])
            res = [None] * 4
            attention(*args, emit_split(xhi[:, 4:8, :], xlo[:, 4:8, :], res))
            xn_tok[4:8] = res

        def turn_chunks(src, n, toks, banks, scale=None):
            pe.wait(toks, t_id)
            for b in banks:
                pe.wait(free[b])
            out_ = []
            for c in range(n):
                for t in range(2):
                    o = ps[:, banks[c // 2], (c % 2) * T + t * P:(c % 2) * T + (t + 1) * P]
                    ins = nc.tensor.transpose(o, src[:, t, c * P:(c + 1) * P], ident[:, :])
                out_.append(pe.done(ins))
            return out_

        def turn_split(src, n, toks, hi, lo, c0=0, banks=(G0, G1, G2, G3)):
            tk = turn_chunks(src, n, toks, banks[:n // 2])
            res = []
            for j in range(n // 2):
                b = banks[j]
                h = hi[:, c0 + 2 * j:c0 + 2 * j + 2, :].rearrange("p k n -> p (k n)")
                l = lo[:, c0 + 2 * j:c0 + 2 * j + 2, :].rearrange("p k n -> p (k n)")
                act.wait(tk[2 * j + 1])
                th = act.done(nc.scalar.activation(h, ps[:, b, :], ACT.Copy))
                dve.wait(th, tk[2 * j + 1])
                tl = dve.done(nc.vector.tensor_tensor(l, ps[:, b, :], h.bitcast(F32), ALU.subtract))
                free[b] = tl
                res += [[th, tl], [th, tl]]
            return res

        def head_norm(b0, b1, tok, gain, dstT, turned=False):
            y = ps[:, b0:b0 + 2, :].rearrange("p t (h d) -> p (t h) d", d=64)
            tm, hs = wk["tm"], wk["hs"]
            act.wait(tok, wk["tmf"])
            ta = act.done(nc.scalar.activation(tm[:, :, :], ps[:, b0:b0 + 2, :], ACT.Square))
            dve.wait(ta)
            t1 = dve.done(nc.vector.tensor_reduce(hs[:, 0, :], tm[:, :, :].rearrange("p t (h d) -> p (t h) d", d=64),
                                                  AX.X, ALU.add))
            act.wait(t1)
            t2 = act.done(nc.scalar.activation(hs[:, 1, :], hs[:, 0, :], ACT.Sqrt, scale=1.0 / 64,
                                               bias=epst[:, 0:1]))
            dve.wait(t2)
            t3 = dve.done(nc.vector.reciprocal(hs[:, 2, :], hs[:, 1, :]))
            dve.wait(t3, tok, wk["tmf"])
            tv = tm[:, :, :].rearrange("p t (h d) -> p (t h) d", d=64)
            t4 = dve.done(nc.vector.tensor_tensor(tv, y, hs[:, 2, :].unsqueeze(2).to_broadcast([P, 16, 64]),
                                                  ALU.mult))
            free[b0] = free[b1] = [t4, ta]
            dve.wait(t4)
            t5 = dve.done(nc.vector.tensor_tensor(tv, tv, gain.unsqueeze(1).to_broadcast([P, 16, 64]), ALU.mult))
            if turned:
                r4 = tm[:, :, :].rearrange("p t (h d) -> p t h d", d=64)
                ra = wk["ra"][:, :, :, :]
                dve.wait(t5)
                co, si = rope[:, 0, :, :], rope[:, 1, :, :]
                for t in range(2):
                    dve.done(nc.vector.tensor_tensor(ra[:, t, :, 0:16], r4[:, t, :, 0:16],
                                                     co[:, t, :].unsqueeze(1).to_broadcast([P, 8, 16]), ALU.mult))
                    dve.done(nc.vector.tensor_tensor(ra[:, t, :, 16:24], r4[:, t, :, 8:16],
                                                     si[:, t, 0:8].unsqueeze(1).to_broadcast([P, 8, 8]), ALU.mult))
                    t6 = dve.done(nc.vector.tensor_tensor(ra[:, t, :, 24:32], r4[:, t, :, 0:8],
                                                          si[:, t, 8:16].unsqueeze(1).to_broadcast([P, 8, 8]),
                                                          ALU.mult))
                dve.wait(t6)
                t5 = dve.done(nc.vector.tensor_tensor(
                    tv[:, :, 0:16], ra[:, :, :, 0:16].rearrange("p t h d -> p (t h) d"),
                    ra[:, :, :, 16:32].rearrange("p t h d -> p (t h) d"), ALU.add))
            deferred.append(lambda: head_turn(t5, dstT))

        def head_turn(t5, dstT):
            tk = turn_chunks(wk["tm"], 4, t5, (D0, D1))
            act.wait(tk[-1])
            te = act.done(nc.scalar.activation(dstT[:, :, :], ps[:, D0:D0 + 2, :].rearrange(
                "p b (c n) -> p (b c) n", c=2), ACT.Copy))
            free[D0] = free[D1] = te
            wk["tmf"] = tk[-1]
            wk["at"].append(te)

        def keep_v(b0, b1, tok, dst):
            act.wait(tok)
            t = act.done(nc.scalar.activation(dst, ps[:, b0:b0 + 2, :], ACT.Copy))
            free[b0] = free[b1] = t
            wk["at"].append(t)

        def fox_begin():
            c = wk["ctx"]
            wk["at"] = []
            wk["tmf"] = None
            wk["fq"] = [[sb(f"fox_{n}{hh}", shape, F32, c) for n, shape in
                         (("q", [P, 4, T]), ("k", [P, 4, T]), ("v", [P, 2, 512]))] for hh in range(2)]
            wk["tm"] = sb("ftm", [P, 2, 512], F32, c)
            wk["hs"] = sb("fhs", [P, 3, 16], F32, c)
            wk["oT"] = sb("foT", [P, 4, T], F32, c)
            wk["cm"] = sb("fcm", [P, T], F32, c)
            wk["gq"] = sb("fgq", [P, 2, 64], F32, c)
            wk["nbuf"] = sb("fnb", [P, 4, T], F32, c)
            wk["bf"] = sb("fbf", [16, 1], F32, c)
            wk["fl"] = sb("ffl", [16, 4, T], F32, c)
            wk["cT"] = sb("fcT", [P, T], F32, c)
            attn_scratch(c, T)
            load(wk["cm"][:, :], a["k_causal"])
            load(wk["gq"][:, 0, :], a["fox_q_g"])
            load(wk["gq"][:, 1, :], a["fox_k_g"])
            load(wk["bf"][:, :], a["fox_b_f"])
            wk["ldt"] = loads_done()

        def fox_gain():
            dve.wait(wk["ldt"])
            wk["gt"] = dve.done(nc.vector.tensor_scalar(wk["gq"][:, 0, :], wk["gq"][:, 0, :], -0.125, None, ALU.mult))

        def fox_f():
            b, _ = next_pair()
            pe.wait(free[b])
            vh, vl, pc = next_piece(NC, 16)
            for kc in range(NC):
                pe.wait(xn_tok[kc])
                ins = triple(ps[0:16, b, 0:T], vh[:, kc, :], vl[:, kc, :], xhi[:, kc, :], xlo[:, kc, :], kc == 0,
                             kc == NC - 1)
            tok = pe.done(ins)
            piece_used(pc, tok)
            fl = wk["fl"]
            z, t_, l_, o_ = fl[:, 0, :], fl[:, 1, :], fl[:, 2, :], fl[:, 3, :]
            act.wait(tok, wk["ldt"])
            t1 = act.done(nc.scalar.activation(z, ps[0:16, b, 0:T], ACT.Identity, bias=wk["bf"][:, 0:1]))
            free[b] = t1
            act.wait(t1)
            t2 = act.done(nc.scalar.activation(t_, z, ACT.Abs))
            act.wait(t2)
            t3 = act.done(nc.scalar.activation(t_, t_, ACT.Exp, scale=-1.0))
            act.wait(t3)
            t4 = act.done(nc.scalar.activation(l_, t_, ACT.Ln, bias=1.0))
            t0 = dve.done(nc.vector.memset(wk["cT"][:, :], 0.0))
            dve.wait(t4)
            t5 = dve.done(nc.vector.scalar_tensor_tensor(out=z, in0=z, scalar=0.0, in1=l_, op0=ALU.min,
                                                         op1=ALU.subtract))
            t6 = dve.done(nc.vector.memset(o_, 1.0))
            dve.wait(t5, t6, t0)
            wk["ct"] = dve.done(nc.vector.tensor_tensor_scan(wk["cT"][0:16, :], o_, z, 0.0, ALU.mult, ALU.add))

        def fox_in(hh, r):
            if r == 0:
                wk["at"] = []
            b0, b1, tok = token_unit(need_x)
            if r < 2:
                act.wait(wk["gt"])
                dve.wait(wk["gt"], wk["ldt"])
                head_norm(b0, b1, tok, wk["gq"][:, r, :], wk["fq"][hh][r])
            else:
                keep_v(b0, b1, tok, wk["fq"][hh][2][:, :, :])

        def fox_attn(hh):
            pe.wait(wk["ct"])
            dve.wait(wk["ldt"])
            if hh:
                while beside:
                    beside.pop(0)()
            mix_attention(hh, [wk["fq"][hh]], lambda qt: P * (qt + 1),
                          lambda h, qt: wk["cm"][:, P:T] if qt == 0 else wk["cm"][:, :],
                          lambda h, kl: (ident[:, 8 * hh + h:8 * hh + h + 1].to_broadcast([P, P]), wk["cT"][:, 0:kl]),
                          wk["at"], compact=not hh)

        def dil_begin():
            c = wk["ctx"]
            wk["at"] = []
            wk["tmf"] = None
            for g in range(3):
                wk[f"qT{g}"] = sb(f"dqT{g}", [P, 4, T], F32, c)
                wk[f"kT{g}"] = sb(f"dkT{g}", [P, 4, T], F32, c)
                wk[f"v{g}"] = sb(f"dv{g}", [P, 2, 512], F32, c)
            wk["tm"] = sb("dtm", [P, 2, 512], F32, c)
            wk["hs"] = sb("dhs", [P, 3, 16], F32, c)
            wk["ra"] = sb("dra", [P, 2, 8, 32], F32, c)
            wk["oT"] = sb("doT", [P, 4, T], F32, c)
            wk["mask"] = sb("dmask", [P, 1152], F32, c)
            wk["gn"] = sb("dgn", [P, 2, 3, 64], F32, c)
            attn_scratch(c, 768)
            load(wk["mask"][:, :], a["k_mask"])
            load(wk["gn"][:, 0, :, :], a["dil_q_g"])
            load(wk["gn"][:, 1, :, :], a["dil_k_g"])
            wk["ldt"] = loads_done()

        def dil_gain():
            dve.wait(wk["ldt"])
            wk["gt"] = dve.done(nc.vector.tensor_scalar(wk["gn"][:, 0, :, :], wk["gn"][:, 0, :, :], -0.125, None,
                                                        ALU.mult))

        def rope_angles():
            rp = wk["rp"] = sb("rp", [P, 7, 2, 16], F32, wk["ctx"])
            posf = sb("posf", [P, 2], F32, wk["ctx"])
            V = nc.gpsimd
            c1 = 6.28125
            c2 = 0.0019350051879882812
            c3 = 2 * math.pi - c1 - c2
            magic = 12582912.0
            ang = rp[:, 0, :, :]

            def chain(*fs):
                for f in fs:
                    t = pool.done(f())
                    pool.wait(t)
                return t

            pool.wait(t_small)
            chain(lambda: V.tensor_copy(posf[:, :], pos[:, :]))
            for t in range(2):
                chain(lambda: V.tensor_scalar(rp[:, 0, t, :], inv[:, 0, :], posf[:, t:t + 1], None, ALU.mult))
            for w, (off, q, r) in enumerate(((0.25, 1, 2), (0.0, 3, 4))):
                n, d = rp[:, q, :, :], rp[:, r, :, :]
                prev = ang
                chain(lambda: V.tensor_scalar(n, ang, 1.0 / (2 * math.pi), off, ALU.mult, ALU.add),
                      lambda: V.tensor_scalar(n, n, magic, None, ALU.add),
                      lambda: V.tensor_scalar(n, n, -magic, None, ALU.add))
                for c in (c1, c2, c3):
                    chain(lambda: V.tensor_scalar(rp[:, 5 + w, :, :], n, -c, None, ALU.mult),
                          lambda: V.tensor_tensor(d, prev, rp[:, 5 + w, :, :], ALU.add))
                    prev = d
                t = chain(lambda: V.tensor_scalar(d, d, math.pi / 2 if w == 0 else 0.0, None, ALU.add),
                          lambda: V.tensor_scalar(d, d, 3.1415925, -3.1415925, ALU.min, ALU.max))
            wk["rpt"] = t

        def rope_tables():
            rp = wk["rp"]
            act.wait(wk["rpt"])
            act.done(nc.scalar.activation(rope[:, 0, :, :], rp[:, 2, :, :], ACT.Sin))
            t = act.done(nc.scalar.activation(rp[:, 0, :, :], rp[:, 4, :, :], ACT.Sin))
            pool.wait(t)
            wk["rt"] = pool.done(nc.gpsimd.tensor_tensor(rope[:, 1, :, :], rp[:, 0, :, :], inv[:, 1, :].unsqueeze(1)
                                                         .to_broadcast([P, 2, 16]), ALU.mult))

        def dil_in(hh, g, r):
            if r == 0 and g == 0:
                wk["at"] = []
            b0, b1, tok = token_unit(need_x)
            if r < 2:
                dve.wait(wk["gt"], wk["ldt"], wk["rt"])
                head_norm(b0, b1, tok, wk["gn"][:, r, g, :], wk[f"{'qk'[r]}T{g}"], turned=True)
            else:
                keep_v(b0, b1, tok, wk[f"v{g}"][:, :, :])

        def dil_attn(hh):
            mix_attention(hh, [(wk[f"qT{g}"], wk[f"kT{g}"], wk[f"v{g}"]) for g in range(3)],
                          lambda qt: P * (qt + 1),
                          lambda h, qt: wk["mask"][:, 0:384] if qt == 0 else wk["mask"][:, 384:1152], None, wk["at"])

        def layer_norm(i, j, nxt, tok):
            preload(ACT.Sqrt)
            for m in range(NC):
                dve.wait(tok, xt[m])
                xt[m] = dve.done(nc.vector.tensor_tensor(x[:, m, :], x[:, m, :], ps[:, G0, 0:T], ALU.subtract))
                pe.wait(square(m, xt[m]))
                if m == 0:
                    pe.wait(free[G1])
                tk = pe.done(mm(ps[:, G1, 0:T], mean[:, :], sqb[:, m % 4, :], m == 0, m == NC - 1))
                sq_free[m % 4] = tk
            free[G0] = xt[-1]
            tb = rstd_row(tk, 1, G1, G0)
            pair[0] = 0
            pend = []

            def low(m, th):
                dve.wait(th, xt[m])
                xn_tok[m] = [th, dve.done(nc.vector.tensor_tensor(xlo[:, m, :], x[:, m, :],
                                                                  xhi[:, m, :].bitcast(F32), ALU.subtract))]

            for m in range(NC):
                if m == 4:
                    ensure(2)
                dve.wait(tb, xt[m])
                t1 = dve.done(nc.vector.tensor_tensor(x[:, m, :], x[:, m, :], ps[:, G0, 0:T], ALU.mult))
                act.wait(t1, t_small)
                g, b = ln[:, i, 2 * j, m:m + 1], ln[:, i, 2 * j + 1, m:m + 1]
                if nxt:
                    act.wait(xread[0])
                    th = act.done(nc.scalar.activation(xhi[:, m, :], x[:, m, :], ACT.Identity, scale=g, bias=b))
                xt[m] = act.done(nc.scalar.activation(x[:, m, :], x[:, m, :], ACT.Identity, scale=g, bias=b))
                if nxt:
                    pend.append((m, th))
                    if len(pend) > 1:
                        low(*pend.pop(0))
            if nxt:
                low(*pend.pop(0))
            free[G0] = t1
            ensure()

        def na_begin(i):
            c = enter()
            wk["ctx"] = c
            wk["yahi"] = sb("yahi" + tag(), [P, 4, T], F32R, c)
            wk["yalo"] = sb("yalo" + tag(), [P, 4, T], F32R, c)
            wk["sg"] = sb("sg" + tag(), [P, 2, 2, 1024], F32, c)
            wk["sgt"] = [[None, None], [None, None]]
            wk["rctx"] = ExitStack()
            wk["v"] = sb("rv" + tag(), [P, 2, 1024], F32, wk["rctx"])
            wk["g"] = sb("rg" + tag(), [P, 2, 1024], F32, wk["rctx"])
            wk["pt"] = sb("rpt" + tag(), [P, 2, 2, T], F32, wk["rctx"])
            wk["dk"] = sb("rdk" + tag(), [P, 5, 8], F32, wk["rctx"])
            wk["at"] = []
            n = ExitStack()
            wk["nctx"] = n
            wk["nq"] = sb("nqT" + tag(), [P, 4, T], F32, n)
            wk["nk"] = sb("nkT" + tag(), [P, 4, T], F32, n)
            wk["nv"] = sb("nv" + tag(), [P, 2, 512], F32, n)
            wk["nbias"] = sb("nbias" + tag(), [P, 2, 2, 2, T], F32, n)
            wk["nat"] = []
            wk["nbt"] = [None] * 4
            attn_scratch(n, T)
            for c in range(2):
                na_bias(i, c)
            load(pT[:, :, :], a["p_2"][i])
            wk["pld"] = loads_done()
            wk["rel"] = wk["pt"]
            load(wk["rel"][:, :, :, :], a["k_rel"])
            load(wk["dk"][:, 0, :], a["decay"][i])
            wk["ldt"] = loads_done()

        def na_bias(i, c, *toks):
            b = wk["nbias"][:, c % 2, :, :, :]
            t = load(b, a["na_rpb_2"][i][:, 2 * c:2 * c + 2, :, :], *toks)
            pool.wait(t)
            wk["nbt"][c] = pool.done(nc.gpsimd.tensor_scalar(b, b, -1.0, None, ALU.mult))

        def na_in(u):
            if u < 2:
                b0, b1, tok = feature_unit(xhi, xlo, need_x)
                dst = (wk["nq"], wk["nk"])[u]
                act.wait(tok)
                t = act.done(nc.scalar.activation(dst[:, :, :], ps[:, b0:b0 + 2, :].rearrange(
                    "p b (c n) -> p (b c) n", c=2), ACT.Copy, scale=-0.125 if u == 0 else 1.0))
                free[b0] = free[b1] = t
                wk["nat"].append(t)
            else:
                b0, b1, tok = token_unit(need_x)
                act.wait(tok)
                t = act.done(nc.scalar.activation(wk["nv"][:, :, :], ps[:, b0:b0 + 2, :], ACT.Copy))
                free[b0] = free[b1] = t
                wk["nat"].append(t)

        def na_attn(i):
            wk["yat"] = [None] * 4

            def bias(h, qt):
                dve.wait(wk["nbt"][h // 2])
                return wk["nbias"][:, (h // 2) % 2, h % 2, qt, :]

            steps_ = attention([(wk["nq"], wk["nk"], wk["nv"])], lambda qt: T, bias, None, wk["nat"],
                               emit_split(wk["yahi"], wk["yalo"], wk["yat"]), compact=True)

            def with_bias(p):
                steps_[p]()
                if p in (1, 3):
                    na_bias(i, p // 2 + 2, last(dve))

            beside.extend(lambda p=p: with_bias(p) for p in range(len(steps_)))

        def na_end():
            while beside:
                beside.pop(0)()
            wk["nctx"].close()
            toks = [last(pe), last(act), last(dve), last(pool)]
            for e in (act, dve, pool):
                e.wait(toks)
            ret_alloc(wk["rctx"])

        def ret_alloc(n):
            wk["tmf"] = None
            wk["qT"] = sb("rqT" + tag(), [P, 4, T], F32, n)
            wk["kT"] = sb("rkT" + tag(), [P, 4, T], F32, n)
            wk["dt4"] = sb("rd" + tag(), [P, 4, 2, T], F32, n)
            wk["tm"] = sb("rtm" + tag(), [P, 2, 512], F32, n)
            wk["cs"] = rot
            wk["ptf"] = [None, None]
            wk["rt3"] = []
            wk["bn"] = sb("rbn" + tag(), [P, 8, 6], F32, n)
            wk["mv"] = sb("rmv" + tag(), [P, 8, 2], F32, n)
            wk["sd"] = sb("rsd" + tag(), [P, 2, 8], F32, n)

        def ret_decay():
            ensure()
            dk = wk["dk"]
            act.wait(wk["ldt"])
            t = act.done(nc.scalar.activation(dk[:, 1, :], dk[:, 0, :], ACT.Abs))
            act.wait(t)
            t = act.done(nc.scalar.activation(dk[:, 2, :], dk[:, 1, :], ACT.Exp, scale=-1.0))
            act.wait(t)
            t = act.done(nc.scalar.activation(dk[:, 3, :], dk[:, 2, :], ACT.Ln, bias=1.0))
            dve.wait(t, wk["ldt"])
            t = dve.done(nc.vector.scalar_tensor_tensor(out=dk[:, 4, :], in0=dk[:, 0, :], scalar=0.0,
                                                        in1=dk[:, 3, :], op0=ALU.min, op1=ALU.subtract))
            act.wait(t)
            d4, rel, e = wk["dt4"], wk["rel"], wk["tm"]
            tp = [None, None]
            for h in range(4):
                d = d4[:, h, :, :].rearrange("p b n -> p (b n)")
                act.wait(tp[h % 2])
                act.done(nc.scalar.activation(d, rel[:, 0, :, :].rearrange("p b n -> p (b n)"), ACT.Exp,
                                              scale=dk[:, 4, h:h + 1]))
                t = act.done(nc.scalar.activation(e[:, h % 2, :], rel[:, 1, :, :].rearrange("p b n -> p (b n)"),
                                                  ACT.Exp, scale=dk[:, 4, 4 + h:5 + h]))
                pool.wait(t)
                tp[h % 2] = pool.done(nc.gpsimd.tensor_tensor(d, d, e[:, h % 2, :], ALU.mult))
            wk["d4t"] = tp

        def ret_in(u):
            b0, b1, tok = token_unit(need_x)
            if u < 2:
                tm, cs = wk["tm"], wk["cs"]
                dve.wait(tok, wk["ldt"], wk["tmf"], wk["d4t"])
                rb = wk["pt"]
                for t in range(2):
                    y = ps[:, (b0, b1)[t], :].rearrange("p (h w d) -> p h w d", h=4, w=2)
                    tv = tm[:, t, :].rearrange("p (h w d) -> p h w d", h=4, w=2)
                    rv = rb[:, t, :, :].rearrange("p a (h w d) -> p (a h) w d", w=2, d=64)
                    co = cs[:, 0, t, :].unsqueeze(1)
                    si = cs[:, 1, t, :].unsqueeze(1).to_broadcast([P, 4, 64])
                    t1 = dve.done(nc.vector.tensor_tensor(
                        tm[:, t, :].rearrange("p (a d) -> p a d", d=64),
                        ps[:, (b0, b1)[t], :].rearrange("p (a d) -> p a d", d=64),
                        co.to_broadcast([P, 8, 64]), ALU.mult))
                    t2 = dve.done(nc.vector.tensor_tensor(rv[:, :, 0, :], y[:, :, 1, :], si, ALU.mult))
                    t3 = dve.done(nc.vector.tensor_tensor(rv[:, :, 1, :], y[:, :, 0, :], si, ALU.mult))
                    dve.wait(t3)
                    dve.done(nc.vector.tensor_tensor(tv[:, :, 0, :], tv[:, :, 0, :], rv[:, :, 0, :], ALU.subtract))
                    t4 = dve.done(nc.vector.tensor_tensor(tv[:, :, 1, :], tv[:, :, 1, :], rv[:, :, 1, :], ALU.add))
                free[b0] = free[b1] = t3
                dst = (wk["qT"], wk["kT"])[u]

                def turn():
                    tk = turn_chunks(wk["tm"], 4, t4, (D0, D1))
                    act.wait(tk[-1])
                    te = act.done(nc.scalar.activation(dst[:, :, :], ps[:, D0:D0 + 2, :].rearrange(
                        "p b (c n) -> p (b c) n", c=2), ACT.Copy, scale=1.0 if u == 0 else 128.0 ** -0.5))
                    free[D0] = free[D1] = te
                    wk["tmf"] = tk[-1]
                    wk["at"].append(te)

                deferred.append(turn)
            elif u < 4:
                keep_v(b0, b1, tok, wk["v"][:, :, 512 * (u - 2):512 * (u - 1)])
            else:
                act.wait(tok)
                t = act.done(nc.scalar.activation(wk["g"][:, :, 512 * (u - 4):512 * (u - 3)], ps[:, b0:b0 + 2, :],
                                                  ACT.Silu))
                free[b0] = free[b1] = t
                wk["gt"] = t

        def ret_out(h, nt):
            return ps[:, D2 + h % 2, nt * T:(nt + 1) * T]

        def ret(h):
            qT, kT, d4, pt = wk["qT"], wk["kT"], wk["dt4"], wk["pt"]
            b = D0 + h % 2
            pe.wait(wk["at"], free[b])
            for mb in range(2):
                ins = mm(ps[:, b, mb * T:(mb + 1) * T], kT[:, h, mb * P:(mb + 1) * P], qT[:, h, :], mb == 0, True)
            tok = pe.done(ins)
            dve.wait(tok, wk["d4t"], wk["ptf"][h % 2], wk["at"])
            tp = dve.done(nc.vector.tensor_tensor(pt[:, h % 2, :, :].rearrange("p b n -> p (b n)"), ps[:, b, :],
                                                  d4[:, h, :, :].rearrange("p b n -> p (b n)"), ALU.mult))
            free[b] = tp
            deferred.append(lambda: ret_values(h, tp))

        def ret_values(h, tp):
            v, pt, g = wk["v"], wk["pt"], wk["g"]
            bn, mv, sd, e = wk["bn"], wk["mv"], wk["sd"], wk["tm"]
            bo = D2 + h % 2
            pe.wait(tp, free[bo])
            for nt in range(2):
                for mb in range(2):
                    ins = mm(ret_out(h, nt), pt[:, h % 2, mb, nt * P:(nt + 1) * P], v[:, mb, h * T:(h + 1) * T],
                             mb == 0, mb == 1)
            tok = pe.done(ins)
            wk["ptf"][h % 2] = tok
            dve.wait(tok)
            for nt in range(2):
                t = dve.done(nc.vector.bn_stats(bn[:, 2 * h + nt, :], ret_out(h, nt)))
            dve.wait(t)
            for nt in range(2):
                t = dve.done(nc.vector.bn_aggr(mv[:, 2 * h + nt, :], bn[:, 2 * h + nt, :]))
            act.wait(t, t_ones)
            t = act.done(nc.scalar.activation(sd[:, 0, 2 * h:2 * h + 2], mv[:, 2 * h:2 * h + 2, 1], ACT.Sqrt,
                                              bias=epst[:, 0:1]))
            dve.wait(t)
            t = dve.done(nc.vector.reciprocal(sd[:, 1, 2 * h:2 * h + 2], sd[:, 0, 2 * h:2 * h + 2]))
            dve.wait(t, wk["gt"])
            for nt in range(2):
                j = 2 * h + nt
                tmp = e[:, nt, 0:T]
                t = dve.done(nc.vector.tensor_scalar(tmp, ret_out(h, nt), mv[:, j, 0:1], sd[:, 1, j:j + 1],
                                                     ALU.subtract, ALU.mult))
            free[bo] = t
            dve.wait(t)
            for nt in range(2):
                t = dve.done(nc.vector.tensor_tensor(g[:, nt, h * T:(h + 1) * T], g[:, nt, h * T:(h + 1) * T],
                                                     e[:, nt, 0:T], ALU.mult))
            wk["rt3"].append(t)

        def ret_end():
            act.wait(xread[0])
            dve.wait(xread[0])
            wk["ybt"] = turn_split(wk["g"], 8, wk["rt3"], xhi, xlo, banks=(D0, D1, D2, D3))
            wk["rctx"].close()
            c = wk["ctx"]
            toks = [last(pe), last(act), last(dve), last(pool)]
            for e_ in (act, dve, pool):
                e_.wait(toks)
            wk["mhi"] = sb("mhi" + tag(), [P, NC, T], F32R, c)
            wk["mlo"] = sb("mlo" + tag(), [P, NC, T], F32R, c)
            wk["mt"] = [None] * NC

        def gate(u, b):
            b0, b1, tok = feature_unit(xhi, xlo, need_x)
            act.wait(tok)
            wk["sgt"][b][u] = act.done(nc.scalar.activation(wk["sg"][:, b, u, :], ps[:, b0:b0 + 2, :].rearrange(
                "p b n -> p (b n)"), ACT.Sigmoid))
            free[b0] = free[b1] = wk["sgt"][b][u]

        def branch(u, b):
            if b == 0:
                b0, b1, tok = feature_unit(wk["yahi"], wk["yalo"], lambda kc: wk["yat"][kc], nk=4)
            else:
                b0, b1, tok = feature_unit(xhi, xlo, lambda kc: wk["ybt"][kc])
            pv = ps[:, b0:b0 + 2, :].rearrange("p b n -> p (b n)")
            sg, m = wk["sg"][:, b, u, :], wk["sg"][:, 0, u, :]
            dve.wait(tok, wk["sgt"][b][u])
            t = dve.done(nc.vector.tensor_tensor(sg, sg, pv, ALU.mult))
            free[b0] = free[b1] = wk["sgt"][b][u] = t
            if b == 0:
                return
            h = wk["mhi"][:, 4 * u:4 * u + 4, :].rearrange("p k n -> p (k n)")
            l = wk["mlo"][:, 4 * u:4 * u + 4, :].rearrange("p k n -> p (k n)")
            dve.wait(t, wk["sgt"][0][u])
            for k in range(2):
                c = slice(512 * k, 512 * k + 512)
                t = dve.done(nc.vector.tensor_tensor(m[:, c], m[:, c], sg[:, c], ALU.add))
                act.wait(t)
                th = act.done(nc.scalar.activation(h[:, c], m[:, c], ACT.Copy))
                dve.wait(th)
                tl = dve.done(nc.vector.tensor_tensor(l[:, c], m[:, c], h[:, c].bitcast(F32), ALU.subtract))
                wk["mt"][4 * u + 2 * k] = wk["mt"][4 * u + 2 * k + 1] = [th, tl]

        def update_ln(m):
            dve.wait(wk["dt"][m], xt[m])
            xt[m] = dve.done(nc.vector.scalar_tensor_tensor(
                out=x[:, m, :], in0=x[:, m, :], scalar=ALPHA, in1=dblk(m), op0=ALU.mult, op1=ALU.add))
            free[D0 + m // 2] = xt[m]

        def update_plain(m):
            dve.wait(wk["dt"][m], xt[m])
            xt[m] = dve.done(nc.vector.tensor_tensor(x[:, m, :], x[:, m, :], dblk(m), ALU.add))
            free[D0 + m // 2] = xt[m]

        def second_ffn_begin(i):
            wk["ctx"].close()
            ffn_begin()
            c = wk["ctx"]
            wk["cw"] = cw[:, i, :, :]
            wk["phi"] = sb("phi" + tag(), [P, 2, T], F32R, c)
            wk["plo"] = sb("plo" + tag(), [P, 2, T], F32R, c)
            wk["pg"] = wk["e1"][:, :, :].rearrange("p a n -> p (a n)")
            act.wait(wk["pld"])
            th = act.done(nc.scalar.activation(wk["phi"][:, :, :], pT[:, :, :], ACT.Copy))
            dve.wait(th, wk["pld"])
            tl = dve.done(nc.vector.tensor_tensor(wk["plo"][:, :, :], pT[:, :, :],
                                                  wk["phi"][:, :, :].bitcast(F32), ALU.subtract))
            wk["pt_"] = [th, tl]
            wk["pgf"] = None

        def plegate(u):
            b0, b1, tok = feature_unit(xhi, xlo, need_x)
            act.wait(tok, wk["pgf"])
            wk["pgt"] = act.done(nc.scalar.activation(wk["pg"], ps[:, b0:b0 + 2, :].rearrange(
                "p b n -> p (b n)"), ACT.Sigmoid))
            free[b0] = free[b1] = wk["pgt"]

        def pleproj(u):
            b0, b1, tok = feature_unit(wk["phi"], wk["plo"], lambda kc: wk["pt_"], nk=2)
            dve.wait(tok, wk["pgt"])
            t = dve.done(nc.vector.tensor_tensor(wk["pg"], wk["pg"], ps[:, b0:b0 + 2, :].rearrange(
                "p b n -> p (b n)"), ALU.mult))
            free[b0] = free[b1] = t
            dve.wait(t, *[xn_tok[m] for m in range(4 * u, 4 * u + 4)])
            xv = x[:, 4 * u:4 * u + 4, :].rearrange("p k n -> p (k n)")
            t = dve.done(nc.vector.scalar_tensor_tensor(out=xv, in0=xv, scalar=ALPHA, in1=wk["pg"],
                                                        op0=ALU.mult, op1=ALU.add))
            wk["pgf"] = wk["ef"][0] = wk["ef"][1] = t
            for m in range(4 * u, 4 * u + 4):
                xt[m] = t

        def convup(q):
            b0, b1, tok = feature_unit(xhi, xlo, need_x)
            s = q % 2
            cw = wk["cw"]
            e = (wk["e1"], wk["e2"])
            res = []
            for side, b in ((0, b0), (1, b1)):
                act.wait(tok, wk["ef"][s], t_small)
                for k in range(2):
                    blk = 22 * side + 2 * q + k
                    ta = act.done(nc.scalar.activation(
                        e[side][:, s, k * T:(k + 1) * T], ps[:, b, k * T:(k + 1) * T], ACT.Identity,
                        scale=cw[:, 1, blk:blk + 1], bias=cw[:, 3, blk:blk + 1]))
                for k in range(2):
                    blk = 22 * side + 2 * q + k
                    y = ps[:, b, k * T:(k + 1) * T]
                    o = e[side][:, s, k * T:(k + 1) * T]
                    dve.wait(ta, tok)
                    t = dve.done(nc.vector.scalar_tensor_tensor(
                        out=o[:, 1:T], in0=y[:, 0:T - 1], scalar=cw[:, 0, blk:blk + 1], in1=o[:, 1:T],
                        op0=ALU.mult, op1=ALU.add))
                    dve.wait(t)
                    t = dve.done(nc.vector.scalar_tensor_tensor(
                        out=o[:, 0:T - 1], in0=y[:, 1:T], scalar=cw[:, 2, blk:blk + 1], in1=o[:, 0:T - 1],
                        op0=ALU.mult, op1=ALU.add))
                free[b] = t
                res.append(t)
            ensure()
            act.wait(res[0])
            ta = act.done(nc.scalar.activation(e[0][:, s, :], e[0][:, s, :], ACT.Gelu_apprx_tanh))
            dve.wait(ta, res[1])
            td = dve.done(nc.vector.tensor_tensor(e[1][:, s, :], e[0][:, s, :], e[1][:, s, :], ALU.mult))
            hidden_split(q, e[1][:, s, :], td, s)

        tail = None
        for s in steps:
            k = s["kind"]
            i, u = s.get("i"), s.get("u")
            if k == "mod":
                if tail is None and u == 3:
                    tail = Tail(lambda m: None, "square")
                    for m in range(0, NC, 2):
                        tail.step((m, m + 1))
                    tail.flush(0)
                mod_unit(i, u, s.get("bank", D3) - u % 2, CONV if wk else 0)
            elif k == "norm":
                run_deferred()
                if "ctx" in wk:
                    wk["ctx"].close()
                if s["s"] != 1:
                    ffn_begin()
                else:
                    wk["ctx"] = enter()
                    (dil_begin if i else fox_begin)()
                    if i:
                        wk["nbuf"] = wk["v0"][:, :, :].rearrange("p t n -> p (t n)").rearrange("p (k n) -> p k n", k=4)
                md = s["m"]
                norm(i, s["s"], wk["nbuf"], tail.tok, (lambda: mod_unit(*md, D3 - md[1] % 2, 1)) if md else None)
                if s["s"] == 1:
                    (dil_gain if i else fox_gain)()
            elif k == "gateup":
                gateup(s["q"])
                if (i, s["j"]) == (0, 0) and s["q"] == 0:
                    rope_angles()
                elif (i, s["j"]) == (0, 0) and s["q"] == 6:
                    rope_tables()
            elif k == "down":
                if s["q"] == FB // 2 - 1:
                    tail = Tail(residual(i, 2 * s["j"]), "split" if (i, s["j"]) == (1, 1) else "square")
                down(s["q"], tail)
            elif k == "fox_f":
                fox_f()
            elif k == "fox_in":
                fox_in(s["hh"], s["r"])
            elif k == "fox_attn":
                fox_attn(s["hh"])
            elif k == "dil_in":
                dil_in(s["hh"], s["g"], s["r"])
            elif k == "dil_attn":
                dil_attn(s["hh"])
            elif k == "mix_out":
                if u == 1:
                    tail = Tail(residual(i, 1), "square")
                out_unit(u, xhi, xlo, need_x, tail)
            elif k == "sec_begin":
                wk["ctx"].close()
                na_begin(i)
            elif k == "na_in":
                na_in(u)
            elif k == "na_attn":
                na_attn(i)
            elif k == "ret_in":
                ret_in(u)
            elif k == "ret":
                ret(s["h"])
            elif k == "ret_end":
                ret_end()
            elif k == "gate":
                gate(u, s["b"])
                if (u, s["b"]) == (0, 0):
                    na_end()
                    ret_decay()
            elif k == "branch":
                branch(u, s["b"])
            elif k == "wout":
                if u == 1:
                    tail = Tail(update_ln, "mean")
                out_unit(u, wk["mhi"], wk["mlo"], lambda kc: wk["mt"][kc], tail)
            elif k == "ln":
                layer_norm(i, s["j"], s["j"] == 0 or i == 0, tail.tok)
                if s["j"] == 0:
                    second_ffn_begin(i)
            elif k == "plegate":
                plegate(u)
            elif k == "pleproj":
                pleproj(u)
            elif k == "convup":
                convup(s["q"])
            elif k == "down2":
                if s["q"] == FB // 2 - 1:
                    tail = Tail(update_plain, "mean")
                down(s["q"], tail)
        wk["ctx"].close()
        for m in range(NC):
            sp.wait(xt[m])
            t = sy.done(nc.sync.dma_start(out[:, m, :], x[:, m, :]), "s_st", 16)
        sp.wait(t)


def constants():
    import numpy as np
    k = {}
    k["k_ident"] = np.eye(P, dtype=np.float32)
    s = np.arange(T)
    q = np.arange(P)
    k["k_causal"] = np.where(s[None, :] <= q[:, None] + P, 0.0, BIG).astype(np.float32)
    parts = []
    for qt in range(2):
        for window, dil in ((128, 1), (512, 4), (2048, 16)):
            d = (q[:, None] + P * qt) - np.arange(P * (qt + 1))[None, :]
            parts.append(np.where((d >= 0) & (d <= window) & (d % dil == 0), 0.0, BIG).astype(np.float32))
    k["k_mask"] = np.ascontiguousarray(np.concatenate(parts, axis=1))
    inv = (np.float32(500000.0) ** (-(np.arange(8, dtype=np.float32) * 2.0 / 16))).astype(np.float32)
    sign = np.concatenate([-np.ones(8), np.ones(8)]).astype(np.float32)
    k["k_inv"] = np.ascontiguousarray(np.broadcast_to(np.stack([np.concatenate([inv, inv]), sign]), (P, 2, 16)))
    inv = (np.float32(10000.0) ** (-np.arange(64, dtype=np.float32) / 64)).astype(np.float32)
    ang = (s.astype(np.float32)[:, None] * inv[None, :]).astype(np.float64)
    rot = np.stack([np.cos(ang), np.sin(ang)]).astype(np.float32).reshape(2, 2, P, 64)
    k["k_rot"] = np.ascontiguousarray(rot.transpose(2, 0, 1, 3))
    m = (np.arange(2)[None, :, None] * P + q[:, None, None])
    n = s[None, None, :]
    k["k_rel"] = np.ascontiguousarray(np.stack([np.maximum(n - m, 0), np.maximum(m - n, 0)], axis=1).astype(np.float32))
    return k


def layout(inp):
    import numpy as np
    g = {n: np.asarray(v) for n, v in inp.items()}

    def col(v, n):
        return np.ascontiguousarray(v.reshape(v.shape[:-1] + (n, P)))

    r = {}
    for n in ("mod_w", "ffn_w_gate", "ffn_w_up", "ffn_w_down", "fox_w_in", "fox_w_out", "dil_w_in", "dil_w_out",
              "w_in_2", "w_branch_a_2", "w_branch_b_2", "w_out_2", "w_up_2", "w_down_2", "w_ple_gate_2",
              "w_ple_proj_2"):
        r[n] = np.ascontiguousarray(g[n])
    r["x"] = np.ascontiguousarray(g["x"][0].T.reshape(NC, P, T).transpose(1, 0, 2))
    r["c"] = np.ascontiguousarray(g["c"].reshape(NC, P).T)
    r["mod_b"] = np.ascontiguousarray(g["mod_b"].reshape(2, 72, P).transpose(2, 0, 1))
    r["norm_g"] = np.ascontiguousarray(g["norm_g"].reshape(6, NC, P).transpose(2, 0, 1))
    r["ln"] = np.ascontiguousarray(np.stack([g["ln1_g_2"], g["ln1_b_2"], g["ln2_g_2"], g["ln2_b_2"]], axis=1)
                                   .reshape(2, 4, NC, P).transpose(3, 0, 1, 2))
    r["fox_q_g"] = np.ascontiguousarray(np.broadcast_to(g["fox_q_g"], (P, 64)))
    r["fox_k_g"] = np.ascontiguousarray(np.broadcast_to(g["fox_k_g"], (P, 64)))
    r["fox_b_f"] = np.ascontiguousarray(g["fox_b_f"].reshape(16, 1))
    r["dil_q_g"] = np.ascontiguousarray(np.broadcast_to(g["dil_q_g"][0], (P, 3, 64)))
    r["dil_k_g"] = np.ascontiguousarray(np.broadcast_to(g["dil_k_g"][0], (P, 3, 64)))
    r["positions"] = np.ascontiguousarray(g["positions"].reshape(2, P).T)
    q = np.arange(T)
    rr, cc = q // 64, q % 64
    start = np.clip(cc - 8, 0, 48)
    dr = rr[None, :] - rr[:, None] + 7
    inside = (cc[None, :] >= start[:, None]) & (cc[None, :] < start[:, None] + 16)
    dc = np.where(inside, cc[None, :] - cc[:, None] + 15, 31)
    padded = np.pad(g["na_rpb_2"], ((0, 0), (0, 0), (0, 0), (0, 1)), constant_values=-BIG)
    b = padded[:, :, dr, dc]
    r["na_rpb_2"] = np.ascontiguousarray(b.reshape(2, 8, 2, P, T).transpose(0, 3, 1, 2, 4))
    dec = np.concatenate([g["ret_decay_f_2"], g["ret_decay_b_2"]], axis=1)
    r["decay"] = np.ascontiguousarray(np.broadcast_to(dec[:, None, :], (2, P, 8)))
    cw = np.concatenate([g["conv_w_2"], g["conv_b_2"][:, None, :]], axis=1)
    r["conv"] = np.ascontiguousarray(cw.reshape(2, 4, 44, P).transpose(3, 0, 1, 2))
    r["p_2"] = np.ascontiguousarray(g["p_2"][:, 0].transpose(0, 2, 1).reshape(2, 2, P, T).transpose(0, 2, 1, 3))
    r.update(constants())
    return r


def kernel(**inputs):
    import concourse.bacc as bacc
    import numpy as np
    from concourse.bass_utils import run_bass_kernel_spmd

    nc = bacc.Bacc("TRN2", target_bir_lowering=False, num_devices=1)
    arrays = {f"in_{n}": v for n, v in layout(inputs).items()}
    args = {n[3:]: nc.dram_tensor(n, v.shape, mybir.dt.from_np(v.dtype), kind="ExternalInput").ap()
            for n, v in arrays.items()}
    out = nc.dram_tensor("out_x", (P, NC, T), F32, kind="ExternalOutput").ap()
    build(nc, args, out)
    r = run_bass_kernel_spmd(nc, [arrays], core_ids=[0])
    y = r.results[0]["out_x"]
    return np.ascontiguousarray(np.asarray(y).transpose(1, 0, 2).reshape(1, D, T).transpose(0, 2, 1))
```
